# Optimizing a Trainium2 kernel written in Bass

```python
import jax, jax.numpy as jnp
from jax import lax
import numpy as np

D_MODEL = 1024
BATCH = 1
SEQ = 512
DEPTH = 1

HEAD_DIM = D_MODEL // 16
RET_HEADS = 8
NSA_HEADS = 8
NSA_KV_GROUPS = 2
HEADS_PER_GROUP = NSA_HEADS // NSA_KV_GROUPS
RET_WIDTH = RET_HEADS * HEAD_DIM
NSA_WIDTH = NSA_HEADS * HEAD_DIM
MIX_WIDTH = RET_WIDTH + NSA_WIDTH
KV_WIDTH = NSA_KV_GROUPS * HEAD_DIM
RET_CHUNK = 128
RET_ROPE_BASE = 10000.0
NSA_ROPE_BASE = 500000.0
ROPE_DIM = HEAD_DIM // 4
CMP_BLOCK = 32
CMP_STRIDE = 16
CMP_HIDDEN = 256
SLC_BLOCK = 64
SLC_TOPK = 16
WINDOW = 512
NSA_QBLK = 64
NEG = -1e30
BIG = 1e9
EPS = 1e-6
SPLITS = (RET_WIDTH, RET_WIDTH, RET_WIDTH, RET_WIDTH, NSA_WIDTH, 6 * KV_WIDTH, 3 * NSA_HEADS, NSA_WIDTH)
PROJ_WIDTH = sum(SPLITS)


def rmsnorm(x, g):
    xf = x.astype(jnp.float32)
    y = xf * lax.rsqrt(jnp.mean(xf * xf, axis=-1, keepdims=True) + EPS) * g.astype(jnp.float32)
    return y.astype(x.dtype)

def rotary(x, pos, base, rot_dim):
    half = rot_dim // 2
    inv = jnp.power(base, -jnp.arange(half, dtype=jnp.float32) / half)
    ang = pos.astype(jnp.float32)[..., None] * inv
    cos = jnp.cos(ang)[:, :, None, :]
    sin = jnp.sin(ang)[:, :, None, :]
    x1 = x[..., :half].astype(jnp.float32)
    x2 = x[..., half:rot_dim].astype(jnp.float32)
    out = jnp.concatenate([(x1 * cos - x2 * sin).astype(x.dtype),
                           (x1 * sin + x2 * cos).astype(x.dtype),
                           x[..., rot_dim:]], axis=-1)
    return out

def masked_softmax(s, mask):
    s = jnp.where(mask, s.astype(jnp.float32), NEG)
    return jax.nn.softmax(s, axis=-1) * mask

def retention(q, k, v, pos):
    B, S, H, Dh = q.shape
    q = rotary(q, pos, RET_ROPE_BASE, Dh).astype(jnp.float32) * (Dh ** -0.5)
    k = rotary(k, pos, RET_ROPE_BASE, Dh).astype(jnp.float32)
    v = v.astype(jnp.float32)
    log_g = jnp.log1p(-jnp.power(2.0, -5.0 - jnp.arange(H, dtype=jnp.float32)))
    C = RET_CHUNK
    N = S // C
    qc = q.reshape(B, N, C, H, Dh)
    kc = k.reshape(B, N, C, H, Dh)
    vc = v.reshape(B, N, C, H, Dh)
    idx = jnp.arange(C, dtype=jnp.float32)
    diff = idx[:, None] - idx[None, :]
    decay = jnp.where(diff[None] >= 0, jnp.exp(jnp.maximum(diff, 0.0)[None] * log_g[:, None, None]), 0.0)
    scores = jnp.einsum('bnihd,bnjhd->bnhij', qc, kc) * decay
    inner = jnp.einsum('bnhij,bnjhe->bnihe', scores, vc)
    zeta = jnp.exp((C - 1 - idx)[None, :] * log_g[:, None])
    kv_chunk = jnp.einsum('bnjhd,hj,bnjhe->nbhde', kc, zeta, vc)
    chunk_decay = jnp.exp(C * log_g)[None, :, None, None]

    def step(R, kv):
        return R * chunk_decay + kv, R

    _, R_prev = lax.scan(step, jnp.zeros((B, H, Dh, Dh), jnp.float32), kv_chunk)
    xi = jnp.exp((idx + 1.0)[None, :] * log_g[:, None])
    cross = jnp.einsum('bnihd,nbhde,hi->bnihe', qc, R_prev, xi)
    o = (inner + cross).reshape(B, S, H, Dh)
    mu = jnp.mean(o, axis=-1, keepdims=True)
    var = jnp.mean(jnp.square(o - mu), axis=-1, keepdims=True)
    return (o - mu) * lax.rsqrt(var + 1e-5)

def compress(t, pe, w1, w2):
    B, S, G, Dh = t.shape
    Nc = (S - CMP_BLOCK) // CMP_STRIDE + 1
    cidx = np.arange(Nc)[:, None] * CMP_STRIDE + np.arange(CMP_BLOCK)[None, :]
    blocks = t[:, cidx] + pe[None, None, :, None, :].astype(t.dtype)
    flat = blocks.transpose(0, 1, 3, 2, 4).reshape(B, Nc, G, CMP_BLOCK * Dh)
    return jax.nn.silu(flat @ w1) @ w2

def nsa(q, kv_all, gate_logits, pos, pe_k, w1_k, w2_k, pe_v, w1_v, w2_v):
    B, S, Hq, Dh = q.shape
    G, hpg = NSA_KV_GROUPS, HEADS_PER_GROUP
    kv = kv_all.reshape(B, S, 6, G, Dh)
    k_c, v_c, k_s, v_s, k_w, v_w = [kv[:, :, i] for i in range(6)]
    q = rotary(q, pos, NSA_ROPE_BASE, ROPE_DIM) * (Dh ** -0.5)
    k_s = rotary(k_s, pos, NSA_ROPE_BASE, ROPE_DIM)
    k_w = rotary(k_w, pos, NSA_ROPE_BASE, ROPE_DIM)
    Nc = (S - CMP_BLOCK) // CMP_STRIDE + 1
    NS = S // SLC_BLOCK
    topk = min(SLC_TOPK, NS)
    cmp_start = np.arange(Nc) * CMP_STRIDE
    cmp_end = cmp_start + CMP_BLOCK - 1
    slc_start = np.arange(NS) * SLC_BLOCK
    overlap = jnp.asarray(((cmp_start[:, None] <= slc_start[None, :] + SLC_BLOCK - 1) &
                           (cmp_end[:, None] >= slc_start[None, :])).astype(np.float32))
    kc = rotary(compress(k_c, pe_k, w1_k, w2_k), pos[:, cmp_end], NSA_ROPE_BASE, ROPE_DIM)
    vc = compress(v_c, pe_v, w1_v, w2_v)
    kcT = kc.transpose(0, 2, 1, 3)
    vcT = vc.transpose(0, 2, 1, 3)
    qg = q.reshape(B, S, G, hpg, Dh).transpose(0, 2, 3, 1, 4)
    ks_blk = k_s.reshape(B, NS, SLC_BLOCK, G, Dh).transpose(0, 3, 1, 2, 4)
    vs_blk = v_s.reshape(B, NS, SLC_BLOCK, G, Dh).transpose(0, 3, 1, 2, 4)
    pad = ((0, 0), (0, 0), (WINDOW, 0), (0, 0))
    kw_pad = jnp.pad(k_w.transpose(0, 2, 1, 3), pad)
    vw_pad = jnp.pad(v_w.transpose(0, 2, 1, 3), pad)
    bidx = jnp.arange(B)[:, None, None, None]
    gidx = jnp.arange(G)[None, :, None, None]
    blk_ids = jnp.arange(NS)

    def block(bi):
        t0 = bi * NSA_QBLK
        qb = lax.dynamic_slice_in_dim(qg, t0, NSA_QBLK, axis=3)
        tq = t0 + jnp.arange(NSA_QBLK)
        s = jnp.einsum('bghqd,bgnd->bghqn', qb, kcT)
        p_cmp = masked_softmax(s, cmp_end[None, :] <= tq[:, None])
        o_cmp = jnp.einsum('bghqn,bgnd->bghqd', p_cmp, vcT.astype(jnp.float32))
        imp = jnp.einsum('bghqn,ns->bgqs', p_cmp, overlap)
        cur = tq // SLC_BLOCK
        valid = blk_ids[None, :] <= cur[:, None]
        forced = (blk_ids[None, :] == 0) | (blk_ids[None, :] == cur[:, None]) | (blk_ids[None, :] == cur[:, None] - 1)
        score = jnp.where(forced, BIG, jnp.where(valid, imp, NEG))
        top_val, top_idx = lax.top_k(score, topk)
        kg = ks_blk[bidx, gidx, top_idx]
        vg = vs_blk[bidx, gidx, top_idx]
        s = jnp.einsum('bghqd,bgqnkd->bghqnk', qb, kg).reshape(B, G, hpg, NSA_QBLK, topk * SLC_BLOCK)
        tok = top_idx[..., None] * SLC_BLOCK + jnp.arange(SLC_BLOCK)
        m = (tok <= tq[None, None, :, None, None]) & (top_val > 0.5 * NEG)[..., None]
        p_slc = masked_softmax(s, m.reshape(B, G, 1, NSA_QBLK, topk * SLC_BLOCK))
        o_slc = jnp.einsum('bghqm,bgqmd->bghqd', p_slc,
                           vg.reshape(B, G, NSA_QBLK, topk * SLC_BLOCK, Dh).astype(jnp.float32))
        kwb = lax.dynamic_slice_in_dim(kw_pad, t0, WINDOW + NSA_QBLK, axis=2)
        vwb = lax.dynamic_slice_in_dim(vw_pad, t0, WINDOW + NSA_QBLK, axis=2)
        kp = t0 - WINDOW + jnp.arange(WINDOW + NSA_QBLK)
        mw = (kp[None, :] >= 0) & (kp[None, :] <= tq[:, None]) & (tq[:, None] - kp[None, :] < WINDOW)
        s = jnp.einsum('bghqd,bgkd->bghqk', qb, kwb)
        p_win = masked_softmax(s, mw)
        o_win = jnp.einsum('bghqk,bgkd->bghqd', p_win, vwb.astype(jnp.float32))
        return o_cmp, o_slc, o_win

    o_cmp, o_slc, o_win = lax.map(block, jnp.arange(S // NSA_QBLK))
    to_bshd = lambda o: o.transpose(1, 0, 4, 2, 3, 5).reshape(B, S, Hq, Dh)
    g = jax.nn.sigmoid(gate_logits.astype(jnp.float32)).reshape(B, S, Hq, 3)
    o = g[..., 0:1] * to_bshd(o_cmp) + g[..., 1:2] * to_bshd(o_slc) + g[..., 2:3] * to_bshd(o_win)
    return o

def first_inputs(seed: int = 0) -> dict:
    key = jax.random.key(seed)
    ks = jax.random.split(key, 20)
    f32 = jnp.float32
    nrm = lambda k, shape, scale: jax.random.normal(k, shape, f32) * scale
    x = jax.random.normal(ks[0], (BATCH, SEQ, D_MODEL), f32)
    c = jax.random.normal(ks[1], (BATCH, D_MODEL), f32)
    start = jax.random.randint(ks[2], (BATCH, 1), 0, 1024, dtype=jnp.int32)
    positions = start + jnp.arange(SEQ, dtype=jnp.int32)[None, :]
    return {
        "x": x,
        "c": c,
        "positions": positions,
        "w_ada": nrm(ks[3], (DEPTH, D_MODEL, 3 * D_MODEL), 0.5 * D_MODEL ** -0.5),
        "b_ada": nrm(ks[4], (DEPTH, 3 * D_MODEL), 0.02),
        "g_pre": 1.0 + nrm(ks[5], (DEPTH, D_MODEL), 0.05),
        "g_post": 1.0 + nrm(ks[6], (DEPTH, D_MODEL), 0.05),
        "w_in": nrm(ks[7], (DEPTH, D_MODEL, PROJ_WIDTH), D_MODEL ** -0.5),
        "w_out": nrm(ks[8], (DEPTH, MIX_WIDTH, D_MODEL), MIX_WIDTH ** -0.5),
        "cmp_pe_k": nrm(ks[9], (DEPTH, CMP_BLOCK, HEAD_DIM), 0.1),
        "cmp_w1_k": nrm(ks[10], (DEPTH, CMP_BLOCK * HEAD_DIM, CMP_HIDDEN), (CMP_BLOCK * HEAD_DIM) ** -0.5),
        "cmp_w2_k": nrm(ks[11], (DEPTH, CMP_HIDDEN, HEAD_DIM), CMP_HIDDEN ** -0.5),
        "cmp_pe_v": nrm(ks[12], (DEPTH, CMP_BLOCK, HEAD_DIM), 0.1),
        "cmp_w1_v": nrm(ks[13], (DEPTH, CMP_BLOCK * HEAD_DIM, CMP_HIDDEN), (CMP_BLOCK * HEAD_DIM) ** -0.5),
        "cmp_w2_v": nrm(ks[14], (DEPTH, CMP_HIDDEN, HEAD_DIM), CMP_HIDDEN ** -0.5),
    }

def first_block(x, c, positions, w_ada, b_ada, g_pre, g_post, w_in, w_out,
              cmp_pe_k, cmp_w1_k, cmp_w2_k, cmp_pe_v, cmp_w1_v, cmp_w2_v):
    B, S, _ = x.shape
    offsets = np.cumsum(SPLITS)[:-1].tolist()
    for l in range(DEPTH):
        mod = jax.nn.silu(c) @ w_ada[l] + b_ada[l]
        shift, scale, gate = jnp.split(mod, 3, axis=-1)
        h = rmsnorm(x, g_pre[l]) * (1.0 + scale[:, None, :]) + shift[:, None, :]
        proj = h @ w_in[l]
        rq, rk, rv, rg, nq, nkv, ngl, ng = jnp.split(proj, offsets, axis=-1)
        hd = lambda t, H: t.reshape(B, S, H, HEAD_DIM)
        ret = retention(hd(rq, RET_HEADS), hd(rk, RET_HEADS), hd(rv, RET_HEADS), positions)
        ret = ret.reshape(B, S, RET_WIDTH) * jax.nn.silu(rg.astype(jnp.float32))
        att = nsa(hd(nq, NSA_HEADS), nkv, ngl, positions,
                  cmp_pe_k[l], cmp_w1_k[l], cmp_w2_k[l], cmp_pe_v[l], cmp_w1_v[l], cmp_w2_v[l])
        att = att.reshape(B, S, NSA_WIDTH) * jax.nn.silu(ng.astype(jnp.float32))
        mixed = jnp.concatenate([ret, att], axis=-1).astype(x.dtype)
        y = rmsnorm(mixed @ w_out[l], g_post[l])
        x = x + gate[:, None, :].astype(x.dtype) * y
    return x


MEM_LEN = 256
CONV_CH = 512
CONV_GROUPS = 8
CONV_WIDTH = 3
MOBA_HEADS = 8
MOBA_HEAD_DIM = 64
MOBA_WIDTH = MOBA_HEADS * MOBA_HEAD_DIM
MOBA_BLOCK = 256
MOBA_TOPK = 3
MOBA_QCHUNK = 16
MEM_HEADS = 4
MEM_HEAD_DIM = 128
MEM_WIDTH = MEM_HEADS * MEM_HEAD_DIM
N_BRANCH = 3
IN_SPLITS = [CONV_CH, CONV_CH, CONV_CH, MOBA_WIDTH, MOBA_WIDTH, MOBA_WIDTH, MEM_WIDTH,
             D_MODEL, D_MODEL, D_MODEL]
IN_COLS = sum(IN_SPLITS)
D_FF = 2816
FFN_CONV_WIDTH = 3


def rmsnorm_2(x, g):
    xf = x.astype(jnp.float32)
    y = xf * lax.rsqrt(jnp.mean(xf * xf, axis=-1, keepdims=True) + EPS)
    return y.astype(x.dtype) * g

def causal_dwconv3(u, w, b):
    s = u.shape[1]
    up = jnp.pad(u, ((0, 0), (2, 0), (0, 0)))
    return up[:, :s] * w[0] + up[:, 1:s + 1] * w[1] + up[:, 2:] * w[2] + b

def moba_attention(q, k, v):
    bsz, s, h, dh = q.shape
    L = MOBA_BLOCK
    nb = -(-s // L)
    sp = nb * L
    pad = ((0, 0), (0, sp - s), (0, 0), (0, 0))
    q, k, v = jnp.pad(q, pad), jnp.pad(k, pad), jnp.pad(v, pad)
    qh = q.transpose(0, 2, 1, 3)
    kb = k.reshape(bsz, nb, L, h, dh).transpose(0, 3, 1, 2, 4)
    vb = v.reshape(bsz, nb, L, h, dh).transpose(0, 3, 1, 2, 4)
    kbar = jnp.mean(kb, axis=3)
    n_sel = min(MOBA_TOPK, nb - 1)
    scale = dh ** -0.5
    gather = jax.vmap(jax.vmap(lambda blocks, idx: blocks[idx]))

    def one_chunk(ci):
        start = ci * MOBA_QCHUNK
        own = start // L
        qc = lax.dynamic_slice_in_dim(qh, start, MOBA_QCHUNK, axis=2)
        qpos = start + jnp.arange(MOBA_QCHUNK)
        kpos = own * L + jnp.arange(L)
        k_own = lax.dynamic_index_in_dim(kb, own, axis=2, keepdims=False)
        v_own = lax.dynamic_index_in_dim(vb, own, axis=2, keepdims=False)
        s_own = jnp.einsum('bhqd,bhkd->bhqk', qc, k_own).astype(jnp.float32) * scale
        s_own = jnp.where(kpos[None, :] <= qpos[:, None], s_own, -jnp.inf)
        if n_sel == 0:
            p = jax.nn.softmax(s_own, axis=-1).astype(v.dtype)
            return jnp.einsum('bhqk,bhkd->bhqd', p, v_own)
        gate = jnp.einsum('bhqd,bhnd->bhqn', qc, kbar)
        gate = jnp.where(jnp.arange(nb) < own, gate, -jnp.inf)
        _, idx = lax.top_k(gate, n_sel)
        valid = idx < own
        k_sel = gather(kb, idx)
        v_sel = gather(vb, idx)
        s_sel = jnp.einsum('bhqd,bhqnkd->bhqnk', qc, k_sel).astype(jnp.float32) * scale
        s_sel = jnp.where(valid[..., None], s_sel, -jnp.inf)
        s_sel = s_sel.reshape(bsz, h, MOBA_QCHUNK, n_sel * L)
        p = jax.nn.softmax(jnp.concatenate([s_sel, s_own], axis=-1), axis=-1).astype(v.dtype)
        p_sel = p[..., :n_sel * L].reshape(bsz, h, MOBA_QCHUNK, n_sel, L)
        p_own = p[..., n_sel * L:]
        return (jnp.einsum('bhqnk,bhqnkd->bhqd', p_sel, v_sel)
                + jnp.einsum('bhqk,bhkd->bhqd', p_own, v_own))

    out = lax.map(one_chunk, jnp.arange(sp // MOBA_QCHUNK))
    out = out.transpose(1, 0, 3, 2, 4).reshape(bsz, sp, h * dh)
    return out[:, :s]

def memory_cross_attention(q_m, mem_n, w_mem_kv, memq_gain, memk_gain):
    bsz, s, _ = q_m.shape
    m = mem_n.shape[1]
    q = rmsnorm_2(q_m.reshape(bsz, s, MEM_HEADS, MEM_HEAD_DIM), memq_gain)
    k_m, v_m = jnp.split(mem_n @ w_mem_kv, 2, axis=-1)
    k = rmsnorm_2(k_m.reshape(bsz, m, MEM_HEADS, MEM_HEAD_DIM), memk_gain)
    v = v_m.reshape(bsz, m, MEM_HEADS, MEM_HEAD_DIM)
    sc = jnp.einsum('bshd,bmhd->bhsm', q, k).astype(jnp.float32) * (MEM_HEAD_DIM ** -0.5)
    p = jax.nn.softmax(sc, axis=-1).astype(v.dtype)
    o = jnp.einsum('bhsm,bmhd->bshd', p, v)
    return o.reshape(bsz, s, MEM_WIDTH)

def second_inputs(seed: int = 0) -> dict:
    key = jax.random.key(seed)
    ks = jax.random.split(key, 24)
    nrm = lambda k, shape, scale: jax.random.normal(k, shape, jnp.float32) * scale
    D = D_MODEL
    return {
        "x": nrm(ks[0], (BATCH, SEQ, D), 1.0),
        "mem": nrm(ks[1], (BATCH, MEM_LEN, D), 1.0),
        "g_mix": 1.0 + nrm(ks[2], (D,), 0.02),
        "w_in": nrm(ks[3], (D, IN_COLS), D ** -0.5),
        "b_gate": nrm(ks[4], (N_BRANCH * D,), 0.02),
        "conv_w": nrm(ks[5], (CONV_WIDTH, CONV_CH), CONV_WIDTH ** -0.5),
        "conv_b": nrm(ks[6], (CONV_CH,), 0.02),
        "moba_q_gain": 1.0 + nrm(ks[7], (MOBA_HEAD_DIM,), 0.02),
        "moba_k_gain": 1.0 + nrm(ks[8], (MOBA_HEAD_DIM,), 0.02),
        "g_mem": 1.0 + nrm(ks[9], (D,), 0.02),
        "w_mem_kv": nrm(ks[10], (D, 2 * MEM_WIDTH), D ** -0.5),
        "memq_gain": 1.0 + nrm(ks[11], (MEM_HEAD_DIM,), 0.02),
        "memk_gain": 1.0 + nrm(ks[12], (MEM_HEAD_DIM,), 0.02),
        "w_br_conv": nrm(ks[13], (CONV_CH, D), CONV_CH ** -0.5),
        "w_br_moba": nrm(ks[14], (MOBA_WIDTH, D), MOBA_WIDTH ** -0.5),
        "w_br_mem": nrm(ks[15], (MEM_WIDTH, D), MEM_WIDTH ** -0.5),
        "w_o": nrm(ks[16], (D, D), D ** -0.5),
        "g_ffn": 1.0 + nrm(ks[17], (D,), 0.02),
        "w_up": nrm(ks[18], (D, 2 * D_FF), D ** -0.5),
        "ffn_conv_w": nrm(ks[19], (FFN_CONV_WIDTH, D_FF), FFN_CONV_WIDTH ** -0.5),
        "ffn_conv_b": nrm(ks[20], (D_FF,), 0.02),
        "w_down": nrm(ks[21], (D_FF, D), D_FF ** -0.5),
    }

def second_block(x, mem, g_mix, w_in, b_gate, conv_w, conv_b, moba_q_gain, moba_k_gain,
              g_mem, w_mem_kv, memq_gain, memk_gain, w_br_conv, w_br_moba, w_br_mem,
              w_o, g_ffn, w_up, ffn_conv_w, ffn_conv_b, w_down):
    bsz, s, D = x.shape
    mem_n = rmsnorm_2(mem, g_mem)
    for _ in range(DEPTH):
        h = rmsnorm_2(x, g_mix)
        proj = h @ w_in
        cuts = list(np.cumsum(IN_SPLITS)[:-1])
        (c_b, c_c, c_x, q, k, v, q_m, g1, g2, g3) = jnp.split(proj, cuts, axis=-1)
        bg1, bg2, bg3 = jnp.split(b_gate, N_BRANCH)

        y_conv = c_b * causal_dwconv3(c_c * c_x, conv_w, conv_b)

        qh = rmsnorm_2(q.reshape(bsz, s, MOBA_HEADS, MOBA_HEAD_DIM), moba_q_gain)
        kh = rmsnorm_2(k.reshape(bsz, s, MOBA_HEADS, MOBA_HEAD_DIM), moba_k_gain)
        vh = v.reshape(bsz, s, MOBA_HEADS, MOBA_HEAD_DIM)
        y_moba = moba_attention(qh, kh, vh)

        y_mem = memory_cross_attention(q_m, mem_n, w_mem_kv, memq_gain, memk_gain)

        merged = (jax.nn.sigmoid(g1 + bg1) * (y_conv @ w_br_conv)
                  + jax.nn.sigmoid(g2 + bg2) * (y_moba @ w_br_moba)
                  + jax.nn.sigmoid(g3 + bg3) * (y_mem @ w_br_mem))
        x = x + merged @ w_o

        h2 = rmsnorm_2(x, g_ffn)
        a, b = jnp.split(h2 @ w_up, 2, axis=-1)
        a = causal_dwconv3(a, ffn_conv_w, ffn_conv_b)
        x = x + (jax.nn.silu(a) * b) @ w_down
    return x


def setup_inputs(seed=0):
    out = dict(first_inputs(seed))
    for name, value in second_inputs(seed + 1).items():
        if name != "x":
            out[name + "_2"] = value
    return out


def reference(
    x, c, positions, w_ada, b_ada, g_pre, g_post, w_in, w_out, cmp_pe_k, cmp_w1_k, cmp_w2_k,
    cmp_pe_v, cmp_w1_v, cmp_w2_v, mem_2, g_mix_2, w_in_2, b_gate_2, conv_w_2, conv_b_2,
    moba_q_gain_2, moba_k_gain_2, g_mem_2, w_mem_kv_2, memq_gain_2, memk_gain_2, w_br_conv_2,
    w_br_moba_2, w_br_mem_2, w_o_2, g_ffn_2, w_up_2, ffn_conv_w_2, ffn_conv_b_2, w_down_2,
):
    x = first_block(
        x, c, positions, w_ada, b_ada, g_pre, g_post, w_in, w_out, cmp_pe_k, cmp_w1_k, cmp_w2_k,
        cmp_pe_v, cmp_w1_v, cmp_w2_v,
    )
    return second_block(
        x, mem_2, g_mix_2, w_in_2, b_gate_2, conv_w_2, conv_b_2, moba_q_gain_2, moba_k_gain_2,
        g_mem_2, w_mem_kv_2, memq_gain_2, memk_gain_2, w_br_conv_2, w_br_moba_2, w_br_mem_2,
        w_o_2, g_ffn_2, w_up_2, ffn_conv_w_2, ffn_conv_b_2, w_down_2,
    )


_drawn_inputs = setup_inputs


def setup_inputs(seed=0):
    import zlib

    import numpy as np

    out = dict(_drawn_inputs(seed))
    spreads = {}
    factors = {'g_post': 2.691,
     'cmp_pe_k': 8.0,
     'cmp_pe_v': 6.545,
     'g_mix_2': 3.185,
     'b_gate_2': 8.0,
     'conv_b_2': 26.444,
     'moba_q_gain_2': 32.975,
     'moba_k_gain_2': 32.206,
     'g_mem_2': 8.0,
     'memq_gain_2': 8.0,
     'memk_gain_2': 8.0,
     'g_ffn_2': 16.209,
     'ffn_conv_b_2': 22.848}
    for name, (base, spread) in spreads.items():
        noise = np.random.default_rng([zlib.crc32(name.encode()), seed]).standard_normal(out[name].shape)
        drawn = base * np.exp(spread * noise) if base else spread * noise
        out[name] = __import__('jax').numpy.asarray(drawn.astype(out[name].dtype))
    for name, factor in factors.items():
        out[name] = (out[name] * factor).astype(out[name].dtype)
    return out
```

```python
from contextlib import ExitStack

import numpy as np

import concourse.bass as bass
from concourse import mybir

ALU = mybir.AluOpType
ACT = mybir.ActivationFunctionType
F32 = mybir.dt.float32
F32R = mybir.dt.float32r
BF16 = mybir.dt.bfloat16
I32 = mybir.dt.int32
AX_X = mybir.AxisListType.X

P = 128
S = 512
D = 1024
NT = S // P
H = 8
DH = 64
MEM = 256
MH, MDH = 4, 128
KT = D // P
NCMP = 31
DFF = 2816
EPS = 1e-6
NEG = -1e30
TWO_PI_A = 6.28125
TWO_PI_B = float(np.float32(np.float16(2 * np.pi - TWO_PI_A)))
TWO_PI_C = float(2 * np.pi - TWO_PI_A - TWO_PI_B)
ROUND = 12582912.0
NF_RET, NF_NSA = 32, 8
NF = NF_RET + NF_NSA

C_INV, C_VSC, C_XI, C_TRI = 0, NF, NF + 8, NF + 16
C_ID = C_TRI + P
C_DEC = C_ID + P
C_CMPB = C_DEC + 4
C_ROW = C_CMPB + NT * 32
CST = C_ROW + NT
N_CONST, N_PARAM = 7, 21


def constants():
    c = np.zeros((P, CST), np.float32)
    f = np.float32
    c[:, C_INV:C_INV + NF_RET] = np.power(f(10000.0), -np.arange(NF_RET, dtype=f) / f(NF_RET))
    c[:, C_INV + NF_RET:C_INV + NF] = np.power(f(500000.0), -np.arange(NF_NSA, dtype=f) / f(NF_NSA))
    log_g = np.log1p(-np.power(2.0, -5.0 - np.arange(H)))
    p = np.arange(P)
    c[:, C_VSC:C_VSC + H] = np.exp(-(p[:, None] + 1.0) * log_g)
    even_odd = [0, 2, 4, 6, 1, 3, 5, 7]
    c[:, C_XI:C_XI + H] = np.exp((p[:, None] + 1.0) * log_g[even_odd])
    c[:, C_TRI:C_TRI + P] = p[:, None] <= p[None, :]
    for h in range(H):
        c[(h % 2) * DH:(h % 2) * DH + DH, C_DEC + h // 2] = np.exp(P * log_g[h])
    c[:, C_ID:C_ID + P] = np.eye(P, dtype=f)
    for t in range(NT):
        for n in range(32):
            ok = (n < NCMP) & (16 * n + 31 <= t * P + p)
            c[:, C_CMPB + t * 32 + n] = np.where(ok, 0.0, NEG)
        c[:, C_ROW + t] = (t * P + p >= 31)
    return c


PANELS1 = [
    ("N1", 2560, 512), ("N2", 3072, 280), ("NQ", 2048, 512), ("RQ", 0, 512), ("RK", 512, 512),
    ("RV", 1024, 512), ("NG", 3352, 512), ("RG", 1536, 512)]
PANELS2 = [("Q", "A", 1536), ("K", "A", 2048), ("V", "A", 2560), ("QM", "A", 3072),
           ("CC", "B", 512), ("CX", "B", 1024), ("CB", "B", 0)]
GATE0 = 3584
FFN_GROUPS = [4, 4, 4, 4, 4, 2]


class Plan:

    def __init__(self):
        self.beats, self.steps, self.units, self.src = [], [], [], []

    def panel(self, name, form, cols, srcs, tiles=4, base=0, n=512, **more):
        first = len(self.beats)
        for i, s in enumerate(srcs):
            self.units.append(s)
            for j in range(tiles):
                self.beats.append(dict(name=name, form=form, u=len(self.units) - 1, j=j, n=n,
                                       first=i == 0, last=i == len(srcs) - 1,
                                       kts=[(base[i] + q, q) for q in range(4)], steps=[],
                                       unit_first=j == 0, bank=j, **more))
        return first

    def step(self, start, **s):
        s["k"] = len(self.steps)
        self.steps.append(s)
        self.beats[start]["steps"].append(s["k"])
        return s["k"]


def segments(family):
    for a in range(0, H, 4):
        for e in range(2):
            for h in (a + e, a + e + 2):
                yield [(h, 3, 0)]
                yield [(h, 0, 0), (h, 2, P)]
            yield [(a + e, 1, 0), (a + e + 2, 1, 2 * P)]


def make_plan():
    pl = Plan()
    step, beats = pl.step, pl.beats
    b0 = {}
    for name, c0, n in PANELS1:
        b0[name] = pl.panel(name, "A", c0, [("w_in", 512 * i, c0, n) for i in range(2)], base=[0, 4], n=n)
    for j in range(NT):
        step(b0["N1"] + 4 + j, kind="tr", to="n1", j=j, nb=4, beat=b0["N1"] + 4 + j)
    step(b0["N2"], kind="nop")
    for j in range(NT):
        step(b0["N2"] + 4 + j, kind="tr", to="n2", j=j, nb=2, beat=b0["N2"] + 4 + j)
    step(b0["NQ"], kind="nop")
    pl.cmv = step(b0["NQ"] + 1, kind="cmv")
    step(b0["NQ"] + 2, kind="hid")
    step(b0["NQ"] + 3, kind="kct")
    for j in range(NT):
        step(b0["NQ"] + 4 + j, kind="tr", to="nq", j=j, nb=4, beat=b0["NQ"] + 4 + j)
    step(b0["RQ"], kind="gates")
    todo = [dict(kind="cmp", j=t) for t in range(NT)]
    for br in range(2):
        todo += [dict(kind="sm", fam="nsa", br=br, segs=s) for s in segments("nsa")]
    at = b0["RQ"] + 1
    while at < b0["NG"] + 3:
        b = beats[at]
        if b["name"] in ("RQ", "RK") and b["last"]:
            step(at, kind="tr", to=b["name"].lower(), j=b["j"], nb=4, beat=at)
        for _ in range(1 if b["last"] else 2):
            if todo:
                step(at, **todo.pop(0))
        at += 1
    while todo:
        step(b0["NG"] + 3, **todo.pop(0))
    step(b0["NG"] + 3, kind="nop")
    step(b0["NG"] + 3, kind="nop")
    ret = [dict(kind="ret", j=n, half=h) for n in range(NT) for h in range(2)]
    at = b0["NG"] + 4
    for n in range(NT):
        for h in range(2):
            step(at, kind="ret", j=n, half=h)
            if beats[at]["name"] == "NG":
                step(at, kind="trh", src="att", j=at - b0["NG"] - 4, kt=12, beat=at)
            at += 1
        if n:
            step(at - 1, kind="gn", j=n - 1)
    step(at, kind="nop")
    step(at, kind="gn", j=3)
    for j in range(NT):
        step(b0["RG"] + 4 + j, kind="trh", src="ret", j=j, kt=8, beat=b0["RG"] + 4 + j)
    wo = [pl.panel("WO", "A", c, [("w_out", 512 * i, 512 * c, 512) for i in range(2)], base=[8, 12], c=c)
          for c in range(2)]
    step(wo[0] - 1, kind="nop")
    step(wo[0] - 1, kind="nop")
    for i in range(2):
        step(wo[0] + 2 * i, kind="mnorm", j=i)
        step(wo[0] + 2 * i + 1, kind="nop")
        for half in range(2):
            step(wo[0] + 2 * i + 1, kind="trh", src="mem", j=i, half=half, kt=4 * half, scale="g_mem")
    step(wo[0] + 4, kind="nop")
    step(wo[0] + 4, kind="nop")
    mk = pl.panel("MK", "A", 0, [("w_mem", 512 * i, 0, 512) for i in range(2)], tiles=2, base=[0, 4])
    mv = pl.panel("MV", "A", 1, [("w_mem", 512 * i, 512, 512) for i in range(2)], tiles=2, base=[0, 4])
    where = [wo[1] + 5, wo[1] + 7, mk + 1, mk + 3]
    for j in range(NT):
        step(where[j], kind="j1", j=j, beat=wo[1] + 4 + j)
        step(where[j], kind="j2", j=j, which=0)
        step(where[j], kind="nop")
        for half in range(2):
            step(where[j], kind="trh", src="x", j=j, half=half, kt=8 + 4 * half, scale="g_mix")
    for j in range(2):
        step(mk + 3, kind="qn", src="mk", j=j, nh=MH, beat=mk + 2 + j)
        step(mk + 3, kind="tr", to="mk", j=j, nb=4, beat=mk + 2 + j)
    step(mv, kind="nop")
    step(mv, kind="nop")
    e0 = {}
    for name, form, c0 in PANELS2:
        e0[name] = pl.panel(name, form, c0, [("w_in_2", 512 * i, c0, 512) for i in range(2)], base=[8, 12])
    for name in ("Q", "K", "QM"):
        for j in range(NT):
            b = e0[name] + 4 + j
            step(b, kind="qn", src=name, j=j, nh=MH if name == "QM" else H, beat=b)
            step(b, kind="tr", to=name, j=j, nb=4, beat=b)
        step(b + 1, kind="nop")
    branches = [("conv", 0, 0), ("mem", 2, 4), ("moba", 1, 0)]
    g0 = {}
    for i, (name, gi, base) in enumerate(branches):
        for c in range(2):
            col = GATE0 + D * gi + 512 * c
            g0[name, c] = pl.panel("G", "B", col, [("w_in_2", 512 * q, col, 512) for q in range(2)],
                                   base=[8, 12], gi=gi, c=c)
            pl.panel("B", "B", c, [("w_br_" + name, 0, 512 * c, 512)], base=[base], i=i, c=c)
    todo = []
    for t in range(NT):
        todo += [dict(kind="sm", fam="mem", segs=[(2 * a, t, 0), (2 * a + 1, t, MEM)]) for a in range(2)]
        todo += [dict(kind="nop"), dict(kind="trh", src="ymem", j=t, kt=4)]
    todo += [dict(kind="sm", fam="moba", segs=s) for s in segments("moba")]
    todo += [dict(kind="nop")] * 2
    todo += [dict(kind="trh", src="ymoba", j=t, kt=0) for t in range(NT)] + [dict(kind="nop")]
    at = e0["CC"] + 1
    while len(todo) > 5:
        step(at, **todo.pop(0))
        if beats[at]["name"] == "CC" or todo[0]["kind"] == "nop":
            step(at, **todo.pop(0))
        at += 1
    assert at < g0["conv", 0] + 8
    at = g0["mem", 0]
    while todo:
        step(at, **todo.pop(0))
        at += 1
    w2 = [pl.panel("WY", "A", c, [("w_o", 512 * i, 512 * c, 512) for i in range(2)], base=[4, 8], c=c)
          for c in range(2)]
    for j in range(NT):
        at = w2[1] + min(5 + j, 7)
        step(at, kind="j2", j=j, which=1, beat=w2[1] + 4 + j)
        step(at, kind="nop")
        for half in range(2):
            step(at, kind="trh", src="x2", j=j, half=half, kt=12 if half == 0 else 0, scale="g_ffn")
    for _ in range(2):
        step(w2[1] + 7, kind="nop")
    ch = 0
    for g, nt in enumerate(FFN_GROUPS):
        act = 4 if g % 2 == 0 else 8
        n = nt * P
        if nt == 4:
            pl.panel("UA", "B", 0, [("w_up", 512 * i, ch, n) for i in range(2)], base=[12, 0], ch=ch // P, act=act)
            pl.panel("UB", "B", 0, [("w_up", 512 * i, DFF + ch, n) for i in range(2)], base=[12, 0], ch=ch // P,
                     act=act)
            for c in range(2):
                pl.panel("DN", "A", c, [("w_down", ch, 512 * c, 512)], base=[act], c=c, final=False)
        else:
            f = pl.panel("UX", "B", 0, [("w_up2", 512 * i, ch, n) for i in range(2)], base=[12, 0], ch=ch // P,
                         act=act, packed=True)
            for b in beats[f:]:
                b["name"] = "UA" if b["j"] < 2 else "UB"
            pl.units.append(("w_down2", ch, 0, 0))
            for c in range(2):
                for j in range(NT):
                    beats.append(dict(name="DN", form="A", u=len(pl.units) - 1, j=j, n=512, first=True, last=True,
                                      kts=[(act + q, 2 * q + c) for q in range(2)], steps=[], bank=j,
                                      unit_first=c == 0 and j == 0, c=c, final=True))
        ch += n
    for i, b in enumerate(beats):
        b["b"] = i
    return finish_plan(pl)


def has(s, phase):
    kind = s["kind"]
    return phase in {
        "nop": (), "tr": ("turn", "take"), "trh": ("turn", "take"), "cmv": ("rows",),
        "hid": ("scores", "probs", "turn", "take"), "kct": ("turn", "take"), "gates": ("probs",),
        "cmp": ("scores", "rows", "probs", "turn", "take", "values", "out"),
        "sm": ("scores", "rows", "probs", "turn", "take", "values", "out"),
        "ret": ("scores", "rows", "turn", "take", "values", "out") if s.get("j") != 3 else
        ("scores", "rows", "values", "out"),
        "gn": ("rows", "probs"), "mnorm": ("probs", "take"), "j1": ("probs", "take"), "j2": ("probs", "take"),
        "qn": ("probs", "take"),
    }[kind]


def finish_plan(pl):
    pl.count = {}
    for phase in ("scores", "rows", "probs", "turn", "values", "out"):
        n, at = 0, []
        for s in pl.steps:
            n += has(s, phase)
            at.append(n)
        pl.count[phase] = at
    for who in ("act", "dve"):
        n, at = 0, []
        for s in pl.steps:
            n += has(s, "take") and (s["kind"] == "sm") == (who == "act")
            at.append(n)
        pl.count["take_" + who] = at
    na = nd = 0
    for b in pl.beats:
        b["evac"] = None
        if b["last"]:
            b["evac"] = "act" if b["name"] in ("CC", "G") else "dve"
            if b["evac"] == "act":
                na += 1
                b["evac_n"] = na
            else:
                nd += 1
                b["evac_n"] = nd
    pl.unit_end = {}
    for b in pl.beats:
        pl.unit_end[b["u"]] = b["b"]
    last = {}
    for b in pl.beats:
        if b["first"]:
            b["bank_prev"] = last.get(b["bank"])
        if b["last"]:
            last[b["bank"]] = b["b"]
    for s in pl.steps:
        s["in_beat"] = next(b["b"] for b in pl.beats if s["k"] in b["steps"])
    n = 0
    prev = {}
    pl.src_of_beat = {}
    pl.src_mem = {}
    uses = [s for s in pl.steps if (s["kind"] == "tr" and s["to"] != "rk") or s["kind"] == "trh" and s["src"] == "ymem"]
    uses.sort(key=lambda s: s["k"])
    for s in uses:
        s["slot"] = n % 2
        s["slot_prev"] = prev.get(n % 2)
        prev[n % 2] = s["k"]
        if s["kind"] == "tr":
            pl.src_of_beat[s["beat"]] = s
        else:
            pl.src_mem[s["j"]] = s
        n += 1
    for s in pl.steps:
        if s["kind"] == "qn":
            s["slot"] = pl.src_of_beat[s["beat"]]["slot"]
    return pl


def kib(arena, a, n):
    return arena[:, a * 256:(a + n) * 256]


def build(nc, t_in, out):
    pl = make_plan()
    beats, steps, units, count = pl.beats, pl.steps, pl.units, pl.count
    NU = len(units)
    with ExitStack() as ctx:
        def sb(name, shape, dt=F32):
            return ctx.enter_context(nc.sbuf_tensor(name, shape, dt))

        def ps(name):
            return ctx.enter_context(nc.psum_tensor(name, [P, 512], F32))

        def sem(name):
            return ctx.enter_context(nc.semaphore(name))

        raw = sb("raw", [P, 2, 2048])
        w_hi = sb("w_hi", [P, 2, 4, 512], F32R)
        w_lo = sb("w_lo", [P, 2, 4, 512], F32R)
        a_hi = sb("a_hi", [P, 16, S], F32R)
        a_lo = sb("a_lo", [P, 16, S], F32R)
        arena = sb("arena", [P, 84 * 256])
        cst = sb("cst", [P, CST])
        idb = sb("idb", [P, P], BF16)
        maskb = sb("maskb", [P, P], BF16)
        rope_c = sb("rope_c", [P, 5, NF])
        rope_s = sb("rope_s", [P, 5, NF])
        gp = sb("gp", [P, D])
        cols = sb("cols", [P, 160])
        ffw = sb("ffw", [P, 4, 22])
        w2s = sb("w2s", [P, 2, 2, DH])
        small = sb("small", [P, 160])
        posi = sb("posi", [P, 5], I32)
        ident = cst[:, C_ID:C_ID + P]
        tri = cst[:, C_TRI:C_TRI + P]
        cmpb = cst[:, C_CMPB:C_CMPB + NT * 32].rearrange("p (t n) -> p t n", t=NT)

        def view(start, size, pat=None, **kw):
            v = kib(arena, start, size)
            return v.rearrange(pat, **kw) if pat else v

        ada_w = view(0, 64, "p (s k n) -> p s k n", s=4, k=KT)
        x0 = view(64, 16, "p (t d) -> p t d", t=NT)
        gpost = view(56, 4)
        stage = view(32, 2, "p (b n) -> p b n", b=4)
        scb = view(80, 4, "p (k m) -> p k m", k=KT)
        tmp = view(80, 4, "p (s n) -> p s n", s=2)
        ncT = view(0, 8, "p (b n) -> p b n", b=4)
        nqT = view(8, 8, "p (b n) -> p b n", b=4)
        w1 = view(16, 32, "p (v m n) -> p v m n", v=2, m=16)
        cblk = view(48, 8, "p (v g n) -> p v g n", v=2, g=2)
        cmv = view(56, 8, "p (v m g n) -> p v m g n", v=2, m=16, g=2)
        kvT = view(68, 4, "p (v n) -> p v n", v=2)
        rqT = view(16, 8, "p (b n) -> p b n", b=4)
        rkT = view(24, 8, "p (b n) -> p b n", b=4)
        rk = view(32, 8, "p (t n) -> p t n", t=NT)
        rv = view(40, 8, "p (t n) -> p t n", t=NT)
        att = view(48, 8, "p (t n) -> p t n", t=NT)
        prob = view(56, 4, "p (s n) -> p s n", s=2)
        probT = view(60, 4, "p (s n) -> p s n", s=2)
        src = view(64, 4, "p (s n) -> p s n", s=2)
        Rst = view(68, 2, "p (s c e) -> p s c e", s=2, c=4)
        vsel = view(72, 2, "p (t n) -> p t n", t=NT)
        vwin = view(74, 2, "p (t n) -> p t n", t=NT)
        vbd = view(76, 2, "p (g r n) -> p g r n", g=2, r=4)
        kcT = arena[:, 78 * 256:78 * 256 + 128].rearrange("p (g e n) -> p g e n", g=2, e=2)
        kcr = arena[:, 78 * 256 + 128:78 * 256 + 256]
        sg = view(0, 8, "p (t n) -> p t n", t=NT)
        yo = view(16, 16, "p (t d) -> p t d", t=NT)
        x1 = view(0, 16, "p (t d) -> p t d", t=NT)
        memr = view(40, 8, "p (t d) -> p t d", t=2)
        xn = view(68, 4)
        kmT = view(72, 4, "p (h n) -> p h n", h=MH)
        vm = view(48, 4, "p (t n) -> p t n", t=2)
        qT = view(16, 8, "p (b n) -> p b n", b=4)
        kT = view(24, 8, "p (b n) -> p b n", b=4)
        vmo = view(32, 8, "p (t n) -> p t n", t=NT)
        qmT = view(40, 8, "p (b n) -> p b n", b=4)
        ymo = view(0, 8, "p (t n) -> p t n", t=NT)
        ucv = view(8, 8, "p (t n) -> p t n", t=NT)
        tg = view(8, 8, "p (t n) -> p t n", t=NT)
        merged = view(16, 16, "p (t n) -> p t n", t=8)
        x2 = view(32, 16, "p (t d) -> p t d", t=NT)
        fcv = view(8, 8, "p (t n) -> p t n", t=NT)
        fsi = view(0, 8, "p (t n) -> p t n", t=NT)

        x1_dram = nc.dram_tensor("x1_scratch", [S, D], F32).ap()

        CI = {}
        at = 0
        for name, n in (("c", 8), ("sc", 8), ("b_ada", 24), ("g_pre", 8), ("ca", 8), ("cb", 8), ("g_mem", 8),
                        ("g_mix", 8), ("g_ffn", 8), ("b_gate", 24), ("conv_w", 12), ("conv_b", 4), ("gq", 1),
                        ("gk", 1), ("gmq", 1), ("gmk", 1), ("eps", 1), ("epsg", 1)):
            CI[name] = cols[:, at:at + n]
            at += n
        assert at <= 160
        cpe = sb("cpe", [P, 2, 16])
        glog = sb("glog", [P, NT, 24])
        nmax = sb("nmax", [P, 4, 2])
        rsum = sb("rsum", [P, 4, 2])
        st8 = small[:, 0:8]
        rs8 = small[:, 8:16]
        cf8 = small[:, 16:24]
        gvar = small[:, 24:56].rearrange("p (t n) -> p t n", t=NT)
        ri = small[:, 56:58]
        cf = small[:, 58:60]
        ss = small[:, 60:64]
        sd = small[:, 64:68]
        rr = small[:, 68:72]
        qss = small[:, 72:88].rearrange("p (s n) -> p s n", s=2)
        qsd = small[:, 88:104].rearrange("p (s n) -> p s n", s=2)
        qri = small[:, 104:112]

        pj = [ps(f"pj{i}") for i in range(4)]
        sc = [ps(f"sc{i}") for i in range(2)]
        pt = ps("pt")
        po = ps("po")

        consts_in = sem("consts_in")
        params_in = sem("params_in")
        gpost_in = sem("gpost_in")
        x_in = sem("x_in")
        ada_in = [sem(f"ada_in{i}") for i in range(4)]
        mem_in = sem("mem_in")
        xres_in = sem("xres_in")
        w1_in = sem("w1_in")
        gather_in = sem("gather_in")
        x1_saved = sem("x1_saved")
        x1_back = sem("x1_back")
        out_saved = sem("out_saved")
        raw_in = [sem(f"raw_in{i}") for i in range(2)]
        hi_ready = sem("hi_ready")
        lo_ready = sem("lo_ready")
        beat_done = sem("beat_done")
        scores_ready = sem("scores_ready")
        turned = sem("turned")
        values_ready = sem("values_ready")
        rows_ready = sem("rows_ready")
        probs_ready = sem("probs_ready")
        taken_act = sem("taken_act")
        taken_dve = sem("taken_dve")
        out_taken = sem("out_taken")
        evac_act = sem("evac_act")
        evac_dve = sem("evac_dve")
        ready_dve = sem("ready_dve")
        ready_act = sem("ready_act")
        ready_pe = sem("ready_pe")
        pair_act = sem("pair_act")
        chain_dve = sem("chain_dve")
        chain_act = sem("chain_act")

        pair_n = {}
        n = 0
        for b in beats:
            if b["last"] and b["name"] in ("NG", "RG", "UA"):
                n += 1
                pair_n[b["b"]] = n

        def wait_beat(eng, b):
            eng.wait_ge(beat_done, b + 1)

        def wait_evac(eng, b):
            if beats[b]["evac"] == "act":
                eng.wait_ge(evac_act, beats[b]["evac_n"])
            else:
                eng.wait_ge(evac_dve, beats[b]["evac_n"])

        def wait_taken(eng, k):
            if steps[k]["kind"] == "sm":
                eng.wait_ge(taken_act, count["take_act"][k])
            else:
                eng.wait_ge(taken_dve, count["take_dve"][k])

        def wait_probs_slot(eng, k):
            if k < 2:
                return
            s = steps[k - 2]
            if s["kind"] == "ret":
                eng.wait_ge(values_ready, count["values"][k - 2])
            elif s["kind"] in ("sm", "cmp", "hid"):
                eng.wait_ge(turned, count["turn"][k - 2])

        def wait_region(eng, kt, upto):
            for b in reversed(beats[:upto + 1]):
                if any(a == kt for a, _ in b["kts"]):
                    wait_beat(eng, b["b"])
                    return

        writers = {}
        for s in steps:
            if s["kind"] == "trh":
                for q in range(4):
                    writers.setdefault(s["kt"] + q, []).append((s["in_beat"], "step", s["k"], s["j"]))
        for b in beats:
            if b["last"]:
                if b["name"] == "CB":
                    b["act_kt"] = 0 + b["j"]
                elif b["name"] == "B" and b["i"] == 2:
                    b["act_kt"] = (4 if b["c"] == 0 else 8) + b["j"]
                elif b["name"] == "UB":
                    b["act_kt"] = b["act"] + b["j"] - (2 if b.get("packed") else 0)
                else:
                    continue
                writers.setdefault(b["act_kt"], []).append((b["b"], "beat", b["b"], b["j"]))
        waited = {}

        def wait_activations(pe, b):
            if b["b"] == 0:
                pe.wait_ge(ready_dve, DVE_X)
            for kind in ("step", "beat"):
                found = [w[2] for a, _ in b["kts"] for w in writers.get(a, []) if w[0] < b["b"] and w[1] == kind and
                         (kind == "beat" or b["form"] == "B" or w[3] == b["j"])]
                if found and max(found) > waited.get(kind, -1):
                    waited[kind] = max(found)
                    if kind == "step":
                        wait_taken(pe, max(found))
                    else:
                        wait_evac(pe, max(found))

        DVE_TAB, DVE_SC, DVE_COL = 1, 2, 3
        DVE_X = 3 + 2 * NT

        with nc.Block() as block:

            @block.sync
            def _(sp):
                n = 0

                which = consts_in

                def load(dst, s):
                    nonlocal n
                    n += 16
                    sp.dma_start(dst, s).then_inc(which, 16)

                load(cst[:], t_in["cst"])
                load(posi[:, 0:4], t_in["positions"].rearrange("a (t p) -> p (a t)", p=P))
                load(CI["c"], t_in["c"].rearrange("a (k p) -> p (a k)", p=P))
                load(CI["b_ada"], t_in["b_ada"].rearrange("a (k p) -> p (a k)", p=P))
                load(CI["g_pre"], t_in["g_pre"].rearrange("a (k p) -> p (a k)", p=P))
                for g in range(2):
                    load(posi[32 * g:32 * g + NCMP, 4:5],
                         t_in["positions"][0, 31:512].rearrange("(n s) -> n s", s=1)[0:481:16])
                sp.dma_start(x0, t_in["x"].rearrange("a (t p) d -> p (a t) d", p=P)).then_inc(x_in, 16)
                ada = t_in["w_ada"].rearrange("a (k p) n -> p (a k) n", p=P)
                for i in range(4):
                    sp.dma_start(ada_w[:, i], ada[:, :, 512 * i:512 * i + 512]).then_inc(ada_in[i], 16)
                assert n == 16 * N_CONST
                which = params_in
                load(gp[:], t_in["b_ada"][:, 2 * D:3 * D].broadcast_to([P, D]))
                for v, kv in enumerate("kv"):
                    load(w2s[:, v], t_in["cmp_w2_" + kv].rearrange("a (m p) n -> p (a m) n", p=P))
                    for l in range(2):
                        load(cpe[DH * l:DH * l + DH, v],
                             t_in["cmp_pe_" + kv].rearrange("a (m l) d -> l d (a m)", l=2)[l])
                for name, key in (("g_mem", "g_mem_2"), ("g_mix", "g_mix_2"), ("g_ffn", "g_ffn_2"),
                                  ("b_gate", "b_gate_2"), ("conv_b", "conv_b_2")):
                    load(CI[name], t_in[key].rearrange("(k p) -> p k", p=P))
                load(CI["conv_w"], t_in["conv_w_2"].rearrange("w (k p) -> p (w k)", p=P))
                load(ffw[:, 0:3], t_in["ffn_conv_w_2"].rearrange("w (k p) -> p w k", p=P))
                load(ffw[:, 3], t_in["ffn_conv_b_2"].rearrange("(k p) -> p k", p=P))
                for l in range(2):
                    load(CI["gq"][DH * l:DH * l + DH], t_in["moba_q_gain_2"].rearrange("(d s) -> d s", s=1))
                    load(CI["gk"][DH * l:DH * l + DH], t_in["moba_k_gain_2"].rearrange("(d s) -> d s", s=1))
                load(CI["gmq"], t_in["memq_gain_2"].rearrange("(d s) -> d s", s=1))
                load(CI["gmk"], t_in["memk_gain_2"].rearrange("(d s) -> d s", s=1))
                assert n == 16 * (N_CONST + N_PARAM)
                sp.wait_ge(ready_pe, 2)
                for i in (0, 1):
                    sp.dma_start(ada_w[:, i], ada[:, :, 512 * (4 + i):512 * (5 + i)]).then_inc(ada_in[i], 16)
                for s in range(2):
                    sp.dma_start(raw[:, s], t_in["weights"][s]).then_inc(raw_in[s], 16)
                wst = t_in["weights"]
                with sp.Fori(1, NU // 2) as i:
                    for s in range(2):
                        sp.wait_ge(lo_ready, i * 2 - 1 + s)
                        sp.dma_start(raw[:, s], wst[bass.ds(i * 2 + s, 1)].rearrange("a p n -> p (a n)")).then_inc(
                            raw_in[s], 16)
                if NU % 2:
                    sp.wait_ge(lo_ready, NU - 2)
                    sp.dma_start(raw[:, 0], wst[NU - 1]).then_inc(raw_in[0], 16)
                for j in range(NT):
                    b = [b for b in beats if b["name"] == "DN" and b["final"] and b["c"] == 1 and b["j"] == j][0]
                    wait_evac(sp, b["b"])
                    sp.dma_start(out.rearrange("a (t p) d -> p (a t) d", p=P)[:, j], x2[:, j]).then_inc(out_saved, 16)
                sp.wait_ge(out_saved, 16 * NT)

            @block.gpsimd
            def _(pool):
                def low(s, n):
                    pool.wait_ge(hi_ready, n)
                    nc.gpsimd.tensor_tensor(w_lo[:, s].rearrange("p k n -> p (k n)"), raw[:, s],
                                            w_hi[:, s].rearrange("p k n -> p (k n)").bitcast(F32),
                                            ALU.subtract).then_inc(lo_ready, 1)
                with pool.Fori(0, NU // 2) as i:
                    for s in range(2):
                        low(s, i * 2 + 1 + s)
                if NU % 2:
                    low(0, NU)

            @block.tensor
            def _(pe):
                pe.wait_ge(ready_act, 1)
                for i in range(4):
                    pe.wait_ge(ada_in[i], 16)
                    for m in range(4):
                        for k in range(KT):
                            mm = pe.matmul(po[:, 4 * i + m:4 * i + m + 1], ada_w[:, i, k, P * m:P * m + P],
                                           CI["sc"][:, k:k + 1], start=k == 0, stop=k == KT - 1)
                    mm.then_inc(ready_pe, 1)
                for j in range(NT):
                    for half in range(2):
                        n = 2 * j + half
                        pe.wait_ge(ready_dve, DVE_COL)
                        if n >= 2:
                            pe.wait_ge(ready_dve, DVE_COL + n - 1)
                        for q in range(4):
                            mm = pe.transpose(sc[n % 2][:, P * q:P * q + P],
                                              x0[:, j, 512 * half + P * q:512 * half + P * q + P], ident)
                        mm.then_inc(ready_pe, 1)
                for c in range(2):
                    pe.wait_ge(ada_in[c], 32)
                    for k in range(KT):
                        mm = pe.matmul(pj[c][:], scb[:, k], ada_w[:, c, k], start=k == 0, stop=k == KT - 1)
                    mm.then_inc(ready_pe, 1)

                def projection(b):
                    if b["unit_first"]:
                        pe.wait_ge(lo_ready, b["u"] + 1)
                    if b["first"]:
                        if b["bank_prev"] is not None:
                            wait_evac(pe, b["bank_prev"])
                        elif b["bank"] < 2:
                            pe.wait_ge(ready_dve, DVE_X + 1)
                    wait_activations(pe, b)
                    s = b["u"] % 2
                    n = b["n"]
                    dst = pj[b["bank"]][:, 0:n] if b["form"] == "A" else pj[b["bank"]][:]
                    last = len(b["kts"]) - 1
                    for i, (a, q) in enumerate(b["kts"]):
                        if b["form"] == "A":
                            st = (a_hi[:, a, P * b["j"]:P * b["j"] + P], a_lo[:, a, P * b["j"]:P * b["j"] + P])
                            mv = (w_hi[:, s, q, 0:n], w_lo[:, s, q, 0:n])
                        else:
                            st = (w_hi[:, s, q, P * b["j"]:P * b["j"] + P], w_lo[:, s, q, P * b["j"]:P * b["j"] + P])
                            mv = (a_hi[:, a], a_lo[:, a])
                        for z, (x, y) in enumerate(((0, 0), (0, 1), (1, 0))):
                            mm = pe.matmul(dst, st[x], mv[y], start=b["first"] and i == 0 and z == 0,
                                           stop=b["last"] and i == last and z == 2)
                    mm.then_inc(beat_done, 1)

                bank_user = {}

                def wait_score_bank(k):
                    p = bank_user.get(k % 2)
                    if p is not None:
                        if has(steps[p], "probs"):
                            pe.wait_ge(probs_ready, count["probs"][p])
                        else:
                            pe.wait_ge(rows_ready, count["rows"][p])
                    else:
                        pe.wait_ge(ready_dve, DVE_X)
                    bank_user[k % 2] = k

                def heads(s, h):
                    if s["fam"] == "mem":
                        return (slice(0, P), qmT[:, h], kmT[:, h], vm[:, :, MDH * h:MDH * h + MDH])
                    p = slice(DH * (h % 2), DH * (h % 2) + DH)
                    if s["fam"] == "moba":
                        return p, qT[:, h // 2], kT[:, h // 2], vmo[:, :, DH * h:DH * h + DH]
                    g = h // 4
                    v = (vsel, vwin)[s["br"]]
                    return p, nqT[:, h // 2], ncT[:, 2 * s["br"] + g], v[:, :, DH * g:DH * g + DH]

                def ready_inputs(k):
                    s = steps[k]
                    to = {"nsa": "nq", "mem": "QM", "moba": "QM"}.get(s.get("fam")) or {"cmp": "nq", "ret": "rk"}[
                        s["kind"]]
                    wait_taken(pe, max(p for p in range(k) if steps[p].get("to") == to))
                    names = {"sm": {"nsa": "NQ", "moba": "V", "mem": "MV"}.get(s.get("fam")), "ret": "RV",
                             "cmp": "NQ"}.get(s["kind"])
                    bb = [b for b in beats if b["name"] == names and b["last"]][-1]
                    wait_evac(pe, bb["b"])

                def scores(k):
                    s = steps[k]
                    if not has(s, "scores"):
                        return
                    wait_score_bank(k)
                    dst = sc[k % 2]
                    if s["kind"] == "hid":
                        pe.wait_ge(rows_ready, count["rows"][pl.cmv])
                        pe.wait_ge(w1_in, 32)
                        for v in range(2):
                            for m in range(2):
                                o = (2 * v + m) * 64
                                for q in range(16):
                                    mm = pe.matmul(dst[:, o:o + 64], w1[:, v, q, P * m:P * m + P],
                                                   cmv[:, v, q].rearrange("p g n -> p (g n)"),
                                                   start=q == 0, stop=q == 15)
                    elif s["kind"] == "cmp":
                        ready_inputs(k)
                        for c in range(H // 2):
                            mm = pe.matmul(dst[:, 64 * c:64 * c + 64], nqT[:, c, P * s["j"]:P * s["j"] + P],
                                           kcT[:, c // 2].rearrange("p e n -> p (e n)"), start=True, stop=True)
                    elif s["kind"] == "ret":
                        ready_inputs(k)
                        p = slice(DH * s["half"], DH * s["half"] + DH)
                        q = slice(P * s["j"], P * s["j"] + P)
                        for c in range(4):
                            mm = pe.matmul(dst[:, P * c:P * c + P], rkT[p, c, q], rqT[p, c, q], start=True,
                                           stop=True)
                    else:
                        ready_inputs(k)
                        for h, t, o in s["segs"]:
                            p, q, kk, _ = heads(s, h)
                            n = MEM if s["fam"] == "mem" else P * (t + 1)
                            mm = pe.matmul(dst[:, o:o + n], q[p, P * t:P * t + P], kk[p, 0:n], start=True,
                                           stop=s["fam"] == "mem")
                            if s["fam"] != "mem":
                                mm = pe.matmul(dst[:, o + n - P:o + n], idb[:], maskb[:], start=False, stop=True)
                    mm.then_inc(scores_ready, 1)

                def turn(k):
                    s = steps[k]
                    if not has(s, "turn"):
                        return
                    for p in range(k - 1, -1, -1):
                        if has(steps[p], "turn"):
                            wait_taken(pe, p)
                            break
                    kind = s["kind"]
                    if kind == "tr":
                        if steps[k - 1]["kind"] == "qn":
                            wait_taken(pe, k - 1)
                        wait_evac(pe, s["beat"])
                        t = rk[:, s["j"]] if s["to"] == "rk" else src[:, s["slot"]]
                        for q in range(s["nb"]):
                            mm = pe.transpose(pt[:, P * q:P * q + P], t[:, P * q:P * q + P], ident)
                    elif kind == "trh":
                        t = {"att": lambda: att[:, s["j"]], "ret": lambda: rk[:, s["j"]],
                             "mem": lambda: memr[:, s["j"], 512 * s["half"]:],
                             "x": lambda: xn[:, 512 * s["half"]:], "x2": lambda: xn[:, 512 * s["half"]:],
                             "ymem": lambda: src[:, s["slot"]], "ymoba": lambda: ymo[:, s["j"]]}[s["src"]]()
                        if s["src"] in ("att", "ret"):
                            wait_evac(pe, s["beat"])
                        elif s["src"] in ("mem", "x", "x2"):
                            p = max(p for p in range(k) if steps[p]["kind"] in ("mnorm", "j2"))
                            wait_taken(pe, p)
                        else:
                            p = max(p for p in range(k) if steps[p]["kind"] == "sm")
                            pe.wait_ge(out_taken, count["out"][p])
                        for q in range(4):
                            mm = pe.transpose(pt[:, P * q:P * q + P], t[:, P * q:P * q + P], ident)
                    elif kind == "hid":
                        pe.wait_ge(probs_ready, count["probs"][k])
                        hk = probT[:, k % 2].rearrange("p (m n) -> p m n", m=8)
                        hv = prob[:, k % 2].rearrange("p (m g n) -> p m g n", m=2, g=2)
                        for m in range(2):
                            pe.matmul(pt[0:64, 0:DH], hk[:, m], w2s[:, 0, m], start=m == 0, stop=m == 1)
                        for g in range(2):
                            for m in range(2):
                                mm = pe.matmul(pt[:, 64 + DH * g:64 + DH * g + DH], hv[:, m, g], w2s[:, 1, m],
                                               start=m == 0, stop=m == 1)
                    elif kind == "kct":
                        wait_taken(pe, k - 1)
                        mm = pe.transpose(pt[:, 0:64], kcr[0:64, :], ident[0:64, 0:64])
                    elif kind == "cmp":
                        pe.wait_ge(probs_ready, count["probs"][k])
                        for g in range(2):
                            mm = pe.transpose(pt[:, P * g:P * g + P], prob[:, k % 2, P * g:P * g + P], ident)
                    elif kind == "ret":
                        e = DH * s["half"]
                        for c in range(4):
                            z = slice(P * c + e, P * c + e + DH)
                            mm = pe.matmul(pt[e:e + DH, DH * c:DH * c + DH], rk[:, s["j"], z], rv[:, s["j"], z],
                                           start=True, stop=True)
                    else:
                        pe.wait_ge(probs_ready, count["probs"][k])
                        b = 0
                        for h, t, o in s["segs"]:
                            for jb in range(2 if s["fam"] == "mem" else t + 1):
                                mm = pe.transpose(pt[:, P * b:P * b + P],
                                                  prob[:, k % 2, o + P * jb:o + P * jb + P], ident)
                                b += 1
                    mm.then_inc(turned, 1)

                def values(k):
                    s = steps[k]
                    if not has(s, "values"):
                        return
                    for p in range(k - 1, -1, -1):
                        if has(steps[p], "out"):
                            pe.wait_ge(out_taken, count["out"][p])
                            break
                    else:
                        pe.wait_ge(ready_dve, DVE_COL)
                    if s["kind"] == "ret":
                        pe.wait_ge(rows_ready, count["rows"][k])
                        if s["j"]:
                            wait_taken(pe, max(p for p in range(k) if steps[p]["kind"] == "ret" and
                                               steps[p]["half"] == s["half"]))
                        e = DH * s["half"]
                        for c in range(4):
                            d = po[:, DH * c:DH * c + DH]
                            if s["j"]:
                                pe.matmul(d, rqT[e:e + DH, c, P * s["j"]:P * s["j"] + P],
                                          Rst[e:e + DH, s["j"] % 2, c], start=True, stop=False)
                            mm = pe.matmul(d, prob[:, k % 2, P * c:P * c + P],
                                           rv[:, s["j"], P * c + e:P * c + e + DH], start=s["j"] == 0, stop=True)
                    elif s["kind"] == "cmp":
                        wait_taken(pe, k)
                        for g in range(2):
                            mm = pe.matmul(po[:, 256 * g:256 * g + 256], probT[:, k % 2, P * g:P * g + P],
                                           vbd[:, g].rearrange("p r n -> p (r n)"), start=True, stop=True)
                    else:
                        wait_taken(pe, k)
                        b = 0
                        for i, (h, t, o) in enumerate(s["segs"]):
                            w = MDH if s["fam"] == "mem" else DH
                            v = heads(s, h)[3]
                            nb = 2 if s["fam"] == "mem" else t + 1
                            for jb in range(nb):
                                mm = pe.matmul(po[:, w * i:w * i + w], probT[:, k % 2, P * b:P * b + P], v[:, jb],
                                               start=jb == 0, stop=jb == nb - 1)
                                b += 1
                    mm.then_inc(values_ready, 1)

                for b in beats:
                    projection(b)
                    for k in b["steps"]:
                        scores(k)
                        if k >= 2:
                            values(k - 2)
                        if k >= 1:
                            turn(k - 1)

            @block.scalar
            def _(act):
                marks = {}

                def link(ins):
                    marks["c"] = marks.get("c", 0) + 1
                    ins.then_inc(chain_act, 1)
                    act.wait_ge(chain_act, marks["c"])

                def done(ins, s, key):
                    marks[key] = marks.get(key, 0) + 1
                    ins.then_inc(s, 1)
                    act.wait_ge(s, marks[key])

                A = nc.scalar.activation

                def high(u):
                    act.wait_ge(raw_in[u % 2], 16 * (u // 2 + 1))
                    if u >= 2:
                        wait_beat(act, pl.unit_end[u - 2])
                    done(A(w_hi[:, u % 2].rearrange("p k n -> p (k n)"), raw[:, u % 2], ACT.Copy), hi_ready, "hi")

                act.wait_ge(consts_in, 16 * N_CONST)
                done(A(CI["sc"], CI["c"], ACT.Silu), ready_act, "r")
                act.wait_ge(ready_dve, DVE_TAB)
                link(A(rope_s[:], rope_s[:], ACT.Sin))
                done(A(rope_c[:], rope_c[:], ACT.Sin), ready_act, "r")
                act.wait_ge(x_in, 16)
                for j in range(NT):
                    link(A(a_lo[:, 8:10].rearrange("p k n -> p (k n)"), x0[:, j], ACT.Square, accum_out=ss[:, j:j + 1]))
                done(A(sd, ss, ACT.Sqrt, bias=CI["eps"], scale=1.0 / D), ready_act, "r")
                high(0)
                high(1)
                act.wait_ge(ready_pe, 4)
                act.dma_start(gpost, t_in["g_post"].broadcast_to([P, D])).then_inc(gpost_in, 16)

                def probs(k):
                    s = steps[k]
                    if not has(s, "probs"):
                        return
                    kind = s["kind"]
                    if kind == "sm":
                        act.wait_ge(rows_ready, count["rows"][k])
                        wait_probs_slot(act, k)
                        for i, (h, t, o) in enumerate(s["segs"]):
                            n = MEM if s["fam"] == "mem" else P * (t + 1)
                            ins = A(prob[:, k % 2, o:o + n], sc[k % 2][:, o:o + n], ACT.Exp,
                                    bias=nmax[:, k % 4, i:i + 1], accum_out=rsum[:, k % 4, i:i + 1])
                            if i < len(s["segs"]) - 1:
                                link(ins)
                        done(ins, probs_ready, "p")
                    elif kind == "cmp":
                        act.wait_ge(rows_ready, count["rows"][k])
                        done(A(prob[:, k % 2, 0:256], prob[:, k % 2, 0:256], ACT.Exp), probs_ready, "p")
                    elif kind == "hid":
                        act.wait_ge(scores_ready, count["scores"][k])
                        link(A(probT[:, k % 2, 0:128], sc[k % 2][:, 0:128], ACT.Silu))
                        hv = prob[:, k % 2].rearrange("p (m g r n) -> p m g r n", m=2, g=2, r=4)
                        sv = sc[k % 2][:, 128:256].rearrange("p (m g n) -> p m g n", m=2, g=2)
                        link(A(hv[:, 0], sv[:, 0].unsqueeze(2).broadcast_to([P, 2, 4, 32]), ACT.Silu))
                        done(A(hv[:, 1], sv[:, 1].unsqueeze(2).broadcast_to([P, 2, 4, 32]), ACT.Silu),
                             probs_ready, "p")
                    elif kind == "gates":
                        wait_evac(act, max(b["b"] for b in beats if b["name"] == "N2"))
                        done(A(glog[:], glog[:], ACT.Tanh, scale=0.5), probs_ready, "p")
                    elif kind == "gn":
                        act.wait_ge(rows_ready, count["rows"][k])
                        done(A(gvar[:, s["j"]], gvar[:, s["j"]], ACT.Sqrt, bias=CI["epsg"], scale=1.0 / DH),
                             probs_ready, "p")
                    elif kind in ("mnorm", "j1", "j2"):
                        if kind == "mnorm":
                            act.wait_ge(mem_in, 16)
                            t = memr[:, s["j"]]
                        elif kind == "j1":
                            wait_evac(act, s["beat"])
                            t = yo[:, s["j"]]
                        elif s["which"] == 0:
                            wait_taken(act, k - 1)
                            t = x1[:, s["j"]]
                        else:
                            wait_evac(act, s["beat"])
                            t = x2[:, s["j"]]
                        p = [q for q in range(k) if has(steps[q], "turn")][-1]
                        act.wait_ge(turned, count["turn"][p])
                        link(A(xn, t, ACT.Square, accum_out=ss[:, 0:1]))
                        done(A(sd[:, 0:1], ss[:, 0:1], ACT.Sqrt, bias=CI["eps"], scale=1.0 / D), probs_ready, "p")
                    elif kind == "qn":
                        wait_evac(act, s["beat"])
                        n, w = s["nh"], S // s["nh"]
                        done(A(qsd[:, s["slot"], 0:n], qss[:, s["slot"], 0:n], ACT.Sqrt, bias=CI["eps"],
                               scale=1.0 / w), probs_ready, "p")

                def take(k):
                    s = steps[k]
                    if s["kind"] != "sm":
                        return
                    act.wait_ge(turned, count["turn"][k])
                    done(A(probT[:, k % 2], pt[:], ACT.Copy), taken_act, "t")

                gathered = False
                last_nsa = max(s["k"] for s in steps if s.get("fam") == "nsa")
                for b in beats:
                    if b["unit_first"] and b["u"] >= 1 and b["u"] + 1 < NU:
                        high(b["u"] + 1)
                    name = b["name"]
                    if name == "N2" and b["first"] and b["j"] == 0:
                        act.wait_ge(ready_dve, DVE_X + 1)
                        for v, kv in enumerate("kv"):
                            act.dma_start(w1[:, v], t_in["cmp_w1_" + kv].rearrange("a (m p) n -> p (a m) n", p=P)
                                          ).then_inc(w1_in, 16)
                    if b["last"]:
                        j = b["j"]
                        if name in ("NG", "RG"):
                            wait_beat(act, b["b"])
                            if name == "NG":
                                act.wait_ge(values_ready, count["values"][last_nsa])
                            else:
                                wait_evac(act, b["b"] - 8)
                            done(A(sg[:, j], pj[b["bank"]][:], ACT.Tanh, scale=0.5), pair_act, "pair")
                        elif name == "CC":
                            wait_beat(act, b["b"])
                            act.wait_ge(x1_saved, 16)
                            done(A(ucv[:, j], pj[b["bank"]][:], ACT.Copy), evac_act, "e")
                        elif name == "G":
                            wait_beat(act, b["b"])
                            prev = [q for q in beats[:b["b"]] if q["name"] in ("CB", "B") and q["last"]
                                    and q["j"] == j][-1]
                            wait_evac(act, prev["b"])
                            done(A(tg[:, j], pj[b["bank"]][:], ACT.Tanh,
                                   bias=CI["b_gate"][:, 8 * b["gi"] + 4 * b["c"] + j:][:, 0:1], scale=0.5),
                                 evac_act, "e")
                        elif name == "UA":
                            wait_evac(act, b["b"])
                            prev = [q for q in beats[:b["b"]] if q["name"] == "UB" and q["last"]]
                            if prev:
                                wait_evac(act, prev[-1]["b"])
                            done(A(fsi[:, j], fcv[:, j], ACT.Silu), pair_act, "pair")
                    for k in b["steps"]:
                        probs(k)
                        if k >= 1:
                            take(k - 1)
                        s = steps[k - 1] if k else None
                        if s and s["kind"] == "tr" and s["to"] == "n1" and s["j"] == NT - 1:
                            wait_taken(act, k - 1)
                            for l in range(2):
                                for g in range(2):
                                    act.dma_start(cblk[DH * l:DH * l + DH, :, g, 0:S - l],
                                                  kvT[DH * g:DH * g + DH, :, l:S]).then_inc(gather_in, 16)
                    if name == "RG" and b["last"] and b["j"] == 3:
                        last_ret = max(s["k"] for s in steps if s["kind"] == "ret")
                        act.wait_ge(out_taken, count["out"][last_ret])
                        act.dma_start(memr, t_in["mem_2"].rearrange("a (t p) d -> p (a t) d", p=P)).then_inc(mem_in, 16)
                    if name == "WO" and b["last"] and b["c"] == 0 and b["j"] == 0:
                        wait_evac(act, max(q["b"] for q in beats if q["name"] == "RG"))
                        act.dma_start(x1, t_in["x"].rearrange("a (t p) d -> p (a t) d", p=P)).then_inc(xres_in, 16)
                    if name == "MV" and b["last"] and b["j"] == 1:
                        p = max(s["k"] for s in steps if s["kind"] == "j1")
                        wait_taken(act, p)
                        act.dma_start(x1_dram.rearrange("(t p) d -> p t d", p=P), x1).then_inc(x1_saved, 16)
                    if name == "B" and b["i"] == 1 and b["c"] == 0 and b["j"] == 3:
                        p = max(s["k"] for s in steps if s["kind"] == "sm")
                        act.wait_ge(out_taken, count["out"][p])
                        act.dma_start(x2, x1_dram.rearrange("(t p) d -> p t d", p=P)).then_inc(x1_back, 16)

            @block.vector
            def _(dve):
                V = nc.vector
                marks = {}

                def link(ins):
                    marks["c"] = marks.get("c", 0) + 1
                    ins.then_inc(chain_dve, 1)
                    dve.wait_ge(chain_dve, marks["c"])

                def done(ins, s, key):
                    marks[key] = marks.get(key, 0) + 1
                    ins.then_inc(s, 1)
                    dve.wait_ge(s, marks[key])

                def split(kt, q, value, s, key):
                    link(V.tensor_copy(a_hi[:, kt, q], value))
                    done(V.tensor_tensor(a_lo[:, kt, q], value, a_hi[:, kt, q].bitcast(F32), ALU.subtract), s, key)

                link(V.memset(CI["eps"], EPS))
                link(V.memset(CI["epsg"], 1e-5))
                dve.wait_ge(consts_in, 16 * N_CONST)
                ang = tmp[:, 0, 0:5 * NF].rearrange("p (t f) -> p t f", t=5)
                rnd = tmp[:, 0, 200:400].rearrange("p (t f) -> p t f", t=5)
                posf = small[:, 120:125]
                link(V.memset(posf, 0.0))
                link(V.tensor_copy(posf[:, 0:4], posi[:, 0:4]))
                for g in range(2):
                    link(V.tensor_copy(posf[32 * g:32 * g + NCMP, 4:5], posi[32 * g:32 * g + NCMP, 4:5]))
                inv = cst[:, C_INV:C_INV + NF]
                link(V.tensor_tensor(ang, posf.unsqueeze(2).broadcast_to([P, 5, NF]),
                                     inv.unsqueeze(1).broadcast_to([P, 5, NF]), ALU.mult))
                link(V.tensor_scalar(rnd, ang, 1.0 / (2 * np.pi), ROUND, ALU.mult, ALU.add))
                link(V.tensor_scalar(rnd, rnd, ROUND, None, ALU.subtract))
                for part in (TWO_PI_A, TWO_PI_B, TWO_PI_C):
                    link(V.scalar_tensor_tensor(ang, rnd, -part, ang, ALU.mult, ALU.add))
                link(V.tensor_scalar(rope_s[:], ang, 3.1415925, -3.1415925, ALU.min, ALU.max))
                link(V.scalar_tensor_tensor(rnd, rope_s[:], -1.0, rope_s[:], ALU.mult, ALU.max))
                done(V.tensor_scalar(rope_c[:], rnd, -1.0, np.pi / 2, ALU.mult, ALU.add), ready_dve, "r")
                dve.wait_ge(ready_act, 1)
                link(V.tensor_copy(scb, CI["sc"].unsqueeze(2).broadcast_to([P, KT, P])))
                link(V.tensor_copy(idb[:], ident))
                link(V.tensor_tensor(pt[:, 0:P], tri, ident, ALU.subtract))
                done(V.tensor_scalar(maskb[:], pt[:, 0:P], NEG, None, ALU.mult), ready_dve, "r")
                dve.wait_ge(ready_pe, 4)
                link(V.tensor_tensor(CI["cb"], po[:, 0:8], CI["b_ada"][:, 0:8], ALU.add))
                link(V.tensor_tensor(CI["ca"], po[:, 8:16], CI["b_ada"][:, 8:16], ALU.add))
                link(V.scalar_tensor_tensor(CI["ca"], CI["ca"], 1.0, CI["g_pre"], ALU.add, ALU.mult))
                dve.wait_ge(ready_act, 3)
                link(V.reciprocal(rr, sd))
                link(V.tensor_scalar(x0[:, 0], x0[:, 0], rr[:, 0:1], None, ALU.mult))
                link(V.tensor_scalar(x0[:, 1], x0[:, 1], rr[:, 1:2], None, ALU.mult))
                link(V.tensor_scalar(x0[:, 2], x0[:, 2], rr[:, 2:3], None, ALU.mult))
                done(V.tensor_scalar(x0[:, 3], x0[:, 3], rr[:, 3:4], None, ALU.mult), ready_dve, "r")
                for j in range(NT):
                    for half in range(2):
                        n = 2 * j + half
                        dve.wait_ge(ready_pe, 5 + n)
                        for q in range(4):
                            kt = 4 * half + q
                            link(V.tensor_scalar(stage[:, q], sc[n % 2][:, P * q:P * q + P], CI["ca"][:, kt:kt + 1],
                                                 CI["cb"][:, kt:kt + 1], ALU.mult, ALU.add))
                        split(slice(4 * half, 4 * half + 4), slice(P * j, P * j + P), stage, ready_dve, "r")
                dve.wait_ge(params_in, 16 * N_PARAM)
                dve.wait_ge(gpost_in, 16)
                for c in range(2):
                    half = gp[:, 512 * c:512 * c + 512]
                    dve.wait_ge(ready_pe, 13 + c)
                    link(V.tensor_tensor(half, half, pj[c][:], ALU.add))
                    link(V.tensor_tensor(half, half, gpost[:, 512 * c:512 * c + 512], ALU.mult))
                link(V.tensor_scalar(CI["b_gate"], CI["b_gate"], 0.5, None, ALU.mult))
                link(V.memset(kcT.rearrange("p g e n -> p (g e n)"), 0.0))
                done(V.memset(vbd.rearrange("p g r n -> p (g r n)"), 0.0), ready_dve, "r")

                def rotate(dst, s, nh, w, half, c, sn, scale_first=None):
                    a = s[:, :, 0:2 * half].rearrange("p h (t f) -> p h t f", t=2)
                    n = nh * 2 * half
                    np_ = s.shape[0]
                    bc = c.unsqueeze(1).unsqueeze(1).broadcast_to([np_, nh, 2, half])
                    bs = sn.unsqueeze(1).unsqueeze(1).broadcast_to([np_, nh, 2, half])
                    tc_ = tmp[0:np_, 0, 0:n].rearrange("p (h t f) -> p h t f", h=nh, t=2)
                    ts_ = tmp[0:np_, 1, 0:n].rearrange("p (h t f) -> p h t f", h=nh, t=2)
                    link(V.tensor_tensor(tc_, a, bc, ALU.mult))
                    link(V.tensor_tensor(ts_, a, bs, ALU.mult))
                    link(V.tensor_tensor(dst[:, :, 0:half], tc_[:, :, 0], ts_[:, :, 1], ALU.subtract))
                    return V.tensor_tensor(dst[:, :, half:2 * half], ts_[:, :, 0], tc_[:, :, 1], ALU.add)

                def h3(ap, w):
                    return ap.rearrange("p (h d) -> p h d", d=w)

                def src_slot(b):
                    s = pl.src_of_beat[b["b"]]
                    if s["slot_prev"] is not None:
                        dve.wait_ge(turned, count["turn"][s["slot_prev"]])
                    return src[:, s["slot"]], s["slot"]

                def evacuate(b):
                    if not b["last"] or b["evac"] != "dve":
                        return
                    wait_beat(dve, b["b"])
                    name, j, bank = b["name"], b["j"], pj[b["bank"]]
                    cr, sr = rope_c[:, j, 0:NF_RET], rope_s[:, j, 0:NF_RET]
                    cn, sn = rope_c[:, j, NF_RET:NF], rope_s[:, j, NF_RET:NF]

                    def e(ins):
                        done(ins, evac_dve, "e")

                    if name == "N1":
                        t, _ = src_slot(b)
                        link(V.tensor_copy(t[:, 0:256], bank[:, 0:256]))
                        d4 = t[:, 256:512].rearrange("p (g r d) -> p g r d", g=2, r=2)
                        link(V.tensor_copy(d4[:, :, 0], h3(bank[:, 256:384], DH)))
                        link(rotate(d4[:, :, 0], h3(bank[:, 256:384], DH), 2, DH, 8, cn, sn))
                        link(V.tensor_copy(d4[:, :, 1], d4[:, :, 0]))
                        e(V.tensor_copy(vsel[:, j], bank[:, 384:512]))
                    elif name == "N2":
                        t, _ = src_slot(b)
                        d4 = t[:, 0:256].rearrange("p (g r d) -> p g r d", g=2, r=2)
                        link(V.tensor_copy(d4[:, :, 0], h3(bank[:, 0:128], DH)))
                        link(rotate(d4[:, :, 0], h3(bank[:, 0:128], DH), 2, DH, 8, cn, sn))
                        link(V.tensor_copy(d4[:, :, 1], d4[:, :, 0]))
                        link(V.tensor_copy(vwin[:, j], bank[:, 128:256]))
                        e(V.tensor_copy(glog[:, j], bank[:, 256:280]))
                    elif name == "NQ":
                        t, _ = src_slot(b)
                        link(V.tensor_copy(t, bank[:]))
                        link(rotate(h3(t, DH), h3(bank[:], DH), H, DH, 8, cn, sn))
                        e(V.tensor_scalar(t, t, DH ** -0.5, None, ALU.mult))
                    elif name == "RQ":
                        t, _ = src_slot(b)
                        link(rotate(h3(t, DH), h3(bank[:], DH), H, DH, 32, cr, sr))
                        e(V.tensor_scalar(t, t, DH ** -0.5, None, ALU.mult))
                    elif name == "RK":
                        e(rotate(h3(rk[:, j], DH), h3(bank[:], DH), H, DH, 32, cr, sr))
                    elif name == "RV":
                        e(V.tensor_tensor(h3(rv[:, j], DH), h3(bank[:], DH),
                                          cst[:, C_VSC:C_VSC + H].unsqueeze(2).broadcast_to([P, H, DH]), ALU.mult))
                    elif name == "NG":
                        dve.wait_ge(pair_act, pair_n[b["b"]])
                        link(V.scalar_tensor_tensor(tmp[:, 0], sg[:, j], 1.0, bank[:], ALU.add, ALU.mult))
                        e(V.scalar_tensor_tensor(att[:, j], tmp[:, 0], 0.25, att[:, j], ALU.mult, ALU.mult))
                    elif name == "RG":
                        dve.wait_ge(pair_act, pair_n[b["b"]])
                        p = [s["k"] for s in steps if s["kind"] == "gn" and s["j"] == j][0]
                        dve.wait_ge(probs_ready, count["probs"][p])
                        link(V.reciprocal(rs8, gvar[:, j]))
                        link(V.tensor_tensor(h3(rk[:, j], DH), h3(rk[:, j], DH),
                                             rs8.unsqueeze(2).broadcast_to([P, H, DH]), ALU.mult))
                        link(V.scalar_tensor_tensor(tmp[:, 0], sg[:, j], 1.0, bank[:], ALU.add, ALU.mult))
                        e(V.scalar_tensor_tensor(rk[:, j], tmp[:, 0], 0.5, rk[:, j], ALU.mult, ALU.mult))
                    elif name == "WO":
                        e(V.tensor_copy(yo[:, j, 512 * b["c"]:512 * b["c"] + 512], bank[:]))
                    elif name == "MV":
                        e(V.tensor_copy(vm[:, j], bank[:]))
                    elif name == "V":
                        e(V.tensor_copy(vmo[:, j], bank[:]))
                    elif name in ("MK", "Q", "K", "QM"):
                        t, slot = src_slot(b)
                        nh = MH if name in ("MK", "QM") else H
                        link(V.tensor_copy(t, bank[:]))
                        link(V.tensor_tensor(tmp[:, 0], t, t, ALU.mult))
                        e(V.reduce_sum(qss[:, slot, 0:nh], h3(tmp[:, 0], S // nh), axis=AX_X))
                    elif name == "CX":
                        wait_evac(dve, b["b"] - 8)
                        e(V.tensor_tensor(ucv[:, j], ucv[:, j], bank[:], ALU.mult))
                    elif name == "CB":
                        w = [CI["conv_w"][:, 4 * i + j:4 * i + j + 1] for i in range(3)]
                        t = tmp[:, 0]
                        link(V.tensor_scalar(t, ucv[:, j], w[2], CI["conv_b"][:, j:j + 1], ALU.mult, ALU.add))
                        link(V.scalar_tensor_tensor(t[:, 1:], ucv[:, j, 0:S - 1], w[1], t[:, 1:], ALU.mult, ALU.add))
                        link(V.scalar_tensor_tensor(t[:, 2:], ucv[:, j, 0:S - 2], w[0], t[:, 2:], ALU.mult, ALU.add))
                        link(V.tensor_tensor(tmp[:, 1], t, bank[:], ALU.mult))
                        wait_region(dve, b["act_kt"], b["b"])
                        split(b["act_kt"], slice(0, S), tmp[:, 1], evac_dve, "e")
                    elif name == "B":
                        m = merged[:, 4 * b["c"] + j]
                        wait_evac(dve, b["b"] - 4)
                        if b["i"] == 0:
                            e(V.scalar_tensor_tensor(m, tg[:, j], 1.0, bank[:], ALU.add, ALU.mult))
                        else:
                            link(V.scalar_tensor_tensor(tmp[:, 0], tg[:, j], 1.0, bank[:], ALU.add, ALU.mult))
                            if b["i"] == 1:
                                e(V.tensor_tensor(m, m, tmp[:, 0], ALU.add))
                            else:
                                link(V.tensor_tensor(m, m, tmp[:, 0], ALU.add))
                                link(V.tensor_scalar(tmp[:, 1], m, 0.5, None, ALU.mult))
                                wait_region(dve, b["act_kt"], b["b"])
                                split(b["act_kt"], slice(0, S), tmp[:, 1], evac_dve, "e")
                    elif name == "WY":
                        if b["c"] == 0 and j == 0:
                            dve.wait_ge(x1_back, 16)
                        t = x2[:, j, 512 * b["c"]:512 * b["c"] + 512]
                        e(V.tensor_tensor(t, t, bank[:], ALU.add))
                    elif name == "UA":
                        ct = b["ch"] + j
                        w = [ffw[:, i, ct:ct + 1] for i in range(4)]
                        t = fcv[:, j]
                        prev = [q for q in beats[:b["b"]] if q["name"] == "UA" and q["last"] and q["j"] == j]
                        if prev:
                            dve.wait_ge(pair_act, pair_n[prev[-1]["b"]])
                        link(V.tensor_scalar(t, bank[:], w[2], w[3], ALU.mult, ALU.add))
                        link(V.scalar_tensor_tensor(t[:, 1:], bank[:, 0:S - 1], w[1], t[:, 1:], ALU.mult, ALU.add))
                        e(V.scalar_tensor_tensor(t[:, 2:], bank[:, 0:S - 2], w[0], t[:, 2:], ALU.mult, ALU.add))
                    elif name == "UB":
                        jj = b["act_kt"] - b["act"]
                        ua = [q for q in beats[:b["b"]] if q["name"] == "UA" and q["last"] and q["j"] == jj][-1]
                        dve.wait_ge(pair_act, pair_n[ua["b"]])
                        link(V.tensor_tensor(tmp[:, 1], fsi[:, jj], bank[:], ALU.mult))
                        wait_region(dve, b["act_kt"], b["b"])
                        split(b["act_kt"], slice(0, S), tmp[:, 1], evac_dve, "e")
                    elif name == "DN":
                        t = x2[:, j, 512 * b["c"]:512 * b["c"] + 512]
                        e(V.tensor_tensor(t, t, bank[:], ALU.add))

                def rows(k):
                    s = steps[k]
                    if not has(s, "rows"):
                        return
                    kind = s["kind"]
                    if kind == "sm":
                        dve.wait_ge(scores_ready, count["scores"][k])
                        for i, (h, t, o) in enumerate(s["segs"]):
                            n = MEM if s["fam"] == "mem" else P * (t + 1)
                            ins = V.tensor_reduce(nmax[:, k % 4, i:i + 1], sc[k % 2][:, o:o + n], AX_X, ALU.max,
                                                  negate=True)
                            if i < len(s["segs"]) - 1:
                                link(ins)
                        done(ins, rows_ready, "s")
                    elif kind == "cmp":
                        dve.wait_ge(scores_ready, count["scores"][k])
                        wait_probs_slot(dve, k)
                        pr = prob[:, k % 2, 0:256].rearrange("p (h n) -> p h n", h=H)
                        link(V.tensor_tensor(pr, sc[k % 2][:, 0:256].rearrange("p (h n) -> p h n", h=H),
                                             cmpb[:, s["j"]].unsqueeze(1).broadcast_to([P, H, 32]), ALU.add))
                        link(V.reduce_max(st8, pr, axis=AX_X))
                        done(V.tensor_tensor(pr, pr, st8.unsqueeze(2).broadcast_to([P, H, 32]), ALU.subtract),
                             rows_ready, "s")
                    elif kind == "ret":
                        dve.wait_ge(scores_ready, count["scores"][k])
                        wait_probs_slot(dve, k)
                        done(V.tensor_tensor(prob[:, k % 2].rearrange("p (h n) -> p h n", h=4),
                                             sc[k % 2][:].rearrange("p (h n) -> p h n", h=4),
                                             tri.unsqueeze(1).broadcast_to([P, 4, P]), ALU.mult), rows_ready, "s")
                    elif kind == "cmv":
                        dve.wait_ge(gather_in, 64)
                        link(V.memset(cmv.rearrange("p v m g n -> p (v m g) n")[:, :, NCMP:32], 0.0))
                        for v in range(2):
                            for g in range(2):
                                for a in range(2):
                                    blk = cblk[:, v, g].rearrange("p (n m l) -> p m n l", m=8, l=2)
                                    ins = V.tensor_tensor(
                                        cmv[:, v, 8 * a:8 * a + 8, g, 0:NCMP], blk[:, :, a:a + NCMP, 0],
                                        cpe[:, v, 8 * a:8 * a + 8].unsqueeze(2).broadcast_to([P, 8, NCMP]), ALU.add)
                                    if (v, g, a) != (1, 1, 1):
                                        link(ins)
                        done(ins, rows_ready, "s")
                    elif kind == "gn":
                        t = h3(rk[:, s["j"]], DH)
                        link(V.reduce_sum(st8, t, axis=AX_X))
                        link(V.tensor_scalar(st8, st8, 1.0 / DH, None, ALU.mult))
                        link(V.tensor_tensor(t, t, st8.unsqueeze(2).broadcast_to([P, H, DH]), ALU.subtract))
                        link(V.tensor_tensor(h3(tmp[:, 0], DH), t, t, ALU.mult))
                        done(V.reduce_sum(gvar[:, s["j"]], h3(tmp[:, 0], DH), axis=AX_X), rows_ready, "s")

                def outputs(k):
                    s = steps[k]
                    if not has(s, "out"):
                        return
                    dve.wait_ge(values_ready, count["values"][k])
                    kind = s["kind"]
                    if kind == "cmp":
                        j = s["j"]
                        link(V.reciprocal(cf8, rs8))
                        gl = glog[:, j].rearrange("p (h c) -> p h c", c=3)[:, :, 0]
                        link(V.scalar_tensor_tensor(cf8, gl, 1.0, cf8, ALU.add, ALU.mult))
                        link(V.tensor_scalar(cf8, cf8, cst[:, C_ROW + j:C_ROW + j + 1], None, ALU.mult))
                        done(V.tensor_tensor(h3(att[:, j], DH), h3(po[:], DH),
                                             cf8.unsqueeze(2).broadcast_to([P, H, DH]), ALU.mult), out_taken, "o")
                    elif kind == "ret":
                        e = s["half"]
                        done(V.tensor_tensor(rk[:, s["j"]].rearrange("p (c e d) -> p c e d", c=4, e=2)[:, :, e],
                                             h3(po[:, 0:256], DH),
                                             cst[:, C_XI + 4 * e:C_XI + 4 * e + 4].unsqueeze(2)
                                             .broadcast_to([P, 4, DH]), ALU.mult), out_taken, "o")
                    else:
                        n = len(s["segs"])
                        link(V.reciprocal(ri[:, 0:n], rsum[:, k % 4, 0:n]))
                        for i, (h, t, o) in enumerate(s["segs"]):
                            if s["fam"] == "nsa":
                                g = 3 * h + 1 + s["br"]
                                link(V.scalar_tensor_tensor(cf[:, i:i + 1], glog[:, t, g:g + 1], 1.0, ri[:, i:i + 1],
                                                            ALU.add, ALU.mult))
                                d = att[:, t, DH * h:DH * h + DH]
                                ins = V.scalar_tensor_tensor(d, po[:, DH * i:DH * i + DH], cf[:, i:i + 1], d,
                                                             ALU.mult, ALU.add)
                            elif s["fam"] == "moba":
                                if i == 0:
                                    dve.wait_ge(x1_saved, 16)
                                ins = V.tensor_scalar(ymo[:, t, DH * h:DH * h + DH], po[:, DH * i:DH * i + DH],
                                                      ri[:, i:i + 1], None, ALU.mult)
                            else:
                                m = pl.src_mem[t]
                                if m["slot_prev"] is not None:
                                    dve.wait_ge(turned, count["turn"][m["slot_prev"]])
                                ins = V.tensor_scalar(src[:, m["slot"], MDH * h:MDH * h + MDH],
                                                      po[:, MDH * i:MDH * i + MDH], ri[:, i:i + 1], None, ALU.mult)
                            if i < n - 1:
                                link(ins)
                        done(ins, out_taken, "o")

                def take(k):
                    s = steps[k]
                    if not has(s, "take") or s["kind"] == "sm":
                        return
                    kind = s["kind"]

                    def f(ins):
                        done(ins, taken_dve, "t")

                    if has(s, "turn"):
                        dve.wait_ge(turned, count["turn"][k])
                    elif has(s, "probs"):
                        dve.wait_ge(probs_ready, count["probs"][k])
                    q = slice(P * s.get("j", 0), P * s.get("j", 0) + P)
                    p4 = pt[:].rearrange("p (b n) -> p b n", b=4)
                    if kind == "tr":
                        to = s["to"]
                        if to == "n1":
                            link(V.tensor_copy(kvT[:, :, q], p4[:, 0:2]))
                            f(V.tensor_copy(ncT[:, 0:2, q], p4[:, 2:4]))
                        elif to == "n2":
                            f(V.tensor_copy(ncT[:, 2:4, q], p4[:, 0:2]))
                        elif to in ("nq", "rq", "rk"):
                            f(V.tensor_copy({"nq": nqT, "rq": rqT, "rk": rkT}[to][:, :, q], p4))
                        elif to == "mk":
                            f(V.tensor_scalar(kmT[:, :, q], p4, CI["gmk"], None, ALU.mult))
                        elif to == "Q":
                            f(V.tensor_scalar(qT[:, :, q], p4, CI["gq"], DH ** -0.5, ALU.mult, ALU.mult))
                        elif to == "K":
                            f(V.tensor_scalar(kT[:, :, q], p4, CI["gk"], None, ALU.mult))
                        else:
                            f(V.tensor_scalar(qmT[:, :, q], p4, CI["gmq"], MDH ** -0.5, ALU.mult, ALU.mult))
                    elif kind == "trh":
                        kt = slice(s["kt"], s["kt"] + 4)
                        wait_region(dve, s["kt"], s["in_beat"])
                        stg = tmp[:, 0].rearrange("p (b n) -> p b n", b=4)
                        if s.get("scale"):
                            g = CI[s["scale"]][:, 4 * s["half"]:4 * s["half"] + 4]
                            link(V.tensor_tensor(stg, p4, g.unsqueeze(2).broadcast_to([P, 4, P]), ALU.mult))
                        else:
                            link(V.tensor_copy(stg, p4))
                        split(kt, q, stg, taken_dve, "t")
                    elif kind == "hid":
                        k3 = kcr[0:64, 0:DH].unsqueeze(1)
                        link(V.tensor_copy(kcr[0:64, 0:DH], pt[0:64, 0:DH]))
                        link(rotate(k3, pt[0:64, 0:DH].unsqueeze(1), 1, DH, 8, rope_c[0:64, 4, NF_RET:NF],
                                    rope_s[0:64, 4, NF_RET:NF]))
                        link(V.tensor_copy(kcr[0:64, DH:2 * DH], kcr[0:64, 0:DH]))
                        for r in range(4):
                            z = slice(32 * r, 32 * r + 32)
                            ins = V.tensor_copy(vbd[z, :, r], pt[z, 64:192].rearrange("p (g n) -> p g n", g=2))
                            if r < 3:
                                link(ins)
                        f(ins)
                    elif kind == "kct":
                        for e in range(2):
                            z = slice(DH * e, DH * e + DH)
                            ins = V.tensor_copy(kcT[z, :, e], pt[z, 0:64].rearrange("p (g n) -> p g n", g=2))
                            if e == 0:
                                link(ins)
                        f(ins)
                    elif kind == "cmp":
                        link(V.reduce_sum(rs8, prob[:, k % 2, 0:256].rearrange("p (h n) -> p h n", h=H), axis=AX_X))
                        f(V.tensor_copy(probT[:, k % 2, 0:256], pt[:, 0:256]))
                    elif kind == "ret":
                        e = slice(DH * s["half"], DH * s["half"] + DH)
                        d, new = Rst[e, (s["j"] + 1) % 2], h3(pt[e, 0:256], DH)
                        decay = cst[e, C_DEC:C_DEC + 4].unsqueeze(2).broadcast_to([DH, 4, DH])
                        if s["j"] == 0:
                            f(V.tensor_tensor(d, new, decay, ALU.mult))
                        else:
                            link(V.tensor_tensor(d, Rst[e, s["j"] % 2], new, ALU.add))
                            f(V.tensor_tensor(d, d, decay, ALU.mult))
                    elif kind == "mnorm":
                        link(V.reciprocal(rr[:, 0:1], sd[:, 0:1]))
                        f(V.tensor_scalar(memr[:, s["j"]], memr[:, s["j"]], rr[:, 0:1], None, ALU.mult))
                    elif kind == "j1":
                        if s["j"] == 0:
                            dve.wait_ge(xres_in, 16)
                        link(V.reciprocal(rr[:, 0:1], sd[:, 0:1]))
                        y = yo[:, s["j"]]
                        link(V.scalar_tensor_tensor(y, y, rr[:, 0:1], gp[:], ALU.mult, ALU.mult))
                        f(V.tensor_tensor(x1[:, s["j"]], x1[:, s["j"]], y, ALU.add))
                    elif kind == "j2":
                        link(V.reciprocal(rr[:, 0:1], sd[:, 0:1]))
                        f(V.tensor_scalar(xn, (x1, x2)[s["which"]][:, s["j"]], rr[:, 0:1], None, ALU.mult))
                    elif kind == "qn":
                        n = s["nh"]
                        t = h3(src[:, s["slot"]], S // n)
                        link(V.reciprocal(qri[:, 0:n], qsd[:, s["slot"], 0:n]))
                        f(V.tensor_tensor(t, t, qri[:, 0:n].unsqueeze(2).broadcast_to([P, n, S // n]), ALU.mult))

                for b in beats:
                    evacuate(b)
                    for k in b["steps"]:
                        rows(k)
                        if k >= 2:
                            outputs(k - 2)
                        if k >= 1:
                            take(k - 1)


def pack(unit, w):
    name, r, c, n = unit
    u = np.zeros((P, 4, 512), np.float32)
    if name == "w_up2":
        for i, c0 in enumerate((c, DFF + c)):
            u[:, :, n * i:n * i + n] = w["w_up"][r:r + 512, c0:c0 + n].reshape(4, P, n).transpose(1, 0, 2)
    elif name == "w_down2":
        u[:] = w["w_down"][r:r + 2 * P].reshape(2, P, 2, 512).transpose(1, 0, 2, 3).reshape(P, 4, 512)
    else:
        u[:, :, 0:n] = w[name][r:r + 512, c:c + n].reshape(4, P, n).transpose(1, 0, 2)
    return u.reshape(P, 2048)


_INS = ["x", "c", "positions", "w_ada", "b_ada", "g_pre", "g_post", "cmp_pe_k", "cmp_w1_k", "cmp_w2_k", "cmp_pe_v",
        "cmp_w1_v", "cmp_w2_v", "mem_2", "b_gate_2", "conv_w_2", "conv_b_2", "moba_q_gain_2", "moba_k_gain_2",
        "g_mem_2", "g_mix_2", "memq_gain_2", "memk_gain_2", "g_ffn_2", "ffn_conv_w_2", "ffn_conv_b_2"]


def kernel(**inputs):
    import concourse.bacc as _bacc
    from concourse.bass_utils import run_bass_kernel_spmd as _run

    a = {k: np.asarray(v) for k, v in inputs.items()}
    w = {"w_in": a["w_in"][0], "w_out": a["w_out"][0], "w_mem": a["w_mem_kv_2"], "w_in_2": a["w_in_2"],
         "w_br_conv": a["w_br_conv_2"], "w_br_mem": a["w_br_mem_2"], "w_br_moba": a["w_br_moba_2"],
         "w_o": a["w_o_2"], "w_up": a["w_up_2"], "w_down": a["w_down_2"]}
    arrays = {k: np.ascontiguousarray(a[k]) for k in _INS}
    arrays["weights"] = np.stack([pack(u, w) for u in make_plan().units])
    arrays["cst"] = constants()

    nc = _bacc.Bacc("TRN2", target_bir_lowering=False, num_devices=1)
    t_in = {}
    named = {}
    for name, v in arrays.items():
        named[f"in_{name}"] = v
        t_in[name] = nc.dram_tensor(f"in_{name}", v.shape, mybir.dt.from_np(v.dtype), kind="ExternalInput").ap()
    out = nc.dram_tensor("out", (1, S, D), F32, kind="ExternalOutput").ap()
    with nc.allow_non_contiguous_dma(reason="small per-channel columns"):
        build(nc, t_in, out)
    r = _run(nc, [named], core_ids=[0])
    return r.results[0]["out"]
```

```python
from contextlib import ExitStack

import numpy as np

import concourse.bass as bass
from concourse import mybir

ALU = mybir.AluOpType
ACT = mybir.ActivationFunctionType
F32 = mybir.dt.float32
F32R = mybir.dt.float32r
BF16 = mybir.dt.bfloat16
I32 = mybir.dt.int32
AX_X = mybir.AxisListType.X

P = 128
S = 512
D = 1024
NT = S // P
H = 8
DH = 64
MEM = 256
MH, MDH = 4, 128
KT = D // P
NCMP = 31
DFF = 2816
EPS = 1e-6
NEG = -1e30
TWO_PI_A = 6.28125
TWO_PI_B = float(np.float32(np.float16(2 * np.pi - TWO_PI_A)))
TWO_PI_C = float(2 * np.pi - TWO_PI_A - TWO_PI_B)
ROUND = 12582912.0
NF_RET, NF_NSA = 32, 8
NF = NF_RET + NF_NSA

C_INV, C_VSC, C_XI, C_TRI = 0, NF, NF + 8, NF + 16
C_ID = C_TRI + P
C_DEC = C_ID + P
C_CMPB = C_DEC + 4
C_ROW = C_CMPB + NT * 32
CST = C_ROW + NT
N_CONST, N_PARAM = 5, 3

COLS = (("c", 8), ("b_ada", 24), ("g_pre", 8), ("b_gate", 24), ("conv_w", 12), ("conv_b", 4), ("gq", 1), ("gk", 1),
        ("gmq", 1), ("gmk", 1), ("ffw", 88), ("cpe", 32), ("sc", 8), ("ca", 8), ("cb", 8), ("eps", 1), ("epsg", 1))
N_COLS = sum(n for _, n in COLS[:12])


def columns(a):
    tile = lambda v: v.reshape(-1, P).T
    pair = lambda v: np.tile(v, 2)[:, None]
    parts = [tile(a["c"][0]), tile(a["b_ada"][0]), tile(a["g_pre"][0]), tile(a["b_gate_2"]),
             tile(a["conv_w_2"].reshape(-1)), tile(a["conv_b_2"]), pair(a["moba_q_gain_2"]),
             pair(a["moba_k_gain_2"]), a["memq_gain_2"][:, None], a["memk_gain_2"][:, None],
             tile(a["ffn_conv_w_2"].reshape(-1)), tile(a["ffn_conv_b_2"]), tile(a["cmp_pe_k"].reshape(-1)),
             tile(a["cmp_pe_v"].reshape(-1))]
    return np.ascontiguousarray(np.concatenate(parts, axis=1))


def constants():
    c = np.zeros((P, CST), np.float32)
    f = np.float32
    c[:, C_INV:C_INV + NF_RET] = np.power(f(10000.0), -np.arange(NF_RET, dtype=f) / f(NF_RET))
    c[:, C_INV + NF_RET:C_INV + NF] = np.power(f(500000.0), -np.arange(NF_NSA, dtype=f) / f(NF_NSA))
    log_g = np.log1p(-np.power(2.0, -5.0 - np.arange(H)))
    p = np.arange(P)
    c[:, C_VSC:C_VSC + H] = np.exp(-(p[:, None] + 1.0) * log_g)
    even_odd = [0, 2, 4, 6, 1, 3, 5, 7]
    c[:, C_XI:C_XI + H] = np.exp((p[:, None] + 1.0) * log_g[even_odd])
    c[:, C_TRI:C_TRI + P] = p[:, None] <= p[None, :]
    for h in range(H):
        c[(h % 2) * DH:(h % 2) * DH + DH, C_DEC + h // 2] = np.exp(P * log_g[h])
    c[:, C_ID:C_ID + P] = np.eye(P, dtype=f)
    for t in range(NT):
        for n in range(32):
            ok = (n < NCMP) & (16 * n + 31 <= t * P + p)
            c[:, C_CMPB + t * 32 + n] = np.where(ok, 0.0, NEG)
        c[:, C_ROW + t] = (t * P + p >= 31)
    return c


PANELS1 = [
    ("N1", 2560, 512), ("N2", 3072, 280), ("NQ", 2048, 512), ("RQ", 0, 512), ("RK", 512, 512),
    ("RV", 1024, 512), ("NG", 3352, 512), ("RG", 1536, 512)]
PANELS2 = [("Q", "A", 1536), ("K", "A", 2048), ("V", "A", 2560), ("QM", "A", 3072),
           ("CC", "B", 512), ("CX", "B", 1024), ("CB", "B", 0)]
GATE0 = 3584
FFN_GROUPS = [4, 4, 4, 4, 4, 2]


class Plan:

    def __init__(self):
        self.beats, self.steps, self.units, self.src = [], [], [], []

    def panel(self, name, form, cols, srcs, tiles=4, base=0, n=512, **more):
        first = len(self.beats)
        for i, s in enumerate(srcs):
            self.units.append(s)
            for j in range(tiles):
                self.beats.append(dict(name=name, form=form, u=len(self.units) - 1, j=j, n=n,
                                       first=i == 0, last=i == len(srcs) - 1,
                                       kts=[(base[i] + q, q) for q in range(4)], steps=[], mid=[],
                                       unit_first=j == 0, bank=j, **more))
        return first

    def step(self, start, mid=False, **s):
        s["k"] = len(self.steps)
        self.steps.append(s)
        self.beats[start]["mid" if mid else "steps"].append(s["k"])
        return s["k"]


def segments(family):
    for a in range(0, H, 4):
        for e in range(2):
            for h in (a + e, a + e + 2):
                yield [(h, 3, 0)]
                yield [(h, 0, 0), (h, 2, P)]
            yield [(a + e, 1, 0), (a + e + 2, 1, 2 * P)]


def make_plan():
    pl = Plan()
    step, beats = pl.step, pl.beats
    b0 = {}
    for name, c0, n in PANELS1:
        b0[name] = pl.panel(name, "A", c0, [("w_in", 512 * i, c0, n) for i in range(2)], base=[0, 4], n=n)
    for j in range(NT):
        step(b0["N1"] + 4 + j, kind="tr", to="n1", j=j, nb=4, beat=b0["N1"] + 4 + j)
    step(b0["N2"], kind="nop")
    for j in range(NT):
        step(b0["N2"] + 4 + j, kind="tr", to="n2", j=j, nb=2, beat=b0["N2"] + 4 + j)
    step(b0["NQ"], kind="nop")
    pl.cmv = step(b0["NQ"] + 1, kind="cmv")
    step(b0["NQ"] + 2, kind="hid")
    step(b0["NQ"] + 3, kind="kct")
    for j in range(NT):
        step(b0["NQ"] + 4 + j, kind="tr", to="nq", j=j, nb=4, beat=b0["NQ"] + 4 + j)
    step(b0["RQ"], kind="gates")
    todo = [dict(kind="cmp", j=t) for t in range(NT)]
    for br in range(2):
        todo += [dict(kind="sm", fam="nsa", br=br, segs=s) for s in segments("nsa")]
    at = b0["RQ"] + 1
    while at < b0["NG"] + 3:
        b = beats[at]
        if todo:
            step(at, mid=True, **todo.pop(0))
        if not b["last"] and todo:
            step(at, **todo.pop(0))
        if b["name"] in ("RQ", "RK") and b["last"]:
            step(at, kind="tr", to=b["name"].lower(), j=b["j"], nb=4, beat=at)
        at += 1
    while todo:
        step(b0["NG"] + 3, **todo.pop(0))
    step(b0["NG"] + 3, kind="nop")
    step(b0["NG"] + 3, kind="nop")
    ret = [dict(kind="ret", j=n, half=h) for n in range(NT) for h in range(2)]
    at = b0["NG"] + 4
    for n in range(NT):
        for h in range(2):
            step(at, kind="ret", j=n, half=h)
            if beats[at]["name"] == "NG":
                step(at, kind="trh", src="att", j=at - b0["NG"] - 4, kt=12, beat=at)
            at += 1
        if n:
            step(at - 1, kind="gn", j=n - 1)
    step(at, kind="nop")
    step(at, kind="gn", j=3)
    for j in range(NT):
        step(b0["RG"] + 4 + j, kind="trh", src="ret", j=j, kt=8, beat=b0["RG"] + 4 + j)
    wo = [pl.panel("WO", "A", c, [("w_out", 512 * i, 512 * c, 512) for i in (1, 0)], base=[12, 8], c=c)
          for c in range(2)]
    step(wo[0], mid=True, kind="nop")
    step(wo[0] + 1, kind="mnorm", j=0)
    step(wo[0] + 2, kind="mnorm", j=1)
    for i in range(2):
        for half in range(2):
            step(wo[0] + 3 + i, mid=half == 0, kind="trh", src="mem", j=i, half=half, kt=4 * half)
    step(wo[0] + 5, kind="nop")
    mk = pl.panel("MK", "A", 0, [("w_mem", 512 * i, 0, 512) for i in range(2)], tiles=2, base=[0, 4])
    mv = pl.panel("MV", "A", 1, [("w_mem", 512 * i, 512, 512) for i in range(2)], tiles=2, base=[0, 4])
    w4 = wo[1] + 4

    def j1(j):
        return dict(kind="j1", j=j, beat=w4 + j)

    def j2(j):
        return dict(kind="j2", j=j, which=0)

    def th(j, half):
        return dict(kind="trh", src="x", j=j, half=half, kt=8 + 4 * half)

    for at, mid, s in ((w4, 0, j1(0)), (w4 + 1, 0, j1(1)), (w4 + 2, 1, j2(0)), (w4 + 2, 0, j1(2)),
                       (w4 + 3, 1, j2(1)), (w4 + 3, 0, j1(3)), (mk, 1, th(0, 0)), (mk, 0, th(0, 1)),
                       (mk + 1, 1, j2(2)), (mk + 1, 0, th(1, 0)), (mk + 2, 1, th(1, 1)), (mk + 2, 0, j2(3)),
                       (mk + 3, 1, th(2, 0)), (mk + 3, 0, th(2, 1)), (mv, 1, th(3, 0)), (mv, 0, th(3, 1))):
        step(at, mid=bool(mid), **s)
    for j in range(2):
        step(mv + 1 + j, mid=True, kind="qn", src="MK", j=j, nh=MH, beat=mk + 2 + j)
        step(mv + 1 + j, kind="tr", to="mk", j=j, nb=4, beat=mk + 2 + j)
    step(mv + 3, kind="nop")
    e0 = {}
    for name, form, c0 in PANELS2:
        e0[name] = pl.panel(name, form, c0, [("w_in_2", 512 * i, c0, 512) for i in range(2)], base=[8, 12])
    for name in ("Q", "K", "QM"):
        for j in range(NT):
            b = e0[name] + 4 + j
            step(b, kind="qn", src=name, j=j, nh=MH if name == "QM" else H, beat=b)
            step(b, kind="tr", to=name, j=j, nb=4, beat=b)
        step(b + 1, kind="nop")
    branches = [("conv", 0, 0), ("mem", 2, 4), ("moba", 1, 0)]
    g0 = {}
    for i, (name, gi, base) in enumerate(branches):
        for c in range(2):
            col = GATE0 + D * gi + 512 * c
            g0[name, c] = pl.panel("G", "B", col, [("w_in_2", 512 * q, col, 512) for q in range(2)],
                                   base=[8, 12], gi=gi, c=c)
            pl.panel("B", "B", c, [("w_br_" + name, 0, 512 * c, 512)], base=[base], i=i, c=c)
    todo = []
    for t in range(NT):
        todo += [dict(kind="sm", fam="mem", segs=[(2 * a, t, 0), (2 * a + 1, t, MEM)]) for a in range(2)]
        todo += [dict(kind="nop"), dict(kind="trh", src="ymem", j=t, kt=4)]
    todo += [dict(kind="sm", fam="moba", segs=s) for s in segments("moba")]
    todo += [dict(kind="nop")] * 2
    todo += [dict(kind="trh", src="ymoba", j=t, kt=0) for t in range(NT)] + [dict(kind="nop")]
    at = e0["CC"] + 1
    while len(todo) > 5:
        step(at, **todo.pop(0))
        if beats[at]["name"] == "CC" or todo[0]["kind"] == "nop":
            step(at, **todo.pop(0))
        at += 1
    assert at < g0["conv", 0] + 8
    at = g0["mem", 0]
    while todo:
        step(at, **todo.pop(0))
        at += 1
    w2 = [pl.panel("WY", "A", c, [("w_o", 512 * i, 512 * c, 512) for i in range(2)], base=[4, 8], c=c)
          for c in range(2)]
    w4 = w2[1] + 4
    for j in range(NT):
        step(w4 + j, kind="j2", j=j, which=1, beat=w4 + j)
        if j:
            for half in range(2):
                step(w4 + min(j + 1, 3), kind="trh", src="x2", j=j - 1, half=half, kt=12 if half == 0 else 0)
    for half in range(2):
        step(w4 + 3, kind="trh", src="x2", j=3, half=half, kt=12 if half == 0 else 0)
    step(w4 + 3, kind="nop")
    def up(g):
        act, ch, n = (4, 8)[g % 2], sum(FFN_GROUPS[:g]), FFN_GROUPS[g] * P
        if FFN_GROUPS[g] == 4:
            for name, c0 in (("UA", 0), ("UB", DFF)):
                pl.panel(name, "B", 0, [("w_up", 512 * i, c0 + ch * P, n) for i in range(2)], base=[12, 0], ch=ch,
                         act=act)
        else:
            f = pl.panel("UX", "B", 0, [("w_up2", 512 * i, ch * P, n) for i in range(2)], base=[12, 0], ch=ch,
                         act=act, packed=True)
            for b in beats[f:]:
                b["name"] = "UA" if b["j"] < 2 else "UB"

    def down(g):
        act, ch = (4, 8)[g % 2], sum(FFN_GROUPS[:g]) * P
        if FFN_GROUPS[g] == 4:
            for c in range(2):
                pl.panel("DN", "A", c, [("w_down", ch, 512 * c, 512)], base=[act], c=c, final=False)
        else:
            pl.units.append(("w_down2", ch, 0, 0))
            for c in range(2):
                for j in range(NT):
                    beats.append(dict(name="DN", form="A", u=len(pl.units) - 1, j=j, n=512, first=True, last=True,
                                      kts=[(act + q, 2 * q + c) for q in range(2)], steps=[], mid=[], bank=j,
                                      unit_first=c == 0 and j == 0, c=c, final=True))

    up(0)
    for g in range(1, len(FFN_GROUPS)):
        up(g)
        down(g - 1)
    down(len(FFN_GROUPS) - 1)
    for i, b in enumerate(beats):
        b["b"] = i
    return finish_plan(pl)


def has(s, phase):
    kind = s["kind"]
    return phase in {
        "nop": (), "tr": ("turn", "take"), "trh": ("turn", "take"), "cmv": ("rows",),
        "hid": ("scores", "probs", "turn", "take"), "kct": ("turn", "take"), "gates": ("probs",),
        "cmp": ("scores", "rows", "probs", "turn", "take", "values", "out"),
        "sm": ("scores", "rows", "probs", "turn", "take", "values", "out"),
        "ret": ("scores", "rows", "turn", "take", "values", "out") if s.get("j") != 3 else
        ("scores", "rows", "values", "out"),
        "gn": ("rows", "probs"), "mnorm": ("probs", "take"), "j1": ("probs", "take"), "j2": ("probs", "take"),
        "qn": ("rows", "probs", "take"),
    }[kind]


def finish_plan(pl):
    pl.count = {}
    for phase in ("scores", "rows", "probs", "turn", "values", "out"):
        n, at = 0, []
        for s in pl.steps:
            n += has(s, phase)
            at.append(n)
        pl.count[phase] = at
    for who in ("act", "dve"):
        n, at = 0, []
        for s in pl.steps:
            n += has(s, "take") and (s["kind"] == "sm") == (who == "act")
            at.append(n)
        pl.count["take_" + who] = at
    n, at = 0, []
    for s in pl.steps:
        n += s["kind"] == "trh"
        at.append(n)
    pl.count["high"] = at
    na = nd = 0
    for b in pl.beats:
        b["evac"] = None
        if b["last"]:
            b["evac"] = "act" if b["name"] in ("CC", "G", "WO", "MK", "MV", "Q", "K", "V", "QM") else "dve"
            if b["evac"] == "act":
                na += 1
                b["evac_n"] = na
            else:
                nd += 1
                b["evac_n"] = nd
    pl.unit_end = {}
    for b in pl.beats:
        pl.unit_end[b["u"]] = b["b"]
    last = {}
    for b in pl.beats:
        if b["first"]:
            b["bank_prev"] = last.get(b["bank"])
        if b["last"]:
            last[b["bank"]] = b["b"]
    for s in pl.steps:
        s["in_beat"] = next(b["b"] for b in pl.beats if s["k"] in b["steps"] + b["mid"])
        s["mid"] = s["k"] in pl.beats[s["in_beat"]]["mid"]
    n = 0
    prev = {}
    pl.src_of_beat = {}
    pl.src_mem = {}
    uses = [s for s in pl.steps if (s["kind"] == "tr" and s["to"] != "rk") or s["kind"] == "trh" and s["src"] == "ymem"]
    uses.sort(key=lambda s: s["k"])
    for s in uses:
        s["slot"] = n % 2
        s["slot_prev"] = prev.get(n % 2)
        prev[n % 2] = s["k"]
        if s["kind"] == "tr":
            pl.src_of_beat[s["beat"]] = s
        else:
            pl.src_mem[s["j"]] = s
        n += 1
    for i, s in enumerate(s for s in pl.steps if s["kind"] in ("mnorm", "j1", "j2")):
        s["norm"] = i
    for s in pl.steps:
        if s["kind"] == "qn":
            s["slot"] = pl.src_of_beat[s["beat"]]["slot"]
    return pl


def kib(arena, a, n):
    return arena[:, a * 256:(a + n) * 256]


def build(nc, t_in, out):
    pl = make_plan()
    beats, steps, units, count = pl.beats, pl.steps, pl.units, pl.count
    NU = len(units)
    with ExitStack() as ctx:
        def sb(name, shape, dt=F32):
            return ctx.enter_context(nc.sbuf_tensor(name, shape, dt))

        def ps(name):
            return ctx.enter_context(nc.psum_tensor(name, [P, 512], F32))

        def sem(name):
            return ctx.enter_context(nc.semaphore(name))

        raw = sb("raw", [P, 2, 2048])
        w_hi = sb("w_hi", [P, 2, 4, 512], F32R)
        w_lo = sb("w_lo", [P, 2, 4, 512], F32R)
        a_hi = sb("a_hi", [P, 16, S], F32R)
        a_lo = sb("a_lo", [P, 16, S], F32R)
        arena = sb("arena", [P, 84 * 256])
        cst = sb("cst", [P, CST])
        idb = sb("idb", [P, P], BF16)
        maskb = sb("maskb", [P, P], BF16)
        rope_c = sb("rope_c", [P, 5, NF])
        rope_s = sb("rope_s", [P, 5, NF])
        gp = sb("gp", [P, D])
        cols = sb("cols", [P, sum(n for _, n in COLS)])
        w2s = sb("w2s", [P, 2, 2, DH])
        small = sb("small", [P, 160])
        posi = sb("posi", [P, 5], I32)
        ident = cst[:, C_ID:C_ID + P]
        tri = cst[:, C_TRI:C_TRI + P]
        cmpb = cst[:, C_CMPB:C_CMPB + NT * 32].rearrange("p (t n) -> p t n", t=NT)

        def view(start, size, pat=None, **kw):
            v = kib(arena, start, size)
            return v.rearrange(pat, **kw) if pat else v

        ada_t = view(0, 32, "p (s m k) -> p s m k", s=4, m=2)
        ada_g = view(32, 32, "p (k n) -> p k n", k=KT)
        x0 = view(64, 16, "p (t d) -> p t d", t=NT)
        gpost = view(0, 4)
        stage = view(4, 4, "p (s b n) -> p s b n", s=2, b=4)
        crow = raw[:, 1, 0:D]
        scb = raw[:, 1, D:2 * D].rearrange("p (k m) -> p k m", k=KT)
        tmp = view(80, 4, "p (s n) -> p s n", s=2)
        ncT = view(0, 8, "p (b n) -> p b n", b=4)
        nqT = view(8, 8, "p (b n) -> p b n", b=4)
        w1 = view(16, 32, "p (v m n) -> p v m n", v=2, m=16)
        cblk = view(48, 8, "p (v g n) -> p v g n", v=2, g=2)
        cmv = view(56, 8, "p (v m g n) -> p v m g n", v=2, m=16, g=2)
        kvT = view(68, 4, "p (v n) -> p v n", v=2)
        rqT = view(16, 8, "p (b n) -> p b n", b=4)
        rkT = view(24, 8, "p (b n) -> p b n", b=4)
        rk = view(32, 8, "p (t n) -> p t n", t=NT)
        rv = view(40, 8, "p (t n) -> p t n", t=NT)
        att = view(48, 8, "p (t n) -> p t n", t=NT)
        prob = view(56, 4, "p (s n) -> p s n", s=2)
        probT = view(60, 4, "p (s n) -> p s n", s=2)
        src = view(64, 4, "p (s n) -> p s n", s=2)
        Rst = view(68, 2, "p (s c e) -> p s c e", s=2, c=4)
        vsel = view(72, 2, "p (t n) -> p t n", t=NT)
        vwin = view(74, 2, "p (t n) -> p t n", t=NT)
        vbd = view(76, 2, "p (g r n) -> p g r n", g=2, r=4)
        kcT = arena[:, 78 * 256:78 * 256 + 128].rearrange("p (g e n) -> p g e n", g=2, e=2)
        kcr = arena[:, 78 * 256 + 128:78 * 256 + 256]
        sg = view(0, 8, "p (t n) -> p t n", t=NT)
        yo = view(16, 16, "p (t d) -> p t d", t=NT)
        x1 = view(0, 16, "p (t d) -> p t d", t=NT)
        memr = view(40, 8, "p (t d) -> p t d", t=2)
        xn = view(56, 8, "p (s d) -> p s d", s=2)
        dump = view(68, 4)
        g_mem_row = view(76, 4)
        g_row = view(52, 4)
        kmT = view(72, 4, "p (h n) -> p h n", h=MH)
        vm = view(48, 4, "p (t n) -> p t n", t=2)
        qT = view(16, 8, "p (b n) -> p b n", b=4)
        kT = view(24, 8, "p (b n) -> p b n", b=4)
        vmo = view(32, 8, "p (t n) -> p t n", t=NT)
        qmT = view(40, 8, "p (b n) -> p b n", b=4)
        ymo = view(0, 8, "p (t n) -> p t n", t=NT)
        ucv = view(8, 8, "p (t n) -> p t n", t=NT)
        tg = view(8, 8, "p (t n) -> p t n", t=NT)
        merged = view(16, 16, "p (t n) -> p t n", t=8)
        x2 = view(32, 16, "p (t d) -> p t d", t=NT)
        fcv = view(8, 8, "p (t n) -> p t n", t=NT)
        fsi = view(0, 8, "p (t n) -> p t n", t=NT)

        x1_dram = nc.dram_tensor("x1_scratch", [S, D], F32).ap()

        CI = {}
        at = 0
        for name, n in COLS:
            CI[name] = cols[:, at:at + n]
            at += n
        cpe = CI["cpe"].rearrange("p (v m) -> p v m", v=2)
        ffw = CI["ffw"].rearrange("p (w k) -> p w k", w=4)
        glog = sb("glog", [P, NT, 24])
        nmax = sb("nmax", [P, 4, 2])
        rsum = sb("rsum", [P, 4, 2])
        st8 = small[:, 0:8]
        rs8 = small[:, 8:16]
        cf8 = small[:, 16:24]
        gvar = small[:, 24:56].rearrange("p (t n) -> p t n", t=NT)
        ri = small[:, 56:58]
        cf = small[:, 58:60]
        ss = small[:, 60:64]
        sd = small[:, 64:68]
        rr = small[:, 68:72]
        norm = small[:, 128:142]
        qss = small[:, 72:88].rearrange("p (s n) -> p s n", s=2)
        qsd = small[:, 88:104].rearrange("p (s n) -> p s n", s=2)
        qri = small[:, 104:112]

        pj = [ps(f"pj{i}") for i in range(4)]
        sc = [ps(f"sc{i}") for i in range(2)]
        pt = ps("pt")
        po = ps("po")

        consts_in = sem("consts_in")
        params_in = sem("params_in")
        gpost_in = sem("gpost_in")
        x_in = sem("x_in")
        ada_in = [sem(f"ada_in{i}") for i in range(4)]
        adag_in = sem("adag_in")
        ada_used = sem("ada_used")
        crow_in = sem("crow_in")
        grow_in = sem("grow_in")
        gmem_in = sem("gmem_in")
        high_taken = sem("high_taken")
        mem_in = sem("mem_in")
        xres_in = sem("xres_in")
        w1_in = sem("w1_in")
        gather_in = sem("gather_in")
        x1_saved = sem("x1_saved")
        x1_back = sem("x1_back")
        out_saved = sem("out_saved")
        raw_in = [sem(f"raw_in{i}") for i in range(2)]
        hi_ready = sem("hi_ready")
        lo_ready = sem("lo_ready")
        beat_done = sem("beat_done")
        scores_ready = sem("scores_ready")
        turned = sem("turned")
        values_ready = sem("values_ready")
        rows_ready = sem("rows_ready")
        probs_ready = sem("probs_ready")
        taken_act = sem("taken_act")
        taken_dve = sem("taken_dve")
        out_taken = sem("out_taken")
        evac_act = sem("evac_act")
        evac_dve = sem("evac_dve")
        ready_dve = sem("ready_dve")
        ready_act = sem("ready_act")
        ready_pe = sem("ready_pe")
        pair_act = sem("pair_act")
        chain_dve = sem("chain_dve")
        chain_act = sem("chain_act")

        pair_n = {}
        n = 0
        for b in beats:
            if b["last"] and b["name"] in ("NG", "RG", "UA"):
                n += 1
                pair_n[b["b"]] = n

        def wait_beat(eng, b):
            eng.wait_ge(beat_done, b + 1)

        def wait_evac(eng, b):
            if beats[b]["evac"] == "act":
                eng.wait_ge(evac_act, beats[b]["evac_n"])
            else:
                eng.wait_ge(evac_dve, beats[b]["evac_n"])

        def wait_taken(eng, k):
            if steps[k]["kind"] == "sm":
                eng.wait_ge(taken_act, count["take_act"][k])
            else:
                eng.wait_ge(taken_dve, count["take_dve"][k])

        def wait_probs_slot(eng, k):
            if k < 2:
                return
            s = steps[k - 2]
            if s["kind"] == "ret":
                eng.wait_ge(values_ready, count["values"][k - 2])
            elif s["kind"] in ("sm", "cmp", "hid"):
                eng.wait_ge(turned, count["turn"][k - 2])

        def wait_region(eng, kt, upto):
            for b in reversed(beats[:upto + 1]):
                if any(a == kt for a, _ in b["kts"]):
                    wait_beat(eng, b["b"])
                    return

        writers = {}
        for s in steps:
            if s["kind"] == "trh":
                for q in range(4):
                    writers.setdefault(s["kt"] + q, []).append((s["in_beat"], "step", s["k"], s["j"]))
        for b in beats:
            if b["last"]:
                if b["name"] == "CB":
                    b["act_kt"] = 0 + b["j"]
                elif b["name"] == "B" and b["i"] == 2:
                    b["act_kt"] = (4 if b["c"] == 0 else 8) + b["j"]
                elif b["name"] == "UB":
                    b["act_kt"] = b["act"] + b["j"] - (2 if b.get("packed") else 0)
                else:
                    continue
                writers.setdefault(b["act_kt"], []).append((b["b"], "beat", b["b"], b["j"]))
        waited = {}

        def wait_activations(pe, b):
            if b["b"] == 0:
                pe.wait_ge(h_taken, 2 * NT)
            for kind in ("step", "beat"):
                found = [w[2] for a, _ in b["kts"] for w in writers.get(a, []) if w[0] < b["b"] and w[1] == kind and
                         (kind == "beat" or b["form"] == "B" or w[3] == b["j"])]
                if found and max(found) > waited.get(kind, -1):
                    waited[kind] = max(found)
                    if kind == "step":
                        wait_taken(pe, max(found))
                    else:
                        wait_evac(pe, max(found))

        DVE_X0, DVE_SCB, DVE_TAB, DVE_X = 1, 2, 3, 4
        PE_GATE = 2 * NT + 2
        eps_ready = sem("eps_ready")
        h_taken = sem("h_taken")
        stage_ready = sem("stage_ready")
        stage_high = sem("stage_high")
        xbank = [sc[0], sc[1], pt, po, pj[2], pj[3]]

        with nc.Block() as block:

            @block.sync
            def _(sp):
                n = 0

                which = consts_in

                def load(dst, s):
                    nonlocal n
                    n += 16
                    sp.dma_start(dst, s).then_inc(which, 16)

                load(cst[:], t_in["cst"])
                load(posi[:, 0:4], t_in["positions"].rearrange("a (t p) -> p (a t)", p=P))
                load(cols[:, 0:N_COLS], t_in["cols"])
                for g in range(2):
                    load(posi[32 * g:32 * g + NCMP, 4:5],
                         t_in["positions"][0, 31:512].rearrange("(n s) -> n s", s=1)[0:481:16])
                sp.dma_start(crow, t_in["c"].broadcast_to([P, D])).then_inc(crow_in, 16)
                sp.dma_start(x0, t_in["x"].rearrange("a (t p) d -> p (a t) d", p=P)).then_inc(x_in, 16)
                ada = t_in["ada_t"].rearrange("(c m p) k -> p c m k", m=2, p=P)
                for i in range(8):
                    if i >= 4:
                        sp.wait_ge(ada_used, i - 3)
                    sp.dma_start(ada_t[:, i % 4], ada[:, i]).then_inc(ada_in[i % 4], 16)
                sp.dma_start(ada_g, t_in["ada_g"].rearrange("(k p) n -> p k n", p=P)).then_inc(adag_in, 16)
                sp.dma_start(raw[:, 0], t_in["weights"][0]).then_inc(raw_in[0], 16)
                assert n == 16 * N_CONST
                which = params_in
                load(gp[:], t_in["b_ada"][:, 2 * D:3 * D].broadcast_to([P, D]))
                for v, kv in enumerate("kv"):
                    load(w2s[:, v], t_in["cmp_w2_" + kv].rearrange("a (m p) n -> p (a m) n", p=P))
                assert n == 16 * (N_CONST + N_PARAM)
                sp.wait_ge(ready_pe, PE_GATE)
                sp.dma_start(raw[:, 1], t_in["weights"][1]).then_inc(raw_in[1], 16)
                wst = t_in["weights"]
                with sp.Fori(1, NU // 2) as i:
                    for s in range(2):
                        sp.wait_ge(lo_ready, i * 2 - 1 + s)
                        sp.dma_start(raw[:, s], wst[bass.ds(i * 2 + s, 1)].rearrange("a p n -> p (a n)")).then_inc(
                            raw_in[s], 16)
                if NU % 2:
                    sp.wait_ge(lo_ready, NU - 2)
                    sp.dma_start(raw[:, 0], wst[NU - 1]).then_inc(raw_in[0], 16)
                for j in range(NT):
                    b = [b for b in beats if b["name"] == "DN" and b["final"] and b["c"] == 1 and b["j"] == j][0]
                    wait_evac(sp, b["b"])
                    sp.dma_start(out.rearrange("a (t p) d -> p (a t) d", p=P)[:, j], x2[:, j]).then_inc(out_saved, 16)
                sp.wait_ge(out_saved, 16 * NT)

            @block.gpsimd
            def _(pool):
                def low(s, n):
                    pool.wait_ge(hi_ready, n)
                    nc.gpsimd.tensor_tensor(w_lo[:, s].rearrange("p k n -> p (k n)"), raw[:, s],
                                            w_hi[:, s].rearrange("p k n -> p (k n)").bitcast(F32),
                                            ALU.subtract).then_inc(lo_ready, 1)
                with pool.Fori(0, NU // 2) as i:
                    for s in range(2):
                        low(s, i * 2 + 1 + s)
                if NU % 2:
                    low(0, NU)

            @block.tensor
            def _(pe):
                pe.wait_ge(ready_dve, DVE_X0)
                for n in range(2 * NT):
                    j, half = divmod(n, 2)
                    if n >= 6:
                        pe.wait_ge(h_taken, n - 5)
                    for q in range(4):
                        mm = pe.transpose(xbank[n % 6][:, P * q:P * q + P],
                                          x0[:, j, 512 * half + P * q:512 * half + P * q + P], ident)
                    mm.then_inc(ready_pe, 1)
                pe.wait_ge(adag_in, 16)
                pe.wait_ge(ready_dve, DVE_SCB)
                for c in range(2):
                    for k in range(KT):
                        mm = pe.matmul(pj[c][:], scb[:, k], ada_g[:, k, 512 * c:512 * c + 512], start=k == 0,
                                       stop=k == KT - 1)
                    mm.then_inc(ready_pe, 1)

                def projection(b):
                    if b["unit_first"]:
                        pe.wait_ge(lo_ready, b["u"] + 1)
                    if b["first"]:
                        if b["bank_prev"] is not None:
                            wait_evac(pe, b["bank_prev"])
                        elif b["bank"] < 2:
                            pe.wait_ge(ready_dve, DVE_X)
                        else:
                            pe.wait_ge(h_taken, 2 * NT)
                    wait_activations(pe, b)
                    s = b["u"] % 2
                    n = b["n"]
                    dst = pj[b["bank"]][:, 0:n] if b["form"] == "A" else pj[b["bank"]][:]
                    last = len(b["kts"]) - 1
                    for i, (a, q) in enumerate(b["kts"]):
                        if i == (last + 1) // 2:
                            for k in b["mid"]:
                                step(k)
                        if b["form"] == "A":
                            st = (a_hi[:, a, P * b["j"]:P * b["j"] + P], a_lo[:, a, P * b["j"]:P * b["j"] + P])
                            mv = (w_hi[:, s, q, 0:n], w_lo[:, s, q, 0:n])
                        else:
                            st = (w_hi[:, s, q, P * b["j"]:P * b["j"] + P], w_lo[:, s, q, P * b["j"]:P * b["j"] + P])
                            mv = (a_hi[:, a], a_lo[:, a])
                        for z, (x, y) in enumerate(((0, 0), (0, 1), (1, 0))):
                            mm = pe.matmul(dst, st[x], mv[y], start=b["first"] and i == 0 and z == 0,
                                           stop=b["last"] and i == last and z == 2)
                    mm.then_inc(beat_done, 1)

                bank_user = {}

                def wait_score_bank(k):
                    p = bank_user.get(k % 2)
                    if p is not None:
                        if steps[p]["kind"] == "trh":
                            wait_taken(pe, p)
                        elif has(steps[p], "probs"):
                            pe.wait_ge(probs_ready, count["probs"][p])
                        else:
                            pe.wait_ge(rows_ready, count["rows"][p])
                    else:
                        pe.wait_ge(h_taken, 2 * NT)
                    bank_user[k % 2] = k

                def heads(s, h):
                    if s["fam"] == "mem":
                        return (slice(0, P), qmT[:, h], kmT[:, h], vm[:, :, MDH * h:MDH * h + MDH])
                    p = slice(DH * (h % 2), DH * (h % 2) + DH)
                    if s["fam"] == "moba":
                        return p, qT[:, h // 2], kT[:, h // 2], vmo[:, :, DH * h:DH * h + DH]
                    g = h // 4
                    v = (vsel, vwin)[s["br"]]
                    return p, nqT[:, h // 2], ncT[:, 2 * s["br"] + g], v[:, :, DH * g:DH * g + DH]

                def ready_inputs(k):
                    s = steps[k]
                    to = {"nsa": "nq", "mem": "QM", "moba": "QM"}.get(s.get("fam")) or {"cmp": "nq", "ret": "rk"}[
                        s["kind"]]
                    wait_taken(pe, max(p for p in range(k) if steps[p].get("to") == to))
                    names = {"sm": {"nsa": "NQ", "moba": "V", "mem": "MV"}.get(s.get("fam")), "ret": "RV",
                             "cmp": "NQ"}.get(s["kind"])
                    bb = [b for b in beats if b["name"] == names and b["last"]][-1]
                    wait_evac(pe, bb["b"])

                def scores(k):
                    s = steps[k]
                    if not has(s, "scores"):
                        return
                    wait_score_bank(k)
                    dst = sc[k % 2]
                    if s["kind"] == "hid":
                        pe.wait_ge(rows_ready, count["rows"][pl.cmv])
                        pe.wait_ge(w1_in, 32)
                        for v in range(2):
                            for m in range(2):
                                o = (2 * v + m) * 64
                                for q in range(16):
                                    mm = pe.matmul(dst[:, o:o + 64], w1[:, v, q, P * m:P * m + P],
                                                   cmv[:, v, q].rearrange("p g n -> p (g n)"),
                                                   start=q == 0, stop=q == 15)
                    elif s["kind"] == "cmp":
                        ready_inputs(k)
                        for c in range(H // 2):
                            mm = pe.matmul(dst[:, 64 * c:64 * c + 64], nqT[:, c, P * s["j"]:P * s["j"] + P],
                                           kcT[:, c // 2].rearrange("p e n -> p (e n)"), start=True, stop=True)
                    elif s["kind"] == "ret":
                        ready_inputs(k)
                        p = slice(DH * s["half"], DH * s["half"] + DH)
                        q = slice(P * s["j"], P * s["j"] + P)
                        for c in range(4):
                            mm = pe.matmul(dst[:, P * c:P * c + P], rkT[p, c, q], rqT[p, c, q], start=True,
                                           stop=True)
                    else:
                        ready_inputs(k)
                        for h, t, o in s["segs"]:
                            p, q, kk, _ = heads(s, h)
                            n = MEM if s["fam"] == "mem" else P * (t + 1)
                            mm = pe.matmul(dst[:, o:o + n], q[p, P * t:P * t + P], kk[p, 0:n], start=True,
                                           stop=s["fam"] == "mem")
                            if s["fam"] != "mem":
                                mm = pe.matmul(dst[:, o + n - P:o + n], idb[:], maskb[:], start=False, stop=True)
                    mm.then_inc(scores_ready, 1)

                def turn(k):
                    s = steps[k]
                    if not has(s, "turn"):
                        return
                    kind = s["kind"]
                    if kind == "trh":
                        wait_score_bank(k)
                    else:
                        for p in range(k - 1, -1, -1):
                            if has(steps[p], "turn") and steps[p]["kind"] != "trh":
                                wait_taken(pe, p)
                                break
                    if kind == "tr":
                        if steps[k - 1]["kind"] == "qn":
                            wait_taken(pe, k - 1)
                        wait_evac(pe, s["beat"])
                        t = rk[:, s["j"]] if s["to"] == "rk" else src[:, s["slot"]]
                        for q in range(s["nb"]):
                            mm = pe.transpose(pt[:, P * q:P * q + P], t[:, P * q:P * q + P], ident)
                    elif kind == "trh":
                        t = {"att": lambda: att[:, s["j"]], "ret": lambda: rk[:, s["j"]],
                             "mem": lambda: memr[:, s["j"], 512 * s["half"]:],
                             "x": lambda: xn[:, s["j"] % 2, 512 * s["half"]:],
                             "x2": lambda: xn[:, s["j"] % 2, 512 * s["half"]:],
                             "ymem": lambda: src[:, s["slot"]], "ymoba": lambda: ymo[:, s["j"]]}[s["src"]]()
                        if s["src"] in ("att", "ret"):
                            wait_evac(pe, s["beat"])
                        elif s["src"] in ("mem", "x", "x2"):
                            p = max(p for p in range(k) if steps[p]["kind"] in ("mnorm", "j2") and
                                    steps[p]["j"] == s["j"])
                            wait_taken(pe, p)
                        else:
                            p = max(p for p in range(k) if steps[p]["kind"] == "sm")
                            pe.wait_ge(out_taken, count["out"][p])
                        for q in range(4):
                            mm = pe.transpose(sc[k % 2][:, P * q:P * q + P], t[:, P * q:P * q + P], ident)
                    elif kind == "hid":
                        pe.wait_ge(probs_ready, count["probs"][k])
                        hk = probT[:, k % 2].rearrange("p (m n) -> p m n", m=8)
                        hv = prob[:, k % 2].rearrange("p (m g n) -> p m g n", m=2, g=2)
                        for m in range(2):
                            pe.matmul(pt[0:64, 0:DH], hk[:, m], w2s[:, 0, m], start=m == 0, stop=m == 1)
                        for g in range(2):
                            for m in range(2):
                                mm = pe.matmul(pt[:, 64 + DH * g:64 + DH * g + DH], hv[:, m, g], w2s[:, 1, m],
                                               start=m == 0, stop=m == 1)
                    elif kind == "kct":
                        wait_taken(pe, k - 1)
                        mm = pe.transpose(pt[:, 0:64], kcr[0:64, :], ident[0:64, 0:64])
                    elif kind == "cmp":
                        pe.wait_ge(probs_ready, count["probs"][k])
                        for g in range(2):
                            mm = pe.transpose(pt[:, P * g:P * g + P], prob[:, k % 2, P * g:P * g + P], ident)
                    elif kind == "ret":
                        e = DH * s["half"]
                        for c in range(4):
                            z = slice(P * c + e, P * c + e + DH)
                            mm = pe.matmul(pt[e:e + DH, DH * c:DH * c + DH], rk[:, s["j"], z], rv[:, s["j"], z],
                                           start=True, stop=True)
                    else:
                        pe.wait_ge(probs_ready, count["probs"][k])
                        b = 0
                        for h, t, o in s["segs"]:
                            for jb in range(2 if s["fam"] == "mem" else t + 1):
                                mm = pe.transpose(pt[:, P * b:P * b + P],
                                                  prob[:, k % 2, o + P * jb:o + P * jb + P], ident)
                                b += 1
                    mm.then_inc(turned, 1)

                def values(k):
                    s = steps[k]
                    if not has(s, "values"):
                        return
                    for p in range(k - 1, -1, -1):
                        if has(steps[p], "out"):
                            pe.wait_ge(out_taken, count["out"][p])
                            break
                    else:
                        pe.wait_ge(h_taken, 2 * NT)
                    if s["kind"] == "ret":
                        pe.wait_ge(rows_ready, count["rows"][k])
                        if s["j"]:
                            wait_taken(pe, max(p for p in range(k) if steps[p]["kind"] == "ret" and
                                               steps[p]["half"] == s["half"]))
                        e = DH * s["half"]
                        for c in range(4):
                            d = po[:, DH * c:DH * c + DH]
                            if s["j"]:
                                pe.matmul(d, rqT[e:e + DH, c, P * s["j"]:P * s["j"] + P],
                                          Rst[e:e + DH, s["j"] % 2, c], start=True, stop=False)
                            mm = pe.matmul(d, prob[:, k % 2, P * c:P * c + P],
                                           rv[:, s["j"], P * c + e:P * c + e + DH], start=s["j"] == 0, stop=True)
                    elif s["kind"] == "cmp":
                        wait_taken(pe, k)
                        for g in range(2):
                            mm = pe.matmul(po[:, 256 * g:256 * g + 256], probT[:, k % 2, P * g:P * g + P],
                                           vbd[:, g].rearrange("p r n -> p (r n)"), start=True, stop=True)
                    else:
                        wait_taken(pe, k)
                        b = 0
                        for i, (h, t, o) in enumerate(s["segs"]):
                            w = MDH if s["fam"] == "mem" else DH
                            v = heads(s, h)[3]
                            nb = 2 if s["fam"] == "mem" else t + 1
                            for jb in range(nb):
                                mm = pe.matmul(po[:, w * i:w * i + w], probT[:, k % 2, P * b:P * b + P], v[:, jb],
                                               start=jb == 0, stop=jb == nb - 1)
                                b += 1
                    mm.then_inc(values_ready, 1)

                def step(k):
                    scores(k)
                    if k >= 2:
                        values(k - 2)
                    if k >= 1:
                        turn(k - 1)

                for b in beats:
                    projection(b)
                    for k in b["steps"]:
                        step(k)

            @block.scalar
            def _(act):
                marks = {}

                def link(ins):
                    marks["c"] = marks.get("c", 0) + 1
                    ins.then_inc(chain_act, 1)
                    act.wait_ge(chain_act, marks["c"])

                def done(ins, s, key):
                    marks[key] = marks.get(key, 0) + 1
                    ins.then_inc(s, 1)
                    act.wait_ge(s, marks[key])

                A = nc.scalar.activation

                def high(u):
                    act.wait_ge(raw_in[u % 2], 16 * (u // 2 + 1))
                    if u >= 2:
                        wait_beat(act, pl.unit_end[u - 2])
                    done(A(w_hi[:, u % 2].rearrange("p k n -> p (k n)"), raw[:, u % 2], ACT.Copy), hi_ready, "hi")

                act.wait_ge(x_in, 16)
                act.wait_ge(consts_in, 16 * N_CONST)
                for j in range(NT):
                    link(A(a_lo[:, 8:10].rearrange("p k n -> p (k n)"), x0[:, j], ACT.Square,
                           accum_out=ss[:, j:j + 1]))
                act.wait_ge(eps_ready, 1)
                done(A(sd, ss, ACT.Sqrt, bias=CI["eps"], scale=1.0 / D), ready_act, "r")
                act.wait_ge(crow_in, 16)
                link(A(crow, crow, ACT.Silu))
                done(A(CI["sc"], CI["c"], ACT.Silu), ready_act, "r")
                act.wait_ge(ready_dve, DVE_TAB)
                link(A(rope_s[:], rope_s[:], ACT.Sin))
                done(A(rope_c[:], rope_c[:], ACT.Sin), ready_act, "r")
                high(0)
                for n in range(2 * NT):
                    j, half = divmod(n, 2)
                    act.wait_ge(stage_ready, n + 1)
                    done(A(a_hi[:, 4 * half:4 * half + 4, P * j:P * j + P], stage[:, n % 2], ACT.Copy),
                         stage_high, "sh")
                act.wait_ge(ada_used, 8)
                act.dma_start(gpost, t_in["g_post"].broadcast_to([P, D])).then_inc(gpost_in, 16)
                high(1)

                def probs(k):
                    s = steps[k]
                    if not has(s, "probs"):
                        return
                    kind = s["kind"]
                    if kind == "sm":
                        act.wait_ge(rows_ready, count["rows"][k])
                        wait_probs_slot(act, k)
                        for i, (h, t, o) in enumerate(s["segs"]):
                            n = MEM if s["fam"] == "mem" else P * (t + 1)
                            ins = A(prob[:, k % 2, o:o + n], sc[k % 2][:, o:o + n], ACT.Exp,
                                    bias=nmax[:, k % 4, i:i + 1], accum_out=rsum[:, k % 4, i:i + 1])
                            if i < len(s["segs"]) - 1:
                                link(ins)
                        done(ins, probs_ready, "p")
                    elif kind == "cmp":
                        act.wait_ge(rows_ready, count["rows"][k])
                        done(A(prob[:, k % 2, 0:256], prob[:, k % 2, 0:256], ACT.Exp), probs_ready, "p")
                    elif kind == "hid":
                        act.wait_ge(scores_ready, count["scores"][k])
                        link(A(probT[:, k % 2, 0:128], sc[k % 2][:, 0:128], ACT.Silu))
                        hv = prob[:, k % 2].rearrange("p (m g r n) -> p m g r n", m=2, g=2, r=4)
                        sv = sc[k % 2][:, 128:256].rearrange("p (m g n) -> p m g n", m=2, g=2)
                        link(A(hv[:, 0], sv[:, 0].unsqueeze(2).broadcast_to([P, 2, 4, 32]), ACT.Silu))
                        done(A(hv[:, 1], sv[:, 1].unsqueeze(2).broadcast_to([P, 2, 4, 32]), ACT.Silu),
                             probs_ready, "p")
                    elif kind == "gates":
                        wait_evac(act, max(b["b"] for b in beats if b["name"] == "N2"))
                        done(A(glog[:], glog[:], ACT.Tanh, scale=0.5), probs_ready, "p")
                    elif kind == "gn":
                        act.wait_ge(rows_ready, count["rows"][k])
                        done(A(gvar[:, s["j"]], gvar[:, s["j"]], ACT.Sqrt, bias=CI["epsg"], scale=1.0 / DH),
                             probs_ready, "p")
                    elif kind in ("mnorm", "j1", "j2"):
                        if kind == "mnorm":
                            act.wait_ge(mem_in, 16)
                            t = memr[:, s["j"]]
                        elif kind == "j1":
                            wait_evac(act, s["beat"])
                            t = yo[:, s["j"]]
                        elif s["which"] == 0:
                            wait_taken(act, max(p for p in range(k) if steps[p]["kind"] == "j1" and
                                                steps[p]["j"] == s["j"]))
                            t = x1[:, s["j"]]
                        else:
                            wait_evac(act, s["beat"])
                            t = x2[:, s["j"]]
                        rms = norm[:, s["norm"]:s["norm"] + 1]
                        link(A(dump, t, ACT.Square, accum_out=rms))
                        done(A(rms, rms, ACT.Sqrt, bias=CI["eps"], scale=1.0 / D),
                             probs_ready, "p")
                    elif kind == "qn":
                        act.wait_ge(rows_ready, count["rows"][k])
                        n, w = s["nh"], S // s["nh"]
                        done(A(qsd[:, s["slot"], 0:n], qss[:, s["slot"], 0:n], ACT.Sqrt, bias=CI["eps"],
                               scale=1.0 / w), probs_ready, "p")

                def take(k):
                    s = steps[k]
                    if s["kind"] not in ("sm", "trh"):
                        return
                    act.wait_ge(turned, count["turn"][k])
                    if s["kind"] == "trh":
                        wait_region(act, s["kt"], s["in_beat"] - s["mid"])
                        done(A(a_hi[:, s["kt"]:s["kt"] + 4, P * s["j"]:P * s["j"] + P],
                               sc[k % 2][:].rearrange("p (b n) -> p b n", b=4), ACT.Copy), high_taken, "h")
                        return
                    done(A(probT[:, k % 2], pt[:], ACT.Copy), taken_act, "t")

                def step(k):
                    probs(k)
                    if k >= 1:
                        take(k - 1)
                        s = steps[k - 1]
                        if s["kind"] == "tr" and s["to"] == "n1" and s["j"] == NT - 1:
                            wait_taken(act, k - 1)
                            for l in range(2):
                                for g in range(2):
                                    act.dma_start(cblk[DH * l:DH * l + DH, :, g, 0:S - l],
                                                  kvT[DH * g:DH * g + DH, :, l:S]).then_inc(gather_in, 16)

                last_nsa = max(s["k"] for s in steps if s.get("fam") == "nsa")
                for b in beats:
                    if b["unit_first"] and b["u"] >= 1 and b["u"] + 1 < NU:
                        high(b["u"] + 1)
                    for k in b["mid"]:
                        step(k)
                    name = b["name"]
                    if name == "N2" and b["first"] and b["j"] == 0:
                        act.wait_ge(ready_dve, DVE_X)
                        for v, kv in enumerate("kv"):
                            act.dma_start(w1[:, v], t_in["cmp_w1_" + kv].rearrange("a (m p) n -> p (a m) n", p=P)
                                          ).then_inc(w1_in, 16)
                    if b["last"]:
                        j = b["j"]
                        if name in ("NG", "RG"):
                            wait_beat(act, b["b"])
                            if name == "NG":
                                act.wait_ge(values_ready, count["values"][last_nsa])
                            else:
                                wait_evac(act, b["b"] - 8)
                            done(A(sg[:, j], pj[b["bank"]][:], ACT.Tanh, scale=0.5), pair_act, "pair")
                        elif name == "WO":
                            wait_beat(act, b["b"])
                            done(A(yo[:, j, 512 * b["c"]:512 * b["c"] + 512], pj[b["bank"]][:], ACT.Copy),
                                 evac_act, "e")
                        elif name in ("MV", "V"):
                            wait_beat(act, b["b"])
                            done(A((vm if name == "MV" else vmo)[:, j], pj[b["bank"]][:], ACT.Copy), evac_act, "e")
                        elif name in ("MK", "Q", "K", "QM"):
                            s = pl.src_of_beat[b["b"]]
                            wait_beat(act, b["b"])
                            if s["slot_prev"] is not None:
                                act.wait_ge(turned, count["turn"][s["slot_prev"]])
                            link(A(src[:, s["slot"]], pj[b["bank"]][:], ACT.Copy))
                            done(A(tmp[:, s["slot"]], pj[b["bank"]][:], ACT.Square), evac_act, "e")
                        elif name == "CC":
                            wait_beat(act, b["b"])
                            act.wait_ge(x1_saved, 16)
                            done(A(ucv[:, j], pj[b["bank"]][:], ACT.Copy), evac_act, "e")
                        elif name == "G":
                            wait_beat(act, b["b"])
                            prev = [q for q in beats[:b["b"]] if q["name"] in ("CB", "B") and q["last"]
                                    and q["j"] == j][-1]
                            wait_evac(act, prev["b"])
                            done(A(tg[:, j], pj[b["bank"]][:], ACT.Tanh,
                                   bias=CI["b_gate"][:, 8 * b["gi"] + 4 * b["c"] + j:][:, 0:1], scale=0.5),
                                 evac_act, "e")
                        elif name == "UA":
                            wait_evac(act, b["b"])
                            prev = [q for q in beats[:b["b"]] if q["name"] == "UB" and q["last"]]
                            if prev:
                                wait_evac(act, prev[-1]["b"])
                            done(A(fsi[:, j], fcv[:, j], ACT.Silu), pair_act, "pair")
                    for k in b["steps"]:
                        step(k)
                    if name == "RG" and b["last"] and b["j"] == 3:
                        last_ret = max(s["k"] for s in steps if s["kind"] == "ret")
                        act.wait_ge(out_taken, count["out"][last_ret])
                        act.dma_start(g_mem_row, t_in["g_mem_2"].rearrange("(a d) -> a d", a=1).broadcast_to([P, D])
                                      ).then_inc(gmem_in, 16)
                        act.dma_start(memr, t_in["mem_2"].rearrange("a (t p) d -> p (a t) d", p=P)).then_inc(mem_in, 16)
                    if name == "WO" and b["first"] and b["c"] == 0 and b["j"] == 0:
                        p = max(s["k"] for s in steps if s["kind"] == "trh" and s["src"] == "att")
                        wait_taken(act, p)
                        act.dma_start(g_row, t_in["g_mix_2"].rearrange("(a d) -> a d", a=1).broadcast_to([P, D])
                                      ).then_inc(grow_in, 16)
                    if name == "WY" and b["first"] and b["c"] == 0 and b["j"] == 0:
                        act.dma_start(g_row, t_in["g_ffn_2"].rearrange("(a d) -> a d", a=1).broadcast_to([P, D])
                                      ).then_inc(grow_in, 16)
                    if name == "WO" and b["last"] and b["c"] == 0 and b["j"] == 0:
                        wait_evac(act, max(q["b"] for q in beats if q["name"] == "RG"))
                        act.dma_start(x1, t_in["x"].rearrange("a (t p) d -> p (a t) d", p=P)).then_inc(xres_in, 16)
                    if name == "MV" and b["last"] and b["j"] == 1:
                        p = max(s["k"] for s in steps if s["kind"] == "j1")
                        wait_taken(act, p)
                        act.dma_start(x1_dram.rearrange("(t p) d -> p t d", p=P), x1).then_inc(x1_saved, 16)
                    if name == "B" and b["i"] == 1 and b["c"] == 0 and b["j"] == 3:
                        p = max(s["k"] for s in steps if s["kind"] == "sm")
                        act.wait_ge(out_taken, count["out"][p])
                        act.dma_start(x2, x1_dram.rearrange("(t p) d -> p t d", p=P)).then_inc(x1_back, 16)

            @block.vector
            def _(dve):
                V = nc.vector
                marks = {}

                def link(ins):
                    marks["c"] = marks.get("c", 0) + 1
                    ins.then_inc(chain_dve, 1)
                    dve.wait_ge(chain_dve, marks["c"])

                def done(ins, s, key):
                    marks[key] = marks.get(key, 0) + 1
                    ins.then_inc(s, 1)
                    dve.wait_ge(s, marks[key])

                def split(kt, q, value, s, key):
                    link(V.tensor_copy(a_hi[:, kt, q], value))
                    done(V.tensor_tensor(a_lo[:, kt, q], value, a_hi[:, kt, q].bitcast(F32), ALU.subtract), s, key)

                link(V.memset(CI["epsg"], 1e-5))
                done(V.memset(CI["eps"], EPS), eps_ready, "eps")
                dve.wait_ge(consts_in, 16 * N_CONST)
                link(V.tensor_copy(idb[:], ident))
                link(V.tensor_tensor(pj[0][:, 0:P], tri, ident, ALU.subtract))
                link(V.tensor_scalar(maskb[:], pj[0][:, 0:P], NEG, None, ALU.mult))
                dve.wait_ge(ready_act, 1)
                link(V.reciprocal(rr, sd))
                for j in range(NT):
                    ins = V.tensor_scalar(x0[:, j], x0[:, j], rr[:, j:j + 1], None, ALU.mult)
                    if j < NT - 1:
                        link(ins)
                done(ins, ready_dve, "r")
                dve.wait_ge(ready_act, 2)
                done(V.tensor_copy(scb, CI["sc"].unsqueeze(2).broadcast_to([P, KT, P])), ready_dve, "r")
                ang = tmp[:, 0, 0:5 * NF].rearrange("p (t f) -> p t f", t=5)
                rnd = tmp[:, 0, 200:400].rearrange("p (t f) -> p t f", t=5)
                posf = small[:, 120:125]
                link(V.memset(posf, 0.0))
                link(V.tensor_copy(posf[:, 0:4], posi[:, 0:4]))
                for g in range(2):
                    link(V.tensor_copy(posf[32 * g:32 * g + NCMP, 4:5], posi[32 * g:32 * g + NCMP, 4:5]))
                inv = cst[:, C_INV:C_INV + NF]
                link(V.tensor_tensor(ang, posf.unsqueeze(2).broadcast_to([P, 5, NF]),
                                     inv.unsqueeze(1).broadcast_to([P, 5, NF]), ALU.mult))
                link(V.tensor_scalar(rnd, ang, 1.0 / (2 * np.pi), ROUND, ALU.mult, ALU.add))
                link(V.tensor_scalar(rnd, rnd, ROUND, None, ALU.subtract))
                for part in (TWO_PI_A, TWO_PI_B, TWO_PI_C):
                    link(V.scalar_tensor_tensor(ang, rnd, -part, ang, ALU.mult, ALU.add))
                link(V.tensor_scalar(rope_s[:], ang, 3.1415925, -3.1415925, ALU.min, ALU.max))
                link(V.scalar_tensor_tensor(rnd, rope_s[:], -1.0, rope_s[:], ALU.mult, ALU.max))
                done(V.tensor_scalar(rope_c[:], rnd, -1.0, np.pi / 2, ALU.mult, ALU.add), ready_dve, "r")
                for i in range(8):
                    dve.wait_ge(ada_in[i % 4], 16 * (i // 4 + 1))
                    for m in range(2):
                        col = (CI["cb"], CI["ca"])[i // 4][:, 2 * (i % 4) + m:2 * (i % 4) + m + 1]
                        ins = V.tensor_tensor_reduce(out=ada_t[:, i % 4, m], in0=ada_t[:, i % 4, m], in1=crow,
                                                     scale=1.0, scalar=0.0, op0=ALU.mult, op1=ALU.add,
                                                     accum_out=col)
                        if m == 0:
                            link(ins)
                    done(ins, ada_used, "ada")
                link(V.tensor_tensor(CI["cb"], CI["cb"], CI["b_ada"][:, 0:8], ALU.add))
                link(V.tensor_tensor(CI["ca"], CI["ca"], CI["b_ada"][:, 8:16], ALU.add))
                link(V.scalar_tensor_tensor(CI["ca"], CI["ca"], 1.0, CI["g_pre"], ALU.add, ALU.mult))

                def h_low(n):
                    j, half = divmod(n, 2)
                    dve.wait_ge(stage_high, n + 1)
                    kt, q = slice(4 * half, 4 * half + 4), slice(P * j, P * j + P)
                    done(V.tensor_tensor(a_lo[:, kt, q], stage[:, n % 2], a_hi[:, kt, q].bitcast(F32),
                                         ALU.subtract), h_taken, "x")

                for n in range(2 * NT):
                    dve.wait_ge(ready_pe, 1 + n)
                    for q in range(4):
                        kt = 4 * (n % 2) + q
                        ins = V.tensor_scalar(stage[:, n % 2, q], xbank[n % 6][:, P * q:P * q + P],
                                              CI["ca"][:, kt:kt + 1], CI["cb"][:, kt:kt + 1], ALU.mult, ALU.add)
                        if q < 3:
                            link(ins)
                    done(ins, stage_ready, "st")
                    if n:
                        h_low(n - 1)
                h_low(2 * NT - 1)
                dve.wait_ge(params_in, 16 * N_PARAM)
                dve.wait_ge(gpost_in, 16)
                for c in range(2):
                    half = gp[:, 512 * c:512 * c + 512]
                    dve.wait_ge(ready_pe, PE_GATE - 1 + c)
                    link(V.tensor_tensor(half, half, pj[c][:], ALU.add))
                    link(V.tensor_tensor(half, half, gpost[:, 512 * c:512 * c + 512], ALU.mult))
                link(V.tensor_scalar(CI["b_gate"], CI["b_gate"], 0.5, None, ALU.mult))
                link(V.memset(kcT.rearrange("p g e n -> p (g e n)"), 0.0))
                done(V.memset(vbd.rearrange("p g r n -> p (g r n)"), 0.0), ready_dve, "r")

                def rotate(dst, s, nh, w, half, c, sn, scale_first=None):
                    a = s[:, :, 0:2 * half].rearrange("p h (t f) -> p h t f", t=2)
                    n = nh * 2 * half
                    np_ = s.shape[0]
                    bc = c.unsqueeze(1).unsqueeze(1).broadcast_to([np_, nh, 2, half])
                    bs = sn.unsqueeze(1).unsqueeze(1).broadcast_to([np_, nh, 2, half])
                    tc_ = tmp[0:np_, 0, 0:n].rearrange("p (h t f) -> p h t f", h=nh, t=2)
                    ts_ = tmp[0:np_, 1, 0:n].rearrange("p (h t f) -> p h t f", h=nh, t=2)
                    link(V.tensor_tensor(tc_, a, bc, ALU.mult))
                    link(V.tensor_tensor(ts_, a, bs, ALU.mult))
                    link(V.tensor_tensor(dst[:, :, 0:half], tc_[:, :, 0], ts_[:, :, 1], ALU.subtract))
                    return V.tensor_tensor(dst[:, :, half:2 * half], ts_[:, :, 0], tc_[:, :, 1], ALU.add)

                def h3(ap, w):
                    return ap.rearrange("p (h d) -> p h d", d=w)

                def src_slot(b):
                    s = pl.src_of_beat[b["b"]]
                    if s["slot_prev"] is not None:
                        dve.wait_ge(turned, count["turn"][s["slot_prev"]])
                    return src[:, s["slot"]], s["slot"]

                def evacuate(b):
                    if not b["last"] or b["evac"] != "dve":
                        return
                    wait_beat(dve, b["b"])
                    name, j, bank = b["name"], b["j"], pj[b["bank"]]
                    cr, sr = rope_c[:, j, 0:NF_RET], rope_s[:, j, 0:NF_RET]
                    cn, sn = rope_c[:, j, NF_RET:NF], rope_s[:, j, NF_RET:NF]

                    def e(ins):
                        done(ins, evac_dve, "e")

                    if name == "N1":
                        t, _ = src_slot(b)
                        link(V.tensor_copy(t[:, 0:256], bank[:, 0:256]))
                        d4 = t[:, 256:512].rearrange("p (g r d) -> p g r d", g=2, r=2)
                        link(V.tensor_copy(d4[:, :, 0], h3(bank[:, 256:384], DH)))
                        link(rotate(d4[:, :, 0], h3(bank[:, 256:384], DH), 2, DH, 8, cn, sn))
                        link(V.tensor_copy(d4[:, :, 1], d4[:, :, 0]))
                        e(V.tensor_copy(vsel[:, j], bank[:, 384:512]))
                    elif name == "N2":
                        t, _ = src_slot(b)
                        d4 = t[:, 0:256].rearrange("p (g r d) -> p g r d", g=2, r=2)
                        link(V.tensor_copy(d4[:, :, 0], h3(bank[:, 0:128], DH)))
                        link(rotate(d4[:, :, 0], h3(bank[:, 0:128], DH), 2, DH, 8, cn, sn))
                        link(V.tensor_copy(d4[:, :, 1], d4[:, :, 0]))
                        link(V.tensor_copy(vwin[:, j], bank[:, 128:256]))
                        e(V.tensor_copy(glog[:, j], bank[:, 256:280]))
                    elif name == "NQ":
                        t, _ = src_slot(b)
                        link(V.tensor_copy(t, bank[:]))
                        link(rotate(h3(t, DH), h3(bank[:], DH), H, DH, 8, cn, sn))
                        e(V.tensor_scalar(t, t, DH ** -0.5, None, ALU.mult))
                    elif name == "RQ":
                        t, _ = src_slot(b)
                        link(rotate(h3(t, DH), h3(bank[:], DH), H, DH, 32, cr, sr))
                        e(V.tensor_scalar(t, t, DH ** -0.5, None, ALU.mult))
                    elif name == "RK":
                        e(rotate(h3(rk[:, j], DH), h3(bank[:], DH), H, DH, 32, cr, sr))
                    elif name == "RV":
                        e(V.tensor_tensor(h3(rv[:, j], DH), h3(bank[:], DH),
                                          cst[:, C_VSC:C_VSC + H].unsqueeze(2).broadcast_to([P, H, DH]), ALU.mult))
                    elif name == "NG":
                        dve.wait_ge(pair_act, pair_n[b["b"]])
                        link(V.scalar_tensor_tensor(tmp[:, 0], sg[:, j], 1.0, bank[:], ALU.add, ALU.mult))
                        e(V.scalar_tensor_tensor(att[:, j], tmp[:, 0], 0.25, att[:, j], ALU.mult, ALU.mult))
                    elif name == "RG":
                        dve.wait_ge(pair_act, pair_n[b["b"]])
                        p = [s["k"] for s in steps if s["kind"] == "gn" and s["j"] == j][0]
                        dve.wait_ge(probs_ready, count["probs"][p])
                        link(V.reciprocal(rs8, gvar[:, j]))
                        link(V.tensor_tensor(h3(rk[:, j], DH), h3(rk[:, j], DH),
                                             rs8.unsqueeze(2).broadcast_to([P, H, DH]), ALU.mult))
                        link(V.scalar_tensor_tensor(tmp[:, 0], sg[:, j], 1.0, bank[:], ALU.add, ALU.mult))
                        e(V.scalar_tensor_tensor(rk[:, j], tmp[:, 0], 0.5, rk[:, j], ALU.mult, ALU.mult))
                    elif name == "CX":
                        wait_evac(dve, b["b"] - 8)
                        e(V.tensor_tensor(ucv[:, j], ucv[:, j], bank[:], ALU.mult))
                    elif name == "CB":
                        w = [CI["conv_w"][:, 4 * i + j:4 * i + j + 1] for i in range(3)]
                        t = tmp[:, 0]
                        link(V.tensor_scalar(t, ucv[:, j], w[2], CI["conv_b"][:, j:j + 1], ALU.mult, ALU.add))
                        link(V.scalar_tensor_tensor(t[:, 1:], ucv[:, j, 0:S - 1], w[1], t[:, 1:], ALU.mult, ALU.add))
                        link(V.scalar_tensor_tensor(t[:, 2:], ucv[:, j, 0:S - 2], w[0], t[:, 2:], ALU.mult, ALU.add))
                        link(V.tensor_tensor(tmp[:, 1], t, bank[:], ALU.mult))
                        wait_region(dve, b["act_kt"], b["b"])
                        split(b["act_kt"], slice(0, S), tmp[:, 1], evac_dve, "e")
                    elif name == "B":
                        m = merged[:, 4 * b["c"] + j]
                        wait_evac(dve, b["b"] - 4)
                        if b["i"] == 0:
                            e(V.scalar_tensor_tensor(m, tg[:, j], 1.0, bank[:], ALU.add, ALU.mult))
                        else:
                            link(V.scalar_tensor_tensor(tmp[:, 0], tg[:, j], 1.0, bank[:], ALU.add, ALU.mult))
                            if b["i"] == 1:
                                e(V.tensor_tensor(m, m, tmp[:, 0], ALU.add))
                            else:
                                link(V.tensor_tensor(m, m, tmp[:, 0], ALU.add))
                                link(V.tensor_scalar(tmp[:, 1], m, 0.5, None, ALU.mult))
                                wait_region(dve, b["act_kt"], b["b"])
                                split(b["act_kt"], slice(0, S), tmp[:, 1], evac_dve, "e")
                    elif name == "WY":
                        if b["c"] == 0 and j == 0:
                            dve.wait_ge(x1_back, 16)
                        t = x2[:, j, 512 * b["c"]:512 * b["c"] + 512]
                        e(V.tensor_tensor(t, t, bank[:], ALU.add))
                    elif name == "UA":
                        ct = b["ch"] + j
                        w = [ffw[:, i, ct:ct + 1] for i in range(4)]
                        t = fcv[:, j]
                        prev = [q for q in beats[:b["b"]] if q["name"] == "UA" and q["last"] and q["j"] == j]
                        if prev:
                            dve.wait_ge(pair_act, pair_n[prev[-1]["b"]])
                        link(V.tensor_scalar(t, bank[:], w[2], w[3], ALU.mult, ALU.add))
                        link(V.scalar_tensor_tensor(t[:, 1:], bank[:, 0:S - 1], w[1], t[:, 1:], ALU.mult, ALU.add))
                        e(V.scalar_tensor_tensor(t[:, 2:], bank[:, 0:S - 2], w[0], t[:, 2:], ALU.mult, ALU.add))
                    elif name == "UB":
                        jj = b["act_kt"] - b["act"]
                        ua = [q for q in beats[:b["b"]] if q["name"] == "UA" and q["last"] and q["j"] == jj][-1]
                        dve.wait_ge(pair_act, pair_n[ua["b"]])
                        link(V.tensor_tensor(tmp[:, 1], fsi[:, jj], bank[:], ALU.mult))
                        wait_region(dve, b["act_kt"], b["b"])
                        split(b["act_kt"], slice(0, S), tmp[:, 1], evac_dve, "e")
                    elif name == "DN":
                        t = x2[:, j, 512 * b["c"]:512 * b["c"] + 512]
                        e(V.tensor_tensor(t, t, bank[:], ALU.add))

                def rows(k):
                    s = steps[k]
                    if not has(s, "rows"):
                        return
                    kind = s["kind"]
                    if kind == "sm":
                        dve.wait_ge(scores_ready, count["scores"][k])
                        for i, (h, t, o) in enumerate(s["segs"]):
                            n = MEM if s["fam"] == "mem" else P * (t + 1)
                            ins = V.tensor_reduce(nmax[:, k % 4, i:i + 1], sc[k % 2][:, o:o + n], AX_X, ALU.max,
                                                  negate=True)
                            if i < len(s["segs"]) - 1:
                                link(ins)
                        done(ins, rows_ready, "s")
                    elif kind == "cmp":
                        dve.wait_ge(scores_ready, count["scores"][k])
                        wait_probs_slot(dve, k)
                        pr = prob[:, k % 2, 0:256].rearrange("p (h n) -> p h n", h=H)
                        link(V.tensor_tensor(pr, sc[k % 2][:, 0:256].rearrange("p (h n) -> p h n", h=H),
                                             cmpb[:, s["j"]].unsqueeze(1).broadcast_to([P, H, 32]), ALU.add))
                        link(V.reduce_max(st8, pr, axis=AX_X))
                        done(V.tensor_tensor(pr, pr, st8.unsqueeze(2).broadcast_to([P, H, 32]), ALU.subtract),
                             rows_ready, "s")
                    elif kind == "ret":
                        dve.wait_ge(scores_ready, count["scores"][k])
                        wait_probs_slot(dve, k)
                        done(V.tensor_tensor(prob[:, k % 2].rearrange("p (h n) -> p h n", h=4),
                                             sc[k % 2][:].rearrange("p (h n) -> p h n", h=4),
                                             tri.unsqueeze(1).broadcast_to([P, 4, P]), ALU.mult), rows_ready, "s")
                    elif kind == "cmv":
                        dve.wait_ge(gather_in, 64)
                        link(V.memset(cmv.rearrange("p v m g n -> p (v m g) n")[:, :, NCMP:32], 0.0))
                        for v in range(2):
                            for g in range(2):
                                for a in range(2):
                                    blk = cblk[:, v, g].rearrange("p (n m l) -> p m n l", m=8, l=2)
                                    ins = V.tensor_tensor(
                                        cmv[:, v, 8 * a:8 * a + 8, g, 0:NCMP], blk[:, :, a:a + NCMP, 0],
                                        cpe[:, v, 8 * a:8 * a + 8].unsqueeze(2).broadcast_to([P, 8, NCMP]), ALU.add)
                                    if (v, g, a) != (1, 1, 1):
                                        link(ins)
                        done(ins, rows_ready, "s")
                    elif kind == "qn":
                        wait_evac(dve, s["beat"])
                        done(V.reduce_sum(qss[:, s["slot"], 0:s["nh"]], h3(tmp[:, s["slot"]], S // s["nh"]),
                                          axis=AX_X), rows_ready, "s")
                    elif kind == "gn":
                        t = h3(rk[:, s["j"]], DH)
                        link(V.reduce_sum(st8, t, axis=AX_X))
                        link(V.tensor_scalar(st8, st8, 1.0 / DH, None, ALU.mult))
                        link(V.tensor_tensor(t, t, st8.unsqueeze(2).broadcast_to([P, H, DH]), ALU.subtract))
                        link(V.tensor_tensor(h3(tmp[:, 0], DH), t, t, ALU.mult))
                        done(V.reduce_sum(gvar[:, s["j"]], h3(tmp[:, 0], DH), axis=AX_X), rows_ready, "s")

                def outputs(k):
                    s = steps[k]
                    if not has(s, "out"):
                        return
                    dve.wait_ge(values_ready, count["values"][k])
                    kind = s["kind"]
                    if kind == "cmp":
                        j = s["j"]
                        link(V.reciprocal(cf8, rs8))
                        gl = glog[:, j].rearrange("p (h c) -> p h c", c=3)[:, :, 0]
                        link(V.scalar_tensor_tensor(cf8, gl, 1.0, cf8, ALU.add, ALU.mult))
                        link(V.tensor_scalar(cf8, cf8, cst[:, C_ROW + j:C_ROW + j + 1], None, ALU.mult))
                        done(V.tensor_tensor(h3(att[:, j], DH), h3(po[:], DH),
                                             cf8.unsqueeze(2).broadcast_to([P, H, DH]), ALU.mult), out_taken, "o")
                    elif kind == "ret":
                        e = s["half"]
                        done(V.tensor_tensor(rk[:, s["j"]].rearrange("p (c e d) -> p c e d", c=4, e=2)[:, :, e],
                                             h3(po[:, 0:256], DH),
                                             cst[:, C_XI + 4 * e:C_XI + 4 * e + 4].unsqueeze(2)
                                             .broadcast_to([P, 4, DH]), ALU.mult), out_taken, "o")
                    else:
                        n = len(s["segs"])
                        link(V.reciprocal(ri[:, 0:n], rsum[:, k % 4, 0:n]))
                        for i, (h, t, o) in enumerate(s["segs"]):
                            if s["fam"] == "nsa":
                                g = 3 * h + 1 + s["br"]
                                link(V.scalar_tensor_tensor(cf[:, i:i + 1], glog[:, t, g:g + 1], 1.0, ri[:, i:i + 1],
                                                            ALU.add, ALU.mult))
                                d = att[:, t, DH * h:DH * h + DH]
                                ins = V.scalar_tensor_tensor(d, po[:, DH * i:DH * i + DH], cf[:, i:i + 1], d,
                                                             ALU.mult, ALU.add)
                            elif s["fam"] == "moba":
                                if i == 0:
                                    dve.wait_ge(x1_saved, 16)
                                ins = V.tensor_scalar(ymo[:, t, DH * h:DH * h + DH], po[:, DH * i:DH * i + DH],
                                                      ri[:, i:i + 1], None, ALU.mult)
                            else:
                                m = pl.src_mem[t]
                                if m["slot_prev"] is not None:
                                    dve.wait_ge(turned, count["turn"][m["slot_prev"]])
                                ins = V.tensor_scalar(src[:, m["slot"], MDH * h:MDH * h + MDH],
                                                      po[:, MDH * i:MDH * i + MDH], ri[:, i:i + 1], None, ALU.mult)
                            if i < n - 1:
                                link(ins)
                        done(ins, out_taken, "o")

                def take(k):
                    s = steps[k]
                    if not has(s, "take") or s["kind"] == "sm":
                        return
                    kind = s["kind"]

                    def f(ins):
                        done(ins, taken_dve, "t")

                    if has(s, "turn"):
                        dve.wait_ge(turned, count["turn"][k])
                    elif has(s, "probs"):
                        dve.wait_ge(probs_ready, count["probs"][k])
                    q = slice(P * s.get("j", 0), P * s.get("j", 0) + P)
                    p4 = pt[:].rearrange("p (b n) -> p b n", b=4)
                    if kind == "tr":
                        to = s["to"]
                        if to == "n1":
                            link(V.tensor_copy(kvT[:, :, q], p4[:, 0:2]))
                            f(V.tensor_copy(ncT[:, 0:2, q], p4[:, 2:4]))
                        elif to == "n2":
                            f(V.tensor_copy(ncT[:, 2:4, q], p4[:, 0:2]))
                        elif to in ("nq", "rq", "rk"):
                            f(V.tensor_copy({"nq": nqT, "rq": rqT, "rk": rkT}[to][:, :, q], p4))
                        elif to == "mk":
                            f(V.tensor_scalar(kmT[:, :, q], p4, CI["gmk"], None, ALU.mult))
                        elif to == "Q":
                            f(V.tensor_scalar(qT[:, :, q], p4, CI["gq"], DH ** -0.5, ALU.mult, ALU.mult))
                        elif to == "K":
                            f(V.tensor_scalar(kT[:, :, q], p4, CI["gk"], None, ALU.mult))
                        else:
                            f(V.tensor_scalar(qmT[:, :, q], p4, CI["gmq"], MDH ** -0.5, ALU.mult, ALU.mult))
                    elif kind == "trh":
                        kt = slice(s["kt"], s["kt"] + 4)
                        dve.wait_ge(high_taken, count["high"][k])
                        f(V.tensor_tensor(a_lo[:, kt, q], sc[k % 2][:].rearrange("p (b n) -> p b n", b=4),
                                          a_hi[:, kt, q].bitcast(F32), ALU.subtract))
                    elif kind == "hid":
                        k3 = kcr[0:64, 0:DH].unsqueeze(1)
                        link(V.tensor_copy(kcr[0:64, 0:DH], pt[0:64, 0:DH]))
                        link(rotate(k3, pt[0:64, 0:DH].unsqueeze(1), 1, DH, 8, rope_c[0:64, 4, NF_RET:NF],
                                    rope_s[0:64, 4, NF_RET:NF]))
                        link(V.tensor_copy(kcr[0:64, DH:2 * DH], kcr[0:64, 0:DH]))
                        for r in range(4):
                            z = slice(32 * r, 32 * r + 32)
                            ins = V.tensor_copy(vbd[z, :, r], pt[z, 64:192].rearrange("p (g n) -> p g n", g=2))
                            if r < 3:
                                link(ins)
                        f(ins)
                    elif kind == "kct":
                        for e in range(2):
                            z = slice(DH * e, DH * e + DH)
                            ins = V.tensor_copy(kcT[z, :, e], pt[z, 0:64].rearrange("p (g n) -> p g n", g=2))
                            if e == 0:
                                link(ins)
                        f(ins)
                    elif kind == "cmp":
                        link(V.reduce_sum(rs8, prob[:, k % 2, 0:256].rearrange("p (h n) -> p h n", h=H), axis=AX_X))
                        f(V.tensor_copy(probT[:, k % 2, 0:256], pt[:, 0:256]))
                    elif kind == "ret":
                        e = slice(DH * s["half"], DH * s["half"] + DH)
                        d, new = Rst[e, (s["j"] + 1) % 2], h3(pt[e, 0:256], DH)
                        decay = cst[e, C_DEC:C_DEC + 4].unsqueeze(2).broadcast_to([DH, 4, DH])
                        if s["j"] == 0:
                            f(V.tensor_tensor(d, new, decay, ALU.mult))
                        else:
                            link(V.tensor_tensor(d, Rst[e, s["j"] % 2], new, ALU.add))
                            f(V.tensor_tensor(d, d, decay, ALU.mult))
                    elif kind == "mnorm":
                        rms = norm[:, s["norm"]:s["norm"] + 1]
                        link(V.reciprocal(rms, rms))
                        dve.wait_ge(gmem_in, 16)
                        m = memr[:, s["j"]]
                        f(V.scalar_tensor_tensor(m, m, rms, g_mem_row, ALU.mult, ALU.mult))
                    elif kind == "j1":
                        rms = norm[:, s["norm"]:s["norm"] + 1]
                        if s["j"] == 0:
                            dve.wait_ge(xres_in, 16)
                        link(V.reciprocal(rms, rms))
                        y = yo[:, s["j"]]
                        link(V.scalar_tensor_tensor(y, y, rms, gp[:], ALU.mult, ALU.mult))
                        f(V.tensor_tensor(x1[:, s["j"]], x1[:, s["j"]], y, ALU.add))
                    elif kind == "j2":
                        rms = norm[:, s["norm"]:s["norm"] + 1]
                        link(V.reciprocal(rms, rms))
                        if s["j"] == 0:
                            dve.wait_ge(grow_in, 16 * (s["which"] + 1))
                        if s["j"] >= 2:
                            p = max(p for p in range(k) if steps[p]["kind"] == "trh" and steps[p]["j"] == s["j"] - 2)
                            dve.wait_ge(turned, count["turn"][p])
                        f(V.scalar_tensor_tensor(xn[:, s["j"] % 2], (x1, x2)[s["which"]][:, s["j"]], rms,
                                                 g_row, ALU.mult, ALU.mult))
                    elif kind == "qn":
                        n = s["nh"]
                        t = h3(src[:, s["slot"]], S // n)
                        link(V.reciprocal(qri[:, 0:n], qsd[:, s["slot"], 0:n]))
                        f(V.tensor_tensor(t, t, qri[:, 0:n].unsqueeze(2).broadcast_to([P, n, S // n]), ALU.mult))

                def step(k):
                    rows(k)
                    if k >= 2:
                        outputs(k - 2)
                    if k >= 1:
                        take(k - 1)

                for b in beats:
                    for k in b["mid"]:
                        step(k)
                    evacuate(b)
                    for k in b["steps"]:
                        step(k)


def pack(unit, w):
    name, r, c, n = unit
    u = np.zeros((P, 4, 512), np.float32)
    if name == "w_up2":
        for i, c0 in enumerate((c, DFF + c)):
            u[:, :, n * i:n * i + n] = w["w_up"][r:r + 512, c0:c0 + n].reshape(4, P, n).transpose(1, 0, 2)
    elif name == "w_down2":
        u[:] = w["w_down"][r:r + 2 * P].reshape(2, P, 2, 512).transpose(1, 0, 2, 3).reshape(P, 4, 512)
    else:
        u[:, :, 0:n] = w[name][r:r + 512, c:c + n].reshape(4, P, n).transpose(1, 0, 2)
    return u.reshape(P, 2048)


_INS = ["x", "c", "positions", "b_ada", "g_post", "cmp_w1_k", "cmp_w2_k", "cmp_w1_v", "cmp_w2_v", "mem_2", "g_mem_2",
        "g_mix_2", "g_ffn_2"]


def kernel(**inputs):
    import concourse.bacc as _bacc
    from concourse.bass_utils import run_bass_kernel_spmd as _run

    a = {k: np.asarray(v) for k, v in inputs.items()}
    w = {"w_in": a["w_in"][0], "w_out": a["w_out"][0], "w_mem": a["w_mem_kv_2"], "w_in_2": a["w_in_2"],
         "w_br_conv": a["w_br_conv_2"], "w_br_mem": a["w_br_mem_2"], "w_br_moba": a["w_br_moba_2"],
         "w_o": a["w_o_2"], "w_up": a["w_up_2"], "w_down": a["w_down_2"]}
    arrays = {k: np.ascontiguousarray(a[k]) for k in _INS}
    arrays["weights"] = np.stack([pack(u, w) for u in make_plan().units])
    arrays["ada_t"] = np.ascontiguousarray(a["w_ada"][0][:, 0:2 * D].T)
    arrays["ada_g"] = np.ascontiguousarray(a["w_ada"][0][:, 2 * D:])
    arrays["cols"] = columns(a)
    arrays["cst"] = constants()

    nc = _bacc.Bacc("TRN2", target_bir_lowering=False, num_devices=1)
    t_in = {}
    named = {}
    for name, v in arrays.items():
        named[f"in_{name}"] = v
        t_in[name] = nc.dram_tensor(f"in_{name}", v.shape, mybir.dt.from_np(v.dtype), kind="ExternalInput").ap()
    out = nc.dram_tensor("out", (1, S, D), F32, kind="ExternalOutput").ap()
    with nc.allow_non_contiguous_dma(reason="small per-channel columns"):
        build(nc, t_in, out)
    r = _run(nc, [named], core_ids=[0])
    return r.results[0]["out"]
```

```python
from contextlib import ExitStack

import numpy as np

import concourse.bass as bass
from concourse import mybir

ALU = mybir.AluOpType
ACT = mybir.ActivationFunctionType
F32 = mybir.dt.float32
F32R = mybir.dt.float32r
BF16 = mybir.dt.bfloat16
I32 = mybir.dt.int32
AX_X = mybir.AxisListType.X

P = 128
S = 512
D = 1024
NT = S // P
H = 8
DH = 64
MEM = 256
MH, MDH = 4, 128
KT = D // P
NCMP = 31
DFF = 2816
EPS = 1e-6
NEG = -1e30
TWO_PI_A = 6.28125
TWO_PI_B = float(np.float32(np.float16(2 * np.pi - TWO_PI_A)))
TWO_PI_C = float(2 * np.pi - TWO_PI_A - TWO_PI_B)
ROUND = 12582912.0
NF_RET, NF_NSA = 32, 8
NF = NF_RET + NF_NSA

C_INV, C_VSC, C_XI, C_TRI = 0, NF, NF + 8, NF + 16
C_ID = C_TRI + P
C_DEC = C_ID + P
C_CMPB = C_DEC + 4
C_ROW = C_CMPB + NT * 32
CST = C_ROW + NT
N_CONST, N_PARAM = 5, 2

COLS = (("b_ada", 24), ("g_pre", 8), ("g_post", 8), ("b_gate", 24), ("conv_w", 12), ("conv_b", 4), ("gq", 1),
        ("gk", 1), ("gmq", 1), ("gmk", 1), ("ffw", 88), ("cpe", 32), ("ca", 8), ("cb", 8), ("cg", 8), ("eps", 1),
        ("epsg", 1))
N_COLS = sum(n for _, n in COLS[:12])


def columns(a):
    tile = lambda v: v.reshape(-1, P).T
    pair = lambda v: np.tile(v, 2)[:, None]
    parts = [tile(a["b_ada"][0]), tile(a["g_pre"][0]), tile(a["g_post"][0]), tile(a["b_gate_2"]),
             tile(a["conv_w_2"].reshape(-1)), tile(a["conv_b_2"]), pair(a["moba_q_gain_2"]),
             pair(a["moba_k_gain_2"]), a["memq_gain_2"][:, None], a["memk_gain_2"][:, None],
             tile(a["ffn_conv_w_2"].reshape(-1)), tile(a["ffn_conv_b_2"]), tile(a["cmp_pe_k"].reshape(-1)),
             tile(a["cmp_pe_v"].reshape(-1))]
    return np.ascontiguousarray(np.concatenate(parts, axis=1))


def constants():
    c = np.zeros((P, CST), np.float32)
    f = np.float32
    c[:, C_INV:C_INV + NF_RET] = np.power(f(10000.0), -np.arange(NF_RET, dtype=f) / f(NF_RET))
    c[:, C_INV + NF_RET:C_INV + NF] = np.power(f(500000.0), -np.arange(NF_NSA, dtype=f) / f(NF_NSA))
    log_g = np.log1p(-np.power(2.0, -5.0 - np.arange(H)))
    p = np.arange(P)
    c[:, C_VSC:C_VSC + H] = np.exp(-(p[:, None] + 1.0) * log_g)
    even_odd = [0, 2, 4, 6, 1, 3, 5, 7]
    c[:, C_XI:C_XI + H] = np.exp((p[:, None] + 1.0) * log_g[even_odd])
    c[:, C_TRI:C_TRI + P] = p[:, None] <= p[None, :]
    for h in range(H):
        c[(h % 2) * DH:(h % 2) * DH + DH, C_DEC + h // 2] = np.exp(P * log_g[h])
    c[:, C_ID:C_ID + P] = np.eye(P, dtype=f)
    for t in range(NT):
        for n in range(32):
            ok = (n < NCMP) & (16 * n + 31 <= t * P + p)
            c[:, C_CMPB + t * 32 + n] = np.where(ok, 0.0, NEG)
        c[:, C_ROW + t] = (t * P + p >= 31)
    return c


PANELS1 = [
    ("N1", 2560, 512), ("N2", 3072, 280), ("NQ", 2048, 512), ("RQ", 0, 512), ("RK", 512, 512),
    ("RV", 1024, 512), ("NG", 3352, 512), ("RG", 1536, 512)]
PANELS2 = [("Q", "A", 1536), ("K", "A", 2048), ("V", "A", 2560), ("QM", "A", 3072),
           ("CC", "B", 512), ("CX", "B", 1024), ("CB", "B", 0)]
GATE0 = 3584
FFN_GROUPS = [4, 4, 4, 4, 4, 2]


class Plan:

    def __init__(self):
        self.beats, self.steps, self.units = [], [], []

    def panel(self, name, form, srcs, tiles=4, base=0, n=512, **more):
        first = len(self.beats)
        for i, s in enumerate(srcs):
            self.units.append(s)
            for j in range(tiles):
                self.beats.append(dict(name=name, form=form, u=len(self.units) - 1, j=j, n=n,
                                       first=i == 0, last=i == len(srcs) - 1,
                                       kts=[(base[i] + q, q) for q in range(4)], steps=[], mid=[],
                                       unit_first=j == 0, bank=j, **more))
        return first

    def step(self, start, mid=False, **s):
        s["k"], s["place"] = len(self.steps), (start, bool(mid))
        self.steps.append(s)
        self.beats[start]["mid" if mid else "steps"].append(s["k"])
        return s["k"]


def segments():
    for a in range(0, H, 4):
        for e in range(2):
            for h in (a + e, a + e + 2):
                yield [(h, 3, 0)]
                yield [(h, 0, 0), (h, 2, P)]
            yield [(a + e, 1, 0), (a + e + 2, 1, 2 * P)]


def spread(pl, todo, b, mid, last, last_mid, also=()):
    places = []
    while (b, -mid) <= (last, -last_mid):
        places.append((b, mid))
        b, mid = (b, 0) if mid else (b + 1, 1)
    free = [p for p in places if not (p[1] == 0 and (p[0], 1) in also)]
    n = 0
    for place in places:
        if place in free:
            i = free.index(place)
            while n < len(todo) and n * len(free) // len(todo) <= i:
                pl.step(place[0], mid=bool(place[1]), **todo[n])
                n += 1
        if place in also:
            pl.step(place[0], mid=bool(place[1]), **also[place])
        if pl.steps[-1]["place"] != (place[0], bool(place[1])):
            pl.step(place[0], mid=bool(place[1]), kind="nop")


def make_plan():
    pl = Plan()
    step, beats = pl.step, pl.beats
    b0 = {}
    for name, c0, n in PANELS1:
        b0[name] = pl.panel(name, "A", [("w_in", 512 * i, c0, n) for i in range(2)], base=[0, 4], n=n)

    def turns(name, to, nb, last=True):
        for j in range(NT):
            b = b0[name] + 4 + j
            step(b + 1, mid=True, kind="tr", to=to, j=j, nb=nb, beat=b)
            if j < NT - 1 or last:
                step(b + 1, kind="nop")

    def nop(b, mid=True):
        step(b, mid=mid, kind="nop")

    turns("N1", "n1", 4)
    nop(b0["N2"] + 1)
    turns("N2", "n2", 2, last=False)
    nop(b0["NQ"], 0)
    nop(b0["NQ"] + 1)
    step(b0["NQ"] + 1, kind="gp", c=0)
    step(b0["NQ"] + 2, mid=True, kind="gp", c=1)
    nop(b0["NQ"] + 2, 0)
    pl.cmv = step(b0["NQ"] + 3, mid=True, kind="cmv")
    step(b0["NQ"] + 4, mid=True, kind="hid")
    step(b0["NQ"] + 4, kind="kct")
    turns("NQ", "nq", 4, last=False)
    step(b0["RQ"], kind="gates")
    nop(b0["RQ"] + 1)
    todo = [dict(kind="cmp", j=t) for t in range(NT)]
    for br in range(2):
        todo += [dict(kind="sm", fam="nsa", br=br, segs=s) for s in segments()]
    also = {}
    for name in ("RQ", "RK"):
        for j in range(NT):
            b = b0[name] + 4 + j
            also[b + 1, 1] = dict(kind="tr", to=name.lower(), j=j, nb=4, beat=b)
    spread(pl, todo, b0["RQ"] + 1, 0, b0["NG"] + 2, 0, also)
    nop(b0["NG"] + 3)
    nop(b0["NG"] + 3, 0)
    ng, rg = b0["NG"] + 4, b0["RG"]
    for i in range(NT):
        step(ng + i, mid=True, kind="ret", j=i // 2, half=i % 2)
        step(ng + i, kind="trh", src="att", j=i, kt=12, beat=ng + i, flip=0)
    nth = NT
    for i, mid, kinds in ((0, 1, ("ret",)), (0, 0, (0,)), (1, 1, ("ret",)), (1, 0, ("ret", 1)), (2, 1, ("ret",)),
                          (2, 0, (2,)), (3, 1, ("nop", "nop")), (3, 0, (3,)), (4, 1, ("nop",))):
        for kind in kinds:
            if kind == "ret":
                step(rg + i, mid=bool(mid), kind="ret", j=nth // 2, half=nth % 2)
                nth += 1
            elif kind == "nop":
                nop(rg + i, mid)
            else:
                step(rg + i, mid=bool(mid), kind="gn", j=kind)
    wo = [pl.panel("WO", "A", [("w_out", 512 * i, 512 * c, 512) for i in (1, 0)], base=[12, 8], c=c)
          for c in range(2)]
    for j in range(NT):
        step(wo[0] + j, kind="trh", src="ret", j=j, kt=8, beat=b0["RG"] + 4 + j)
        nop(wo[0] + j + 1)
    nop(wo[0] + 4, 0)
    for j in range(2):
        step(wo[0] + 5 + j, mid=True, kind="mnorm", j=j)
        nop(wo[0] + 5 + j, 0)
    for i in range(2):
        for half in range(2):
            step(wo[0] + 8 + i, mid=half == 0, kind="trh", src="mem", j=i, half=half, kt=4 * half)
    nop(wo[0] + 10)
    nop(wo[0] + 10, 0)
    mk = pl.panel("MK", "A", [("w_mem", 512 * i, 0, 512) for i in range(2)], tiles=2, base=[0, 4])
    mv = pl.panel("MV", "A", [("w_mem", 512 * i, 512, 512) for i in range(2)], tiles=2, base=[0, 4])
    w4 = wo[1] + 4

    def j1(j):
        return dict(kind="j1", j=j, beat=w4 + j)

    def j2(j):
        return dict(kind="j2", j=j, which=0)

    def th(j, half):
        return dict(kind="trh", src="x", j=j, half=half, kt=8 + 4 * half)

    def qn(j):
        return dict(kind="qn", src="MK", j=j, nh=MH, beat=mk + 2 + j)

    def tr(j):
        return dict(kind="tr", to="mk", j=j, nb=4, beat=mk + 2 + j)

    idle = dict(kind="nop")
    at, mid = w4, False
    for s in (j1(0), idle, j1(1), j2(0), j1(2), j2(1), j1(3), th(0, 0), th(0, 1), j2(2), th(1, 0), th(1, 1), j2(3),
              th(2, 0), th(2, 1), th(3, 0), th(3, 1), qn(0), tr(0), qn(1), tr(1), idle, idle):
        step(at, mid=mid, **s)
        at, mid = (at, False) if mid else (at + 1, True)
    assert at <= mv + 4
    e0 = {}
    for name, form, c0 in PANELS2:
        e0[name] = pl.panel(name, form, [("w_in_2", 512 * i, c0, 512) for i in range(2)], base=[8, 12])
    for name in ("Q", "K", "QM"):
        for j in range(NT):
            b = e0[name] + 4 + j
            step(b, kind="qn", src=name, j=j, nh=MH if name == "QM" else H, beat=b)
            step(b + 1, mid=True, kind="tr", to=name, j=j, nb=4, beat=b)
        nop(b + 1, 0)
        nop(b + 2)
    branches = [("conv", 0, 0), ("mem", 2, 4), ("moba", 1, 0)]
    g0 = {}
    for i, (name, gi, base) in enumerate(branches):
        for c in range(2):
            col = GATE0 + D * gi + 512 * c
            g0[name, c] = pl.panel("G", "B", [("w_in_2", 512 * q, col, 512) for q in range(2)],
                                   base=[8, 12], gi=gi, c=c)
            pl.panel("B", "B", [("w_br_" + name, 0, 512 * c, 512)], base=[base], i=i, c=c)
    todo = []
    for t in range(NT):
        todo += [dict(kind="sm", fam="mem", segs=[(2 * a, t, 0), (2 * a + 1, t, MEM)]) for a in range(2)]
        todo += [dict(kind="nop"), dict(kind="trh", src="ymem", j=t, kt=4)]
    todo += [dict(kind="sm", fam="moba", segs=s) for s in segments()]
    todo += [dict(kind="nop")] * 3
    at = g0["conv", 0] + 6
    spread(pl, todo, e0["CC"] + 1, 0, at, 0)
    todo = [dict(kind="trh", src="ymoba", j=t, kt=0) for t in range(NT)] + [dict(kind="nop")] * 2
    assert at < g0["conv", 0] + 8
    at = g0["mem", 0]
    while todo:
        step(at, **todo.pop(0))
        at += 1
    w2 = [pl.panel("WY", "A", [("w_o", 512 * i, 512 * c, 512) for i in range(2)], base=[4, 8], c=c)
          for c in range(2)]
    w4 = w2[1] + 4

    def th2(j):
        return [dict(kind="trh", src="x2", j=j, half=half, kt=(12, 0)[half]) for half in range(2)]

    def n2(j):
        return [dict(kind="j2", j=j, which=1, beat=w4 + j)]

    for at, mid, todo in ((0, 0, n2(0)), (1, 0, n2(1)), (2, 0, th2(0)[:1] + n2(2)),
                          (3, 0, n2(3) + th2(0)[1:] + th2(1) + th2(2) + th2(3) + [idle] * 2)):
        for s in todo:
            step(w4 + at, mid=bool(mid), **s)
    def up(g):
        act, ch, n = (4, 8)[g % 2], sum(FFN_GROUPS[:g]), FFN_GROUPS[g] * P
        if FFN_GROUPS[g] == 4:
            for name, c0 in (("UA", 0), ("UB", DFF)):
                pl.panel(name, "B", [("w_up", 512 * i, c0 + ch * P, n) for i in range(2)], base=[12, 0], ch=ch,
                         act=act)
        else:
            f = pl.panel("UX", "B", [("w_up2", 512 * i, ch * P, n) for i in range(2)], base=[12, 0], ch=ch,
                         act=act, packed=True)
            for b in beats[f:]:
                b["name"] = "UA" if b["j"] < 2 else "UB"

    def down(g):
        act, ch = (4, 8)[g % 2], sum(FFN_GROUPS[:g]) * P
        if FFN_GROUPS[g] == 4:
            for c in range(2):
                pl.panel("DN", "A", [("w_down", ch, 512 * c, 512)], base=[act], c=c, final=False)
        else:
            pl.units.append(("w_down2", ch, 0, 0))
            for c in range(2):
                for j in range(NT):
                    beats.append(dict(name="DN", form="A", u=len(pl.units) - 1, j=j, n=512, first=True, last=True,
                                      kts=[(act + q, 2 * q + c) for q in range(2)], steps=[], mid=[], bank=j,
                                      unit_first=c == 0 and j == 0, c=c, final=True))

    up(0)
    for g in range(1, len(FFN_GROUPS)):
        up(g)
        down(g - 1)
    down(len(FFN_GROUPS) - 1)
    for i, b in enumerate(beats):
        b["b"] = i
    return finish_plan(pl)


def has(s, phase):
    kind = s["kind"]
    return phase in {
        "nop": (), "tr": ("turn", "take"), "gp": ("turn", "take"), "trh": ("turn", "take"), "cmv": ("rows",),
        "hid": ("scores", "probs", "turn", "take"), "kct": ("turn", "take"), "gates": ("probs",),
        "cmp": ("scores", "rows", "probs", "turn", "take", "values", "out"),
        "sm": ("scores", "rows", "probs", "turn", "take", "values", "out"),
        "ret": ("scores", "rows", "turn", "take", "values", "out") if s.get("j") != 3 else
        ("scores", "rows", "values", "out"),
        "gn": ("rows", "probs", "norm"), "mnorm": ("probs", "norm"), "j1": ("probs", "norm"), "j2": ("probs", "norm"),
        "qn": ("rows", "probs", "norm"),
    }[kind]


def finish_plan(pl):
    pl.count = {}
    for phase in ("scores", "rows", "probs", "norm", "turn", "values", "out"):
        n, at = 0, []
        for s in pl.steps:
            n += has(s, phase)
            at.append(n)
        pl.count[phase] = at
    for who in ("act", "dve"):
        n, at = 0, []
        for s in pl.steps:
            n += has(s, "take") and (s["kind"] == "sm") == (who == "act")
            at.append(n)
        pl.count["take_" + who] = at
    n, at = 0, []
    for s in pl.steps:
        n += s["kind"] == "trh"
        at.append(n)
    pl.count["high"] = at
    na = nd = 0
    for b in pl.beats:
        b["evac"] = None
        if b["last"]:
            b["evac"] = "act" if b["name"] in ("CC", "G", "WO", "MK", "MV", "Q", "K", "V", "QM") else "dve"
            if b["evac"] == "act":
                na += 1
                b["evac_n"] = na
            else:
                nd += 1
                b["evac_n"] = nd
    pl.unit_end = {}
    for b in pl.beats:
        pl.unit_end[b["u"]] = b["b"]
    last = {}
    for b in pl.beats:
        if b["first"]:
            b["bank_prev"] = last.get(b["bank"])
        if b["last"]:
            last[b["bank"]] = b["b"]
    for s in pl.steps:
        s["in_beat"] = next(b["b"] for b in pl.beats if s["k"] in b["steps"] + b["mid"])
        s["mid"] = s["k"] in pl.beats[s["in_beat"]]["mid"]
    for i, s in enumerate(s for s in pl.steps if s["kind"] == "ret"):
        s["nth"] = i
    n = 0
    prev = {}
    pl.src_of_beat = {}
    pl.src_mem = {}
    uses = [s for s in pl.steps if (s["kind"] == "tr" and s["to"] != "rk") or s["kind"] == "trh" and s["src"] == "ymem"]
    uses.sort(key=lambda s: s["k"])
    for s in uses:
        s["slot"] = n % 2
        s["slot_prev"] = prev.get(n % 2)
        prev[n % 2] = s["k"]
        if s["kind"] == "tr":
            pl.src_of_beat[s["beat"]] = s
        else:
            pl.src_mem[s["j"]] = s
        n += 1
    for i, s in enumerate(s for s in pl.steps if s["kind"] in ("mnorm", "j1", "j2")):
        s["norm"] = i
    for s in pl.steps:
        if s["kind"] == "qn":
            s["slot"] = pl.src_of_beat[s["beat"]]["slot"]
    return pl


def kib(arena, a, n):
    return arena[:, a * 256:(a + n) * 256]


def build(nc, t_in, out):
    pl = make_plan()
    beats, steps, units, count = pl.beats, pl.steps, pl.units, pl.count
    NU = len(units)
    with ExitStack() as ctx:
        def sb(name, shape, dt=F32):
            return ctx.enter_context(nc.sbuf_tensor(name, shape, dt))

        def ps(name):
            return ctx.enter_context(nc.psum_tensor(name, [P, 512], F32))

        def sem(name):
            return ctx.enter_context(nc.semaphore(name))

        raw = sb("raw", [P, 2, 2048])
        w_hi = sb("w_hi", [P, 2, 4, 512], F32R)
        w_lo = sb("w_lo", [P, 2, 4, 512], F32R)
        a_hi = sb("a_hi", [P, 16, S], F32R)
        a_lo = sb("a_lo", [P, 16, S], F32R)
        arena = sb("arena", [P, 84 * 256])
        cst = sb("cst", [P, CST])
        idb = sb("idb", [P, P], BF16)
        maskb = sb("maskb", [P, P], BF16)
        rope_c = sb("rope_c", [P, 5, NF])
        rope_s = sb("rope_s", [P, 5, NF])
        gp = sb("gp", [P, D])
        cols = sb("cols", [P, sum(n for _, n in COLS)])
        w2s = sb("w2s", [P, 2, 2, DH])
        small = sb("small", [P, 160])
        posi = sb("posi", [P, 5], I32)
        ident = cst[:, C_ID:C_ID + P]
        tri = cst[:, C_TRI:C_TRI + P]
        cmpb = cst[:, C_CMPB:C_CMPB + NT * 32].rearrange("p (t n) -> p t n", t=NT)

        def view(start, size, pat=None, **kw):
            v = kib(arena, start, size)
            return v.rearrange(pat, **kw) if pat else v

        ada_t = view(0, 48, "p (s m k) -> p s m k", s=6, m=2)
        x0 = view(64, 16, "p (t d) -> p t d", t=NT)
        stage = view(64, 8, "p (s b n) -> p s b n", s=4, b=4)
        crow = view(56, 4)
        gate = view(60, 4, "p (k m) -> p k m", k=KT)
        tmp = view(80, 4, "p (s n) -> p s n", s=2)
        ncT = view(0, 8, "p (b n) -> p b n", b=4)
        nqT = view(8, 8, "p (b n) -> p b n", b=4)
        w1 = view(16, 32, "p (v m n) -> p v m n", v=2, m=16)
        cblk = view(48, 8, "p (v g n) -> p v g n", v=2, g=2)
        cmv = view(56, 8, "p (v m g n) -> p v m g n", v=2, m=16, g=2)
        kvT = view(68, 4, "p (v n) -> p v n", v=2)
        rqT = view(16, 8, "p (b n) -> p b n", b=4)
        rkT = view(24, 8, "p (b n) -> p b n", b=4)
        rk = view(32, 8, "p (t n) -> p t n", t=NT)
        rv = view(40, 8, "p (t n) -> p t n", t=NT)
        att = view(48, 8, "p (t n) -> p t n", t=NT)
        prob = view(56, 4, "p (s n) -> p s n", s=2)
        probT = view(60, 4, "p (s n) -> p s n", s=2)
        pret = view(56, 8, "p (s n) -> p s n", s=4)
        src = view(64, 4, "p (s n) -> p s n", s=2)
        Rst = view(68, 2, "p (s c e) -> p s c e", s=2, c=4)
        vsel = view(72, 2, "p (t n) -> p t n", t=NT)
        vwin = view(74, 2, "p (t n) -> p t n", t=NT)
        vbd = view(76, 2, "p (g r n) -> p g r n", g=2, r=4)
        kcT = arena[:, 78 * 256:78 * 256 + 128].rearrange("p (g e n) -> p g e n", g=2, e=2)
        kcr = arena[:, 78 * 256 + 128:78 * 256 + 256]
        sg = view(0, 8, "p (t n) -> p t n", t=NT)
        yo = view(16, 16, "p (t d) -> p t d", t=NT)
        x1 = view(0, 16, "p (t d) -> p t d", t=NT)
        memr = view(40, 8, "p (t d) -> p t d", t=2)
        xn = [view(a, 4) for a in (56, 60, 64, 72)]
        dump = view(68, 4)
        g_mem_row = view(76, 4)
        g_row = view(52, 4)
        kmT = view(72, 4, "p (h n) -> p h n", h=MH)
        vm = view(48, 4, "p (t n) -> p t n", t=2)
        qT = view(16, 8, "p (b n) -> p b n", b=4)
        kT = view(24, 8, "p (b n) -> p b n", b=4)
        vmo = view(32, 8, "p (t n) -> p t n", t=NT)
        qmT = view(40, 8, "p (b n) -> p b n", b=4)
        ymo = view(0, 8, "p (t n) -> p t n", t=NT)
        ucv = view(8, 8, "p (t n) -> p t n", t=NT)
        tg = view(8, 8, "p (t n) -> p t n", t=NT)
        merged = view(16, 16, "p (t n) -> p t n", t=8)
        x2 = view(32, 16, "p (t d) -> p t d", t=NT)
        fcv = view(8, 8, "p (t n) -> p t n", t=NT)
        fsi = view(0, 8, "p (t n) -> p t n", t=NT)

        x1_dram = nc.dram_tensor("x1_scratch", [S, D], F32).ap()

        CI = {}
        at = 0
        for name, n in COLS:
            CI[name] = cols[:, at:at + n]
            at += n
        cpe = CI["cpe"].rearrange("p (v m) -> p v m", v=2)
        ffw = CI["ffw"].rearrange("p (w k) -> p w k", w=4)
        glog = sb("glog", [P, NT, 24])
        nmax = sb("nmax", [P, 4, 2])
        rsum = sb("rsum", [P, 4, 2])
        st8 = small[:, 0:8]
        rs8 = small[:, 8:16]
        rs8_odd = small[:, 112:120]
        cf8 = small[:, 16:24]
        gvar = small[:, 24:56].rearrange("p (t n) -> p t n", t=NT)
        ri = small[:, 56:58]
        cf = small[:, 58:60]
        ss = small[:, 60:64]
        sd = small[:, 64:68]
        rr = small[:, 68:72]
        norm = small[:, 128:142]
        qss = small[:, 72:88].rearrange("p (s n) -> p s n", s=2)
        qsd = small[:, 88:104].rearrange("p (s n) -> p s n", s=2)
        qri = small[:, 104:112]

        pj = [ps(f"pj{i}") for i in range(4)]
        sc = [ps(f"sc{i}") for i in range(2)]
        pt = ps("pt")
        po = ps("po")

        consts_in = sem("consts_in")
        params_in = sem("params_in")
        x_in = sem("x_in")
        ada_chunk = [0, 1, 4, 5, 2, 3, 6, 7, 8, 9, 10, 11]
        ada_slot = [0, 1, 2, 3, 0, 1, 2, 3, 4, 5, 3, 1]
        ada_in = [sem(f"ada_in{i}") for i in range(6)]
        ada_used = sem("ada_used")
        crow_in = sem("crow_in")
        grow_in = sem("grow_in")
        gmem_in = sem("gmem_in")
        high_taken = sem("high_taken")
        mem_in = sem("mem_in")
        xres_in = sem("xres_in")
        w1_in = sem("w1_in")
        gather_in = sem("gather_in")
        x1_saved = sem("x1_saved")
        x1_back = sem("x1_back")
        out_saved = sem("out_saved")
        raw_in = [sem(f"raw_in{i}") for i in range(2)]
        hi_ready = sem("hi_ready")
        lo_ready = sem("lo_ready")
        beat_done = sem("beat_done")
        scores_ready = sem("scores_ready")
        turned = sem("turned")
        values_ready = sem("values_ready")
        rows_ready = sem("rows_ready")
        probs_ready = sem("probs_ready")
        taken_act = sem("taken_act")
        taken_dve = sem("taken_dve")
        normed = sem("normed")
        out_taken = sem("out_taken")
        evac_act = sem("evac_act")
        evac_dve = sem("evac_dve")
        ready_dve = sem("ready_dve")
        ready_act = sem("ready_act")
        ready_pe = sem("ready_pe")
        pair_act = sem("pair_act")
        chain_dve = sem("chain_dve")
        chain_act = sem("chain_act")

        pair_n = {}
        n = 0
        for b in beats:
            if b["last"] and b["name"] in ("NG", "RG", "UA"):
                n += 1
                pair_n[b["b"]] = n

        def wait_beat(eng, b):
            eng.wait_ge(beat_done, b + 1)

        def wait_evac(eng, b):
            if beats[b]["evac"] == "act":
                eng.wait_ge(evac_act, beats[b]["evac_n"])
            else:
                eng.wait_ge(evac_dve, beats[b]["evac_n"])

        def wait_taken(eng, k):
            if has(steps[k], "norm"):
                eng.wait_ge(normed, count["norm"][k])
            elif steps[k]["kind"] == "sm":
                eng.wait_ge(taken_act, count["take_act"][k])
            else:
                eng.wait_ge(taken_dve, count["take_dve"][k])

        def in_pt(s):
            return has(s, "turn") and (s["kind"] != "trh" or s["src"] in ("ymem", "ymoba"))

        def turn_bank(s):
            return pt if in_pt(s) else sc[score_bank(s)]

        def score_bank(s):
            return (s["k"] + s.get("flip", s["kind"] == "trh")) % 2

        def wait_probs_slot(eng, k):
            if k >= 2 and steps[k - 2]["kind"] in ("sm", "cmp", "hid"):
                eng.wait_ge(turned, count["turn"][k - 2])

        def wait_region(eng, kt, upto):
            for b in reversed(beats[:upto + 1]):
                if any(a == kt for a, _ in b["kts"]):
                    wait_beat(eng, b["b"])
                    return

        writers = {}
        for s in steps:
            if s["kind"] == "trh":
                for q in range(4):
                    writers.setdefault(s["kt"] + q, []).append((s["in_beat"], "step", s["k"], s["j"]))
        for b in beats:
            if b["last"]:
                if b["name"] == "CB":
                    b["act_kt"] = 0 + b["j"]
                elif b["name"] == "B" and b["i"] == 2:
                    b["act_kt"] = (4 if b["c"] == 0 else 8) + b["j"]
                elif b["name"] == "UB":
                    b["act_kt"] = b["act"] + b["j"] - (2 if b.get("packed") else 0)
                else:
                    continue
                writers.setdefault(b["act_kt"], []).append((b["b"], "beat", b["b"], b["j"]))
        waited = {}

        def wait_activations(pe, b):
            if b["b"] < 2 * NT:
                pe.wait_ge(h_taken, b["b"] + 1)
            for kind in ("step", "beat"):
                found = [w[2] for a, _ in b["kts"] for w in writers.get(a, []) if w[0] < b["b"] and w[1] == kind and
                         (kind == "beat" or b["form"] == "B" or w[3] == b["j"])]
                if found and max(found) > waited.get(kind, -1):
                    waited[kind] = max(found)
                    if kind == "step":
                        wait_taken(pe, max(found))
                    else:
                        wait_evac(pe, max(found))

        DVE_TAB, DVE_RMS, DVE_X = 1, 2, 3
        eps_ready = sem("eps_ready")
        h_taken = sem("h_taken")
        stage_ready = sem("stage_ready")
        stage_high = sem("stage_high")
        xbank = [*pj, *sc, pt, po]

        with nc.Block() as block:

            @block.sync
            def _(sp):
                n = 0

                which = consts_in

                def load(dst, s):
                    nonlocal n
                    n += 16
                    sp.dma_start(dst, s).then_inc(which, 16)

                load(cst[:], t_in["cst"])
                load(posi[:, 0:4], t_in["positions"].rearrange("a (t p) -> p (a t)", p=P))
                load(cols[:, 0:N_COLS], t_in["cols"])
                for g in range(2):
                    load(posi[32 * g:32 * g + NCMP, 4:5],
                         t_in["positions"][0, 31:512].rearrange("(n s) -> n s", s=1)[0:481:16])
                sp.dma_start(crow, t_in["c"].broadcast_to([P, D])).then_inc(crow_in, 16)
                sp.dma_start(x0, t_in["x"].rearrange("a (t p) d -> p (a t) d", p=P)).then_inc(x_in, 16)
                ada = t_in["ada_t"].rearrange("(c m p) k -> p c m k", m=2, p=P)
                def load_ada(i):
                    sp.dma_start(ada_t[:, ada_slot[i]], ada[:, ada_chunk[i]]).then_inc(ada_in[ada_slot[i]], 16)

                for i in range(8):
                    if i >= 4:
                        sp.wait_ge(ada_used, i - 3)
                    if i == 3:
                        sp.dma_start(raw[:, 0], t_in["weights"][0]).then_inc(raw_in[0], 16)
                    if i == 7:
                        sp.dma_start(raw[:, 1], t_in["weights"][1]).then_inc(raw_in[1], 16)
                    load_ada(i)
                for i in range(8, 12):
                    if i == 10:
                        sp.wait_ge(lo_ready, 2)
                        sp.dma_start(raw[:, 0], t_in["weights"][2]).then_inc(raw_in[0], 16)
                        sp.wait_ge(ada_used, 8)
                    load_ada(i)
                assert n == 16 * N_CONST
                which = params_in
                for v, kv in enumerate("kv"):
                    load(w2s[:, v], t_in["cmp_w2_" + kv].rearrange("a (m p) n -> p (a m) n", p=P))
                assert n == 16 * (N_CONST + N_PARAM)
                wst = t_in["weights"]
                sp.wait_ge(lo_ready, 4)
                sp.dma_start(raw[:, 1], wst[3]).then_inc(raw_in[1], 16)
                with sp.Fori(2, NU // 2) as i:
                    for s in range(2):
                        sp.wait_ge(lo_ready, i * 4 - 2 + 2 * s)
                        sp.dma_start(raw[:, s], wst[bass.ds(i * 2 + s, 1)].rearrange("a p n -> p (a n)")).then_inc(
                            raw_in[s], 16)
                if NU % 2:
                    sp.wait_ge(lo_ready, 2 * NU - 4)
                    sp.dma_start(raw[:, 0], wst[NU - 1]).then_inc(raw_in[0], 16)
                for j in range(NT):
                    b = [b for b in beats if b["name"] == "DN" and b["final"] and b["c"] == 1 and b["j"] == j][0]
                    wait_evac(sp, b["b"])
                    sp.dma_start(out.rearrange("a (t p) d -> p (a t) d", p=P)[:, j], x2[:, j]).then_inc(out_saved, 16)
                sp.wait_ge(out_saved, 16 * NT)

            @block.gpsimd
            def _(pool):
                def low(s, n):
                    for half in range(2):
                        pool.wait_ge(hi_ready, n + half - 1)
                        z = slice(2 * half, 2 * half + 2)
                        nc.gpsimd.tensor_tensor(w_lo[:, s, z].rearrange("p k n -> p (k n)"),
                                                raw[:, s, 1024 * half:1024 * half + 1024],
                                                w_hi[:, s, z].rearrange("p k n -> p (k n)").bitcast(F32),
                                                ALU.subtract).then_inc(lo_ready, 1)

                def h_low(n):
                    half, j = divmod(n, NT)
                    pool.wait_ge(stage_high, n + 1)
                    kt, q = slice(4 * half, 4 * half + 4), slice(P * j, P * j + P)
                    nc.gpsimd.tensor_tensor(a_lo[:, kt, q], stage[:, n % 4], a_hi[:, kt, q].bitcast(F32),
                                            ALU.subtract).then_inc(h_taken, 1)

                low(0, 2)
                for n in range(NT):
                    h_low(n)
                low(1, 4)
                for n in range(NT, 2 * NT):
                    h_low(n)
                with pool.Fori(1, NU // 2) as i:
                    for s in range(2):
                        low(s, i * 4 + 2 + 2 * s)
                if NU % 2:
                    low(0, 2 * NU)

            @block.tensor
            def _(pe):
                for n in range(2 * NT):
                    half, j = divmod(n, NT)
                    pe.wait_ge(ready_act, j + 3)
                    for q in range(4):
                        mm = pe.transpose(xbank[n][:, P * q:P * q + P],
                                          x0[:, j, 512 * half + P * q:512 * half + P * q + P], ident)
                    mm.then_inc(ready_pe, 1)

                def projection(b):
                    if b["unit_first"]:
                        pe.wait_ge(lo_ready, 2 * b["u"] + 1)
                    if b["first"]:
                        if b["bank_prev"] is not None:
                            if beats[b["bank_prev"]]["name"] in ("NG", "RG"):
                                pe.wait_ge(pair_act, pair_n[b["bank_prev"]])
                            else:
                                wait_evac(pe, b["bank_prev"])
                    wait_activations(pe, b)
                    s = b["u"] % 2
                    n = b["n"]
                    dst = pj[b["bank"]][:, 0:n] if b["form"] == "A" else pj[b["bank"]][:]
                    last = len(b["kts"]) - 1
                    for i, (a, q) in enumerate(b["kts"]):
                        if i == (last + 1) // 2:
                            for k in b["mid"]:
                                step(k)
                        if b["unit_first"] and q == 2:
                            pe.wait_ge(lo_ready, 2 * b["u"] + 2)
                        if b["form"] == "A":
                            st = (a_hi[:, a, P * b["j"]:P * b["j"] + P], a_lo[:, a, P * b["j"]:P * b["j"] + P])
                            mv = (w_hi[:, s, q, 0:n], w_lo[:, s, q, 0:n])
                        else:
                            st = (w_hi[:, s, q, P * b["j"]:P * b["j"] + P], w_lo[:, s, q, P * b["j"]:P * b["j"] + P])
                            mv = (a_hi[:, a], a_lo[:, a])
                        for z, (x, y) in enumerate(((0, 0), (0, 1), (1, 0))):
                            mm = pe.matmul(dst, st[x], mv[y], start=b["first"] and i == 0 and z == 0,
                                           stop=b["last"] and i == last and z == 2)
                    mm.then_inc(beat_done, 1)

                bank_user = {}

                def wait_score_bank(k):
                    n = score_bank(steps[k])
                    p = bank_user.get(n)
                    if p is not None:
                        if steps[p]["kind"] == "trh":
                            wait_taken(pe, p)
                        elif has(steps[p], "probs"):
                            pe.wait_ge(probs_ready, count["probs"][p])
                        else:
                            pe.wait_ge(rows_ready, count["rows"][p])
                    else:
                        pe.wait_ge(h_taken, 2 * NT)
                    bank_user[n] = k

                def heads(s, h):
                    if s["fam"] == "mem":
                        return (slice(0, P), qmT[:, h], kmT[:, h], vm[:, :, MDH * h:MDH * h + MDH])
                    p = slice(DH * (h % 2), DH * (h % 2) + DH)
                    if s["fam"] == "moba":
                        return p, qT[:, h // 2], kT[:, h // 2], vmo[:, :, DH * h:DH * h + DH]
                    g = h // 4
                    v = (vsel, vwin)[s["br"]]
                    return p, nqT[:, h // 2], ncT[:, 2 * s["br"] + g], v[:, :, DH * g:DH * g + DH]

                def ready_inputs(k):
                    s = steps[k]
                    to = {"nsa": "nq", "mem": "QM", "moba": "QM"}.get(s.get("fam")) or {"cmp": "nq", "ret": "rk"}[
                        s["kind"]]
                    wait_taken(pe, max(p for p in range(k) if steps[p].get("to") == to))
                    names = {"sm": {"nsa": "NQ", "moba": "V", "mem": "MV"}.get(s.get("fam")), "ret": "RV",
                             "cmp": "NQ"}.get(s["kind"])
                    bb = [b for b in beats if b["name"] == names and b["last"]][-1]
                    wait_evac(pe, bb["b"])

                def scores(k):
                    s = steps[k]
                    if not has(s, "scores"):
                        return
                    wait_score_bank(k)
                    dst = sc[k % 2]
                    if s["kind"] == "hid":
                        pe.wait_ge(rows_ready, count["rows"][pl.cmv])
                        pe.wait_ge(w1_in, 32)
                        for v in range(2):
                            for m in range(2):
                                o = (2 * v + m) * 64
                                for q in range(16):
                                    mm = pe.matmul(dst[:, o:o + 64], w1[:, v, q, P * m:P * m + P],
                                                   cmv[:, v, q].rearrange("p g n -> p (g n)"),
                                                   start=q == 0, stop=q == 15)
                    elif s["kind"] == "cmp":
                        ready_inputs(k)
                        for c in range(H // 2):
                            mm = pe.matmul(dst[:, 64 * c:64 * c + 64], nqT[:, c, P * s["j"]:P * s["j"] + P],
                                           kcT[:, c // 2].rearrange("p e n -> p (e n)"), start=True, stop=True)
                    elif s["kind"] == "ret":
                        ready_inputs(k)
                        p = slice(DH * s["half"], DH * s["half"] + DH)
                        q = slice(P * s["j"], P * s["j"] + P)
                        for c in range(4):
                            mm = pe.matmul(dst[:, P * c:P * c + P], rkT[p, c, q], rqT[p, c, q], start=True,
                                           stop=True)
                    else:
                        ready_inputs(k)
                        for h, t, o in s["segs"]:
                            p, q, kk, _ = heads(s, h)
                            n = MEM if s["fam"] == "mem" else P * (t + 1)
                            mm = pe.matmul(dst[:, o:o + n], q[p, P * t:P * t + P], kk[p, 0:n], start=True,
                                           stop=s["fam"] == "mem")
                            if s["fam"] != "mem":
                                mm = pe.matmul(dst[:, o + n - P:o + n], idb[:], maskb[:], start=False, stop=True)
                    mm.then_inc(scores_ready, 1)

                def turn(k):
                    s = steps[k]
                    if not has(s, "turn"):
                        return
                    kind = s["kind"]
                    if not in_pt(s):
                        wait_score_bank(k)
                    else:
                        for p in range(k - 1, -1, -1):
                            if in_pt(steps[p]):
                                wait_taken(pe, p)
                                break
                    if kind == "gp":
                        pe.wait_ge(ready_dve, DVE_X)
                        for q in range(4):
                            mm = pe.matmul(pt[:, P * q:P * q + P], gate[:, 4 * s["c"] + q], ident, start=True,
                                           stop=True)
                    elif kind == "tr":
                        for p in range(k - 1, k - 4, -1):
                            if steps[p]["kind"] == "qn" and steps[p]["beat"] == s["beat"]:
                                wait_taken(pe, p)
                        wait_evac(pe, s["beat"])
                        t = rk[:, s["j"]] if s["to"] == "rk" else src[:, s["slot"]]
                        for q in range(s["nb"]):
                            mm = pe.transpose(pt[:, P * q:P * q + P], t[:, P * q:P * q + P], ident)
                    elif kind == "trh":
                        t = {"att": lambda: att[:, s["j"]], "ret": lambda: rk[:, s["j"]],
                             "mem": lambda: memr[:, s["j"], 512 * s["half"]:],
                             "x": lambda: xn[s["j"] % 2][:, 512 * s["half"]:],
                             "x2": lambda: xn[s["j"]][:, 512 * s["half"]:],
                             "ymem": lambda: src[:, s["slot"]], "ymoba": lambda: ymo[:, s["j"]]}[s["src"]]()
                        if s["src"] in ("att", "ret"):
                            wait_evac(pe, s["beat"])
                        elif s["src"] in ("mem", "x", "x2"):
                            p = max(p for p in range(k) if steps[p]["kind"] in ("mnorm", "j2") and
                                    steps[p]["j"] == s["j"])
                            wait_taken(pe, p)
                        else:
                            p = max(p for p in range(k) if steps[p]["kind"] == "sm")
                            pe.wait_ge(out_taken, count["out"][p])
                        for q in range(4):
                            mm = pe.transpose(turn_bank(s)[:, P * q:P * q + P], t[:, P * q:P * q + P], ident)
                    elif kind == "hid":
                        pe.wait_ge(probs_ready, count["probs"][k])
                        pe.wait_ge(params_in, 16 * N_PARAM)
                        hk = probT[:, k % 2].rearrange("p (m n) -> p m n", m=8)
                        hv = prob[:, k % 2].rearrange("p (m g n) -> p m g n", m=2, g=2)
                        for m in range(2):
                            pe.matmul(pt[0:64, 0:DH], hk[:, m], w2s[:, 0, m], start=m == 0, stop=m == 1)
                        for g in range(2):
                            for m in range(2):
                                mm = pe.matmul(pt[:, 64 + DH * g:64 + DH * g + DH], hv[:, m, g], w2s[:, 1, m],
                                               start=m == 0, stop=m == 1)
                    elif kind == "kct":
                        wait_taken(pe, k - 1)
                        mm = pe.transpose(pt[:, 0:64], kcr[0:64, :], ident[0:64, 0:64])
                    elif kind == "cmp":
                        pe.wait_ge(probs_ready, count["probs"][k])
                        for g in range(2):
                            mm = pe.transpose(pt[:, P * g:P * g + P], prob[:, k % 2, P * g:P * g + P], ident)
                    elif kind == "ret":
                        e = DH * s["half"]
                        for c in range(4):
                            z = slice(P * c + e, P * c + e + DH)
                            mm = pe.matmul(pt[e:e + DH, DH * c:DH * c + DH], rk[:, s["j"], z], rv[:, s["j"], z],
                                           start=True, stop=True)
                    else:
                        pe.wait_ge(probs_ready, count["probs"][k])
                        b = 0
                        for h, t, o in s["segs"]:
                            for jb in range(2 if s["fam"] == "mem" else t + 1):
                                mm = pe.transpose(pt[:, P * b:P * b + P],
                                                  prob[:, k % 2, o + P * jb:o + P * jb + P], ident)
                                b += 1
                    mm.then_inc(turned, 1)

                def values(k):
                    s = steps[k]
                    if not has(s, "values"):
                        return
                    for p in range(k - 1, -1, -1):
                        if has(steps[p], "out"):
                            pe.wait_ge(out_taken, count["out"][p])
                            break
                    else:
                        pe.wait_ge(h_taken, 2 * NT)
                    if s["kind"] == "ret":
                        pe.wait_ge(rows_ready, count["rows"][k])
                        if s["j"]:
                            wait_taken(pe, max(p for p in range(k) if steps[p]["kind"] == "ret" and
                                               steps[p]["half"] == s["half"]))
                        e = DH * s["half"]
                        for c in range(4):
                            d = po[:, DH * c:DH * c + DH]
                            if s["j"]:
                                pe.matmul(d, rqT[e:e + DH, c, P * s["j"]:P * s["j"] + P],
                                          Rst[e:e + DH, s["j"] % 2, c], start=True, stop=False)
                            mm = pe.matmul(d, pret[:, s["nth"] % 4, P * c:P * c + P],
                                           rv[:, s["j"], P * c + e:P * c + e + DH], start=s["j"] == 0, stop=True)
                    elif s["kind"] == "cmp":
                        wait_taken(pe, k)
                        for g in range(2):
                            mm = pe.matmul(po[:, 256 * g:256 * g + 256], probT[:, k % 2, P * g:P * g + P],
                                           vbd[:, g].rearrange("p r n -> p (r n)"), start=True, stop=True)
                    else:
                        wait_taken(pe, k)
                        b = 0
                        for i, (h, t, o) in enumerate(s["segs"]):
                            w = MDH if s["fam"] == "mem" else DH
                            v = heads(s, h)[3]
                            nb = 2 if s["fam"] == "mem" else t + 1
                            for jb in range(nb):
                                mm = pe.matmul(po[:, w * i:w * i + w], probT[:, k % 2, P * b:P * b + P], v[:, jb],
                                               start=jb == 0, stop=jb == nb - 1)
                                b += 1
                    mm.then_inc(values_ready, 1)

                def step(k):
                    scores(k)
                    if k >= 3:
                        values(k - 3)
                    if k >= 2:
                        turn(k - 2)

                for b in beats:
                    projection(b)
                    for k in b["steps"]:
                        step(k)

            @block.scalar
            def _(act):
                marks = {}

                def link(ins):
                    marks["c"] = marks.get("c", 0) + 1
                    ins.then_inc(chain_act, 1)
                    act.wait_ge(chain_act, marks["c"])

                def done(ins, s, key):
                    marks[key] = marks.get(key, 0) + 1
                    ins.then_inc(s, 1)
                    act.wait_ge(s, marks[key])

                A = nc.scalar.activation

                def high(u, half):
                    if half == 0:
                        act.wait_ge(raw_in[u % 2], 16 * (u // 2 + 1))
                        if u >= 2:
                            wait_beat(act, pl.unit_end[u - 2])
                    done(A(w_hi[:, u % 2, 2 * half:2 * half + 2].rearrange("p k n -> p (k n)"),
                           raw[:, u % 2, 1024 * half:1024 * half + 1024], ACT.Copy), hi_ready, "hi")

                act.wait_ge(crow_in, 16)
                done(A(crow, crow, ACT.Silu), ready_act, "r")
                act.wait_ge(ready_dve, DVE_TAB)
                link(A(rope_s[:], rope_s[:], ACT.Sin))
                link(A(rope_c[:], rope_c[:], ACT.Sin))
                act.wait_ge(x_in, 16)
                for j in range(NT):
                    link(A(a_lo[:, 8:10].rearrange("p k n -> p (k n)"), x0[:, j], ACT.Square,
                           accum_out=ss[:, j:j + 1]))
                done(A(sd, ss, ACT.Sqrt, bias=CI["eps"], scale=1.0 / D), ready_act, "r")
                act.wait_ge(ready_dve, DVE_RMS)
                for j in range(NT):
                    done(A(x0[:, j], x0[:, j], ACT.Copy, scale=rr[:, j:j + 1]), ready_act, "r")
                high(0, 0)
                high(0, 1)
                for n in range(2 * NT):
                    half, j = divmod(n, NT)
                    act.wait_ge(stage_ready, n + 1)
                    done(A(a_hi[:, 4 * half:4 * half + 4, P * j:P * j + P], stage[:, n % 4], ACT.Copy),
                         stage_high, "sh")
                    if n == 3:
                        high(1, 0)
                        high(1, 1)

                def probs(k):
                    s = steps[k]
                    if not has(s, "probs"):
                        return
                    kind = s["kind"]
                    if kind == "sm":
                        act.wait_ge(rows_ready, count["rows"][k])
                        wait_probs_slot(act, k)
                        for i, (h, t, o) in enumerate(s["segs"]):
                            n = MEM if s["fam"] == "mem" else P * (t + 1)
                            ins = A(prob[:, k % 2, o:o + n], sc[k % 2][:, o:o + n], ACT.Exp,
                                    bias=nmax[:, k % 4, i:i + 1], accum_out=rsum[:, k % 4, i:i + 1])
                        done(ins, probs_ready, "p")
                    elif kind == "cmp":
                        act.wait_ge(rows_ready, count["rows"][k])
                        done(A(prob[:, k % 2, 0:256], prob[:, k % 2, 0:256], ACT.Exp), probs_ready, "p")
                    elif kind == "hid":
                        act.wait_ge(scores_ready, count["scores"][k])
                        link(A(probT[:, k % 2, 0:128], sc[k % 2][:, 0:128], ACT.Silu))
                        hv = prob[:, k % 2].rearrange("p (m g r n) -> p m g r n", m=2, g=2, r=4)
                        sv = sc[k % 2][:, 128:256].rearrange("p (m g n) -> p m g n", m=2, g=2)
                        link(A(hv[:, 0], sv[:, 0].unsqueeze(2).broadcast_to([P, 2, 4, 32]), ACT.Silu))
                        done(A(hv[:, 1], sv[:, 1].unsqueeze(2).broadcast_to([P, 2, 4, 32]), ACT.Silu),
                             probs_ready, "p")
                    elif kind == "gates":
                        wait_evac(act, max(b["b"] for b in beats if b["name"] == "N2"))
                        done(A(glog[:], glog[:], ACT.Tanh, scale=0.5), probs_ready, "p")
                    elif kind == "gn":
                        act.wait_ge(rows_ready, count["rows"][k])
                        if s["j"] >= 2:
                            wait_taken(act, [q["k"] for q in steps if q["kind"] == "gn"][s["j"] - 2])
                        done(A(tmp[:, s["j"] % 2], rk[:, s["j"]], ACT.Square), probs_ready, "p")
                    elif kind in ("mnorm", "j1", "j2"):
                        if kind == "mnorm":
                            act.wait_ge(mem_in, 16)
                            t = memr[:, s["j"]]
                        elif kind == "j1":
                            wait_evac(act, s["beat"])
                            t = yo[:, s["j"]]
                        elif s["which"] == 0:
                            wait_taken(act, max(p for p in range(k) if steps[p]["kind"] == "j1" and
                                                steps[p]["j"] == s["j"]))
                            t = x1[:, s["j"]]
                        else:
                            wait_evac(act, s["beat"])
                            t = x2[:, s["j"]]
                        rms = norm[:, s["norm"]:s["norm"] + 1]
                        link(A(dump, t, ACT.Square, accum_out=rms))
                        done(A(rms, rms, ACT.Sqrt, bias=CI["eps"], scale=1.0 / D),
                             probs_ready, "p")
                    elif kind == "qn":
                        act.wait_ge(rows_ready, count["rows"][k])
                        n, w = s["nh"], S // s["nh"]
                        done(A(qsd[:, s["slot"], 0:n], qss[:, s["slot"], 0:n], ACT.Sqrt, bias=CI["eps"],
                               scale=1.0 / w), probs_ready, "p")

                def take(k):
                    s = steps[k]
                    if s["kind"] not in ("sm", "trh"):
                        return
                    act.wait_ge(turned, count["turn"][k])
                    if s["kind"] == "trh":
                        wait_region(act, s["kt"], s["in_beat"] - s["mid"])
                        done(A(a_hi[:, s["kt"]:s["kt"] + 4, P * s["j"]:P * s["j"] + P],
                               turn_bank(s)[:].rearrange("p (b n) -> p b n", b=4), ACT.Copy), high_taken, "h")
                        return
                    done(A(probT[:, k % 2], pt[:], ACT.Copy), taken_act, "t")

                def step(k):
                    probs(k)
                    if k >= 2:
                        take(k - 2)
                        s = steps[k - 2]
                        if s["kind"] == "tr" and s["to"] == "n1" and s["j"] == NT - 1:
                            wait_taken(act, k - 2)
                            for l in range(2):
                                for g in range(2):
                                    act.dma_start(cblk[DH * l:DH * l + DH, :, g, 0:S - l],
                                                  kvT[DH * g:DH * g + DH, :, l:S]).then_inc(gather_in, 16)

                last_nsa = max(s["k"] for s in steps if s.get("fam") == "nsa")
                for b in beats:
                    if b["unit_first"] and b["u"] >= 1 and b["u"] + 1 < NU:
                        high(b["u"] + 1, 0)
                    for k in b["mid"]:
                        step(k)
                    if b["unit_first"] and b["u"] >= 1 and b["u"] + 1 < NU:
                        high(b["u"] + 1, 1)
                    name = b["name"]
                    if name == "N2" and b["last"] and b["j"] == 0:
                        act.wait_ge(ada_used, 11)
                        for v, kv in enumerate("kv"):
                            act.dma_start(w1[:, v], t_in["cmp_w1_" + kv].rearrange("a (m p) n -> p (a m) n", p=P)
                                          ).then_inc(w1_in, 16)
                    if b["last"]:
                        j = b["j"]
                        if name in ("NG", "RG"):
                            wait_beat(act, b["b"])
                            if name == "NG":
                                act.wait_ge(values_ready, count["values"][last_nsa])
                            else:
                                wait_evac(act, b["b"] - 8)
                                if j == 0:
                                    wait_taken(act, max(s["k"] for s in steps if s["kind"] == "gn"))
                                    link(A(gvar, gvar, ACT.Sqrt, bias=CI["epsg"], scale=1.0 / DH))
                            done(A(sg[:, j], pj[b["bank"]][:], ACT.Silu), pair_act, "pair")
                        elif name == "WO":
                            wait_beat(act, b["b"])
                            done(A(yo[:, j, 512 * b["c"]:512 * b["c"] + 512], pj[b["bank"]][:], ACT.Copy),
                                 evac_act, "e")
                        elif name in ("MV", "V"):
                            wait_beat(act, b["b"])
                            done(A((vm if name == "MV" else vmo)[:, j], pj[b["bank"]][:], ACT.Copy), evac_act, "e")
                        elif name in ("MK", "Q", "K", "QM"):
                            s = pl.src_of_beat[b["b"]]
                            wait_beat(act, b["b"])
                            if s["slot_prev"] is not None:
                                act.wait_ge(turned, count["turn"][s["slot_prev"]])
                            link(A(src[:, s["slot"]], pj[b["bank"]][:], ACT.Copy))
                            done(A(tmp[:, s["slot"]], pj[b["bank"]][:], ACT.Square), evac_act, "e")
                        elif name == "CC":
                            wait_beat(act, b["b"])
                            act.wait_ge(x1_saved, 16)
                            done(A(ucv[:, j], pj[b["bank"]][:], ACT.Copy), evac_act, "e")
                        elif name == "G":
                            wait_beat(act, b["b"])
                            prev = [q for q in beats[:b["b"]] if q["name"] in ("CB", "B") and q["last"]
                                    and q["j"] == j][-1]
                            wait_evac(act, prev["b"])
                            done(A(tg[:, j], pj[b["bank"]][:], ACT.Tanh,
                                   bias=CI["b_gate"][:, 8 * b["gi"] + 4 * b["c"] + j:][:, 0:1], scale=0.5),
                                 evac_act, "e")
                        elif name == "UA":
                            wait_evac(act, b["b"])
                            prev = [q for q in beats[:b["b"]] if q["name"] == "UB" and q["last"]]
                            if prev:
                                wait_evac(act, prev[-1]["b"])
                            done(A(fsi[:, j], fcv[:, j], ACT.Silu), pair_act, "pair")
                    for k in b["steps"]:
                        step(k)
                    if name == "RG" and b["last"] and b["j"] == 3:
                        last_ret = max(s["k"] for s in steps if s["kind"] == "ret")
                        act.wait_ge(out_taken, count["out"][last_ret])
                        act.dma_start(g_mem_row, t_in["g_mem_2"].rearrange("(a d) -> a d", a=1).broadcast_to([P, D])
                                      ).then_inc(gmem_in, 16)
                        act.dma_start(memr, t_in["mem_2"].rearrange("a (t p) d -> p (a t) d", p=P)).then_inc(mem_in, 16)
                    if name == "WO" and b["first"] and b["c"] == 0 and b["j"] == 0:
                        p = max(s["k"] for s in steps if s["kind"] == "trh" and s["src"] == "att")
                        wait_taken(act, p)
                        act.dma_start(g_row, t_in["g_mix_2"].rearrange("(a d) -> a d", a=1).broadcast_to([P, D])
                                      ).then_inc(grow_in, 16)
                    if name == "WY" and b["first"] and b["c"] == 0 and b["j"] == 0:
                        act.dma_start(g_row, t_in["g_ffn_2"].rearrange("(a d) -> a d", a=1).broadcast_to([P, D])
                                      ).then_inc(grow_in, 16)
                    if name == "WO" and b["last"] and b["c"] == 0 and b["j"] == 0:
                        wait_evac(act, max(q["b"] for q in beats if q["name"] == "RG"))
                        act.dma_start(x1, t_in["x"].rearrange("a (t p) d -> p (a t) d", p=P)).then_inc(xres_in, 16)
                    if name == "MV" and b["last"] and b["j"] == 1:
                        p = max(s["k"] for s in steps if s["kind"] == "j1")
                        wait_taken(act, p)
                        act.dma_start(x1_dram.rearrange("(t p) d -> p t d", p=P), x1).then_inc(x1_saved, 16)
                    if name == "B" and b["i"] == 1 and b["c"] == 0 and b["j"] == 3:
                        p = max(s["k"] for s in steps if s["kind"] == "sm")
                        act.wait_ge(out_taken, count["out"][p])
                        act.dma_start(x2, x1_dram.rearrange("(t p) d -> p t d", p=P)).then_inc(x1_back, 16)

            @block.vector
            def _(dve):
                V = nc.vector
                marks = {}

                def link(ins):
                    marks["c"] = marks.get("c", 0) + 1
                    ins.then_inc(chain_dve, 1)
                    dve.wait_ge(chain_dve, marks["c"])

                def done(ins, s, key):
                    marks[key] = marks.get(key, 0) + 1
                    ins.then_inc(s, 1)
                    dve.wait_ge(s, marks[key])

                def split(kt, q, value, s, key):
                    link(V.tensor_copy(a_hi[:, kt, q], value))
                    done(V.tensor_tensor(a_lo[:, kt, q], value, a_hi[:, kt, q].bitcast(F32), ALU.subtract), s, key)

                link(V.memset(CI["epsg"], 1e-5))
                done(V.memset(CI["eps"], EPS), eps_ready, "eps")
                dve.wait_ge(consts_in, 16 * N_CONST)
                link(V.tensor_copy(idb[:], ident))
                link(V.tensor_tensor(pj[0][:, 0:P], tri, ident, ALU.subtract))
                link(V.tensor_scalar(maskb[:], pj[0][:, 0:P], NEG, None, ALU.mult))
                ang = tmp[:, 0, 0:5 * NF].rearrange("p (t f) -> p t f", t=5)
                rnd = tmp[:, 0, 200:400].rearrange("p (t f) -> p t f", t=5)
                posf = small[:, 120:125]
                link(V.memset(posf, 0.0))
                link(V.tensor_copy(posf[:, 0:4], posi[:, 0:4]))
                for g in range(2):
                    link(V.tensor_copy(posf[32 * g:32 * g + NCMP, 4:5], posi[32 * g:32 * g + NCMP, 4:5]))
                inv = cst[:, C_INV:C_INV + NF]
                link(V.tensor_tensor(ang, posf.unsqueeze(2).broadcast_to([P, 5, NF]),
                                     inv.unsqueeze(1).broadcast_to([P, 5, NF]), ALU.mult))
                link(V.tensor_scalar(rnd, ang, 1.0 / (2 * np.pi), ROUND, ALU.mult, ALU.add))
                link(V.tensor_scalar(rnd, rnd, ROUND, None, ALU.subtract))
                for part in (TWO_PI_A, TWO_PI_B, TWO_PI_C):
                    link(V.scalar_tensor_tensor(ang, rnd, -part, ang, ALU.mult, ALU.add))
                link(V.tensor_scalar(rope_s[:], ang, 3.1415925, -3.1415925, ALU.min, ALU.max))
                link(V.scalar_tensor_tensor(rnd, rope_s[:], -1.0, rope_s[:], ALU.mult, ALU.max))
                done(V.tensor_scalar(rope_c[:], rnd, -1.0, np.pi / 2, ALU.mult, ALU.add), ready_dve, "r")

                def adaln(i):
                    s, c = ada_slot[i], ada_chunk[i]
                    dve.wait_ge(ada_in[s], 16 * ada_slot[:i + 1].count(s))
                    for m in range(2):
                        col = CI[("cb", "ca", "cg")[c // 4]][:, 2 * (c % 4) + m:2 * (c % 4) + m + 1]
                        ins = V.tensor_tensor_reduce(out=ada_t[:, s, m], in0=ada_t[:, s, m], in1=crow,
                                                     scale=1.0, scalar=0.0, op0=ALU.mult, op1=ALU.add,
                                                     accum_out=col)
                    done(ins, ada_used, "ada")

                dve.wait_ge(ready_act, 1)
                for half in range(2):
                    for i in range(4 * half, 4 * half + 4):
                        if i == 1:
                            dve.wait_ge(ready_act, 2)
                            done(V.reciprocal(rr, sd), ready_dve, "r")
                        adaln(i)
                    z = slice(4 * half, 4 * half + 4)
                    link(V.tensor_tensor(CI["cb"][:, z], CI["cb"][:, z], CI["b_ada"][:, 0:8][:, z], ALU.add))
                    link(V.tensor_tensor(CI["ca"][:, z], CI["ca"][:, z], CI["b_ada"][:, 8:16][:, z], ALU.add))
                    link(V.scalar_tensor_tensor(CI["ca"][:, z], CI["ca"][:, z], 1.0, CI["g_pre"][:, z], ALU.add,
                                                ALU.mult))
                    dve.wait_ge(ready_pe, 2 * NT)
                    for n in range(NT * half, NT * half + NT):
                        if half:
                            dve.wait_ge(h_taken, n - 3)
                        for q in range(4):
                            kt = 4 * half + q
                            ins = V.tensor_scalar(stage[:, n % 4, q], xbank[n][:, P * q:P * q + P],
                                                  CI["ca"][:, kt:kt + 1], CI["cb"][:, kt:kt + 1], ALU.mult, ALU.add)
                        done(ins, stage_ready, "st")
                link(V.tensor_scalar(CI["b_gate"], CI["b_gate"], 0.5, None, ALU.mult))
                dve.wait_ge(h_taken, 2 * NT)

                def gate_chunk(i):
                    adaln(i)
                    if i == 11:
                        link(V.tensor_tensor(CI["cg"], CI["cg"], CI["b_ada"][:, 16:24], ALU.add))
                        link(V.tensor_tensor(CI["cg"], CI["cg"], CI["g_post"], ALU.mult))
                        link(V.tensor_copy(gate, CI["cg"].unsqueeze(2).broadcast_to([P, KT, P])))
                        link(V.memset(kcT.rearrange("p g e n -> p (g e n)"), 0.0))
                        done(V.memset(vbd.rearrange("p g r n -> p (g r n)"), 0.0), ready_dve, "r")

                def rotate(dst, s, nh, half, c, sn):
                    a = s[:, :, 0:2 * half].rearrange("p h (t f) -> p h t f", t=2)
                    n = nh * 2 * half
                    np_ = s.shape[0]
                    bc = c.unsqueeze(1).unsqueeze(1).broadcast_to([np_, nh, 2, half])
                    bs = sn.unsqueeze(1).unsqueeze(1).broadcast_to([np_, nh, 2, half])
                    tc_ = tmp[0:np_, 0, 0:n].rearrange("p (h t f) -> p h t f", h=nh, t=2)
                    ts_ = tmp[0:np_, 1, 0:n].rearrange("p (h t f) -> p h t f", h=nh, t=2)
                    V.tensor_tensor(tc_, a, bc, ALU.mult)
                    link(V.tensor_tensor(ts_, a, bs, ALU.mult))
                    V.tensor_tensor(dst[:, :, 0:half], tc_[:, :, 0], ts_[:, :, 1], ALU.subtract)
                    return V.tensor_tensor(dst[:, :, half:2 * half], ts_[:, :, 0], tc_[:, :, 1], ALU.add)

                def h3(ap, w):
                    return ap.rearrange("p (h d) -> p h d", d=w)

                def src_slot(b):
                    s = pl.src_of_beat[b["b"]]
                    if s["slot_prev"] is not None:
                        dve.wait_ge(turned, count["turn"][s["slot_prev"]])
                    return src[:, s["slot"]], s["slot"]

                def evacuate(b):
                    if not b["last"] or b["evac"] != "dve":
                        return
                    wait_beat(dve, b["b"])
                    name, j, bank = b["name"], b["j"], pj[b["bank"]]
                    cr, sr = rope_c[:, j, 0:NF_RET], rope_s[:, j, 0:NF_RET]
                    cn, sn = rope_c[:, j, NF_RET:NF], rope_s[:, j, NF_RET:NF]

                    def e(ins):
                        done(ins, evac_dve, "e")

                    if name == "N1":
                        t, _ = src_slot(b)
                        link(V.tensor_copy(t[:, 0:256], bank[:, 0:256]))
                        d4 = t[:, 256:512].rearrange("p (g r d) -> p g r d", g=2, r=2)
                        link(V.tensor_copy(d4[:, :, 0], h3(bank[:, 256:384], DH)))
                        link(rotate(d4[:, :, 0], h3(bank[:, 256:384], DH), 2, 8, cn, sn))
                        link(V.tensor_copy(d4[:, :, 1], d4[:, :, 0]))
                        e(V.tensor_copy(vsel[:, j], bank[:, 384:512]))
                    elif name == "N2":
                        t, _ = src_slot(b)
                        d4 = t[:, 0:256].rearrange("p (g r d) -> p g r d", g=2, r=2)
                        link(V.tensor_copy(d4[:, :, 0], h3(bank[:, 0:128], DH)))
                        link(rotate(d4[:, :, 0], h3(bank[:, 0:128], DH), 2, 8, cn, sn))
                        link(V.tensor_copy(d4[:, :, 1], d4[:, :, 0]))
                        link(V.tensor_copy(vwin[:, j], bank[:, 128:256]))
                        e(V.tensor_copy(glog[:, j], bank[:, 256:280]))
                    elif name == "NQ":
                        t, _ = src_slot(b)
                        link(V.tensor_copy(t, bank[:]))
                        e(rotate(h3(t, DH), h3(bank[:], DH), H, 8, cn, sn))
                    elif name == "RQ":
                        t, _ = src_slot(b)
                        e(rotate(h3(t, DH), h3(bank[:], DH), H, 32, cr, sr))
                    elif name == "RK":
                        e(rotate(h3(rk[:, j], DH), h3(bank[:], DH), H, 32, cr, sr))
                    elif name == "RV":
                        e(V.tensor_tensor(h3(rv[:, j], DH), h3(bank[:], DH),
                                          cst[:, C_VSC:C_VSC + H].unsqueeze(2).broadcast_to([P, H, DH]), ALU.mult))
                    elif name == "NG":
                        dve.wait_ge(pair_act, pair_n[b["b"]])
                        e(V.scalar_tensor_tensor(att[:, j], sg[:, j], 0.5, att[:, j], ALU.mult, ALU.mult))
                    elif name == "RG":
                        dve.wait_ge(pair_act, pair_n[b["b"]])
                        link(V.reciprocal(rs8, gvar[:, j]))
                        link(V.tensor_tensor(h3(rk[:, j], DH), h3(rk[:, j], DH),
                                             rs8.unsqueeze(2).broadcast_to([P, H, DH]), ALU.mult))
                        e(V.tensor_tensor(rk[:, j], sg[:, j], rk[:, j], ALU.mult))
                    elif name == "CX":
                        wait_evac(dve, b["b"] - 8)
                        e(V.tensor_tensor(ucv[:, j], ucv[:, j], bank[:], ALU.mult))
                    elif name == "CB":
                        w = [CI["conv_w"][:, 4 * i + j:4 * i + j + 1] for i in range(3)]
                        t = tmp[:, 0]
                        link(V.tensor_scalar(t, ucv[:, j], w[2], CI["conv_b"][:, j:j + 1], ALU.mult, ALU.add))
                        link(V.scalar_tensor_tensor(t[:, 1:], ucv[:, j, 0:S - 1], w[1], t[:, 1:], ALU.mult, ALU.add))
                        link(V.scalar_tensor_tensor(t[:, 2:], ucv[:, j, 0:S - 2], w[0], t[:, 2:], ALU.mult, ALU.add))
                        link(V.tensor_tensor(tmp[:, 1], t, bank[:], ALU.mult))
                        wait_region(dve, b["act_kt"], b["b"])
                        split(b["act_kt"], slice(0, S), tmp[:, 1], evac_dve, "e")
                    elif name == "B":
                        m = merged[:, 4 * b["c"] + j]
                        wait_evac(dve, b["b"] - 4)
                        if b["i"] == 0:
                            e(V.scalar_tensor_tensor(m, tg[:, j], 1.0, bank[:], ALU.add, ALU.mult))
                        else:
                            link(V.scalar_tensor_tensor(tmp[:, 0], tg[:, j], 1.0, bank[:], ALU.add, ALU.mult))
                            if b["i"] == 1:
                                e(V.tensor_tensor(m, m, tmp[:, 0], ALU.add))
                            else:
                                link(V.tensor_tensor(m, m, tmp[:, 0], ALU.add))
                                link(V.tensor_scalar(tmp[:, 1], m, 0.5, None, ALU.mult))
                                wait_region(dve, b["act_kt"], b["b"])
                                split(b["act_kt"], slice(0, S), tmp[:, 1], evac_dve, "e")
                    elif name == "WY":
                        if b["c"] == 0 and j == 0:
                            dve.wait_ge(x1_back, 16)
                        t = x2[:, j, 512 * b["c"]:512 * b["c"] + 512]
                        e(V.tensor_tensor(t, t, bank[:], ALU.add))
                    elif name == "UA":
                        ct = b["ch"] + j
                        w = [ffw[:, i, ct:ct + 1] for i in range(4)]
                        t = fcv[:, j]
                        prev = [q for q in beats[:b["b"]] if q["name"] == "UA" and q["last"] and q["j"] == j]
                        if prev:
                            dve.wait_ge(pair_act, pair_n[prev[-1]["b"]])
                        link(V.tensor_scalar(t, bank[:], w[2], w[3], ALU.mult, ALU.add))
                        link(V.scalar_tensor_tensor(t[:, 1:], bank[:, 0:S - 1], w[1], t[:, 1:], ALU.mult, ALU.add))
                        e(V.scalar_tensor_tensor(t[:, 2:], bank[:, 0:S - 2], w[0], t[:, 2:], ALU.mult, ALU.add))
                    elif name == "UB":
                        jj = b["act_kt"] - b["act"]
                        ua = [q for q in beats[:b["b"]] if q["name"] == "UA" and q["last"] and q["j"] == jj][-1]
                        dve.wait_ge(pair_act, pair_n[ua["b"]])
                        link(V.tensor_tensor(tmp[:, 1], fsi[:, jj], bank[:], ALU.mult))
                        wait_region(dve, b["act_kt"], b["b"])
                        split(b["act_kt"], slice(0, S), tmp[:, 1], evac_dve, "e")
                    elif name == "DN":
                        t = x2[:, j, 512 * b["c"]:512 * b["c"] + 512]
                        e(V.tensor_tensor(t, t, bank[:], ALU.add))

                def rows(k):
                    s = steps[k]
                    if not has(s, "rows"):
                        return
                    kind = s["kind"]
                    if kind == "sm":
                        dve.wait_ge(scores_ready, count["scores"][k])
                        for i, (h, t, o) in enumerate(s["segs"]):
                            n = MEM if s["fam"] == "mem" else P * (t + 1)
                            ins = V.tensor_reduce(nmax[:, k % 4, i:i + 1], sc[k % 2][:, o:o + n], AX_X, ALU.max,
                                                  negate=True)
                        done(ins, rows_ready, "s")
                    elif kind == "cmp":
                        dve.wait_ge(scores_ready, count["scores"][k])
                        wait_probs_slot(dve, k)
                        pr = prob[:, k % 2, 0:256].rearrange("p (h n) -> p h n", h=H)
                        link(V.tensor_tensor(pr, sc[k % 2][:, 0:256].rearrange("p (h n) -> p h n", h=H),
                                             cmpb[:, s["j"]].unsqueeze(1).broadcast_to([P, H, 32]), ALU.add))
                        link(V.reduce_max(st8, pr, axis=AX_X))
                        done(V.tensor_tensor(pr, pr, st8.unsqueeze(2).broadcast_to([P, H, 32]), ALU.subtract),
                             rows_ready, "s")
                    elif kind == "ret":
                        dve.wait_ge(scores_ready, count["scores"][k])
                        if s["nth"] >= 4:
                            p = [q["k"] for q in steps if q["kind"] == "ret"][s["nth"] - 4]
                        else:
                            p = max(q["k"] for q in steps if q.get("fam") == "nsa")
                        dve.wait_ge(values_ready, count["values"][p])
                        done(V.tensor_tensor(pret[:, s["nth"] % 4].rearrange("p (h n) -> p h n", h=4),
                                             sc[k % 2][:].rearrange("p (h n) -> p h n", h=4),
                                             tri.unsqueeze(1).broadcast_to([P, 4, P]), ALU.mult), rows_ready, "s")
                    elif kind == "cmv":
                        dve.wait_ge(gather_in, 64)
                        dve.wait_ge(turned, count["turn"][max(p for p in range(k) if steps[p]["kind"] == "gp")])
                        link(V.memset(cmv.rearrange("p v m g n -> p (v m g) n")[:, :, NCMP:32], 0.0))
                        for v in range(2):
                            for g in range(2):
                                for a in range(2):
                                    blk = cblk[:, v, g].rearrange("p (n m l) -> p m n l", m=8, l=2)
                                    ins = V.tensor_tensor(
                                        cmv[:, v, 8 * a:8 * a + 8, g, 0:NCMP], blk[:, :, a:a + NCMP, 0],
                                        cpe[:, v, 8 * a:8 * a + 8].unsqueeze(2).broadcast_to([P, 8, NCMP]), ALU.add)
                        done(ins, rows_ready, "s")
                    elif kind == "qn":
                        wait_evac(dve, s["beat"])
                        done(V.reduce_sum(qss[:, s["slot"], 0:s["nh"]], h3(tmp[:, s["slot"]], S // s["nh"]),
                                          axis=AX_X), rows_ready, "s")
                    elif kind == "gn":
                        t = h3(rk[:, s["j"]], DH)
                        link(V.reduce_sum(st8, t, axis=AX_X))
                        link(V.tensor_scalar(st8, st8, -1.0 / DH, None, ALU.mult))
                        done(V.tensor_tensor(t, t, st8.unsqueeze(2).broadcast_to([P, H, DH]), ALU.add), rows_ready,
                             "s")

                def outputs(k):
                    s = steps[k]
                    if not has(s, "out"):
                        return
                    dve.wait_ge(values_ready, count["values"][k])
                    kind = s["kind"]
                    if kind == "cmp":
                        j = s["j"]
                        link(V.reciprocal(cf8, (rs8, rs8_odd)[k % 2]))
                        gl = glog[:, j].rearrange("p (h c) -> p h c", c=3)[:, :, 0]
                        link(V.scalar_tensor_tensor(cf8, gl, 1.0, cf8, ALU.add, ALU.mult))
                        link(V.tensor_scalar(cf8, cf8, cst[:, C_ROW + j:C_ROW + j + 1], None, ALU.mult))
                        done(V.tensor_tensor(h3(att[:, j], DH), h3(po[:], DH),
                                             cf8.unsqueeze(2).broadcast_to([P, H, DH]), ALU.mult), out_taken, "o")
                    elif kind == "ret":
                        e = s["half"]
                        done(V.tensor_tensor(rk[:, s["j"]].rearrange("p (c e d) -> p c e d", c=4, e=2)[:, :, e],
                                             h3(po[:, 0:256], DH),
                                             cst[:, C_XI + 4 * e:C_XI + 4 * e + 4].unsqueeze(2)
                                             .broadcast_to([P, 4, DH]), ALU.mult), out_taken, "o")
                    else:
                        n = len(s["segs"])
                        link(V.reciprocal(ri[:, 0:n], rsum[:, k % 4, 0:n]))
                        for i, (h, t, o) in enumerate(s["segs"]):
                            if s["fam"] == "nsa":
                                g = 3 * h + 1 + s["br"]
                                link(V.scalar_tensor_tensor(cf[:, i:i + 1], glog[:, t, g:g + 1], 1.0, ri[:, i:i + 1],
                                                            ALU.add, ALU.mult))
                                d = att[:, t, DH * h:DH * h + DH]
                                ins = V.scalar_tensor_tensor(d, po[:, DH * i:DH * i + DH], cf[:, i:i + 1], d,
                                                             ALU.mult, ALU.add)
                            elif s["fam"] == "moba":
                                if i == 0:
                                    dve.wait_ge(x1_saved, 16)
                                ins = V.tensor_scalar(ymo[:, t, DH * h:DH * h + DH], po[:, DH * i:DH * i + DH],
                                                      ri[:, i:i + 1], None, ALU.mult)
                            else:
                                m = pl.src_mem[t]
                                if m["slot_prev"] is not None:
                                    dve.wait_ge(turned, count["turn"][m["slot_prev"]])
                                ins = V.tensor_scalar(src[:, m["slot"], MDH * h:MDH * h + MDH],
                                                      po[:, MDH * i:MDH * i + MDH], ri[:, i:i + 1], None, ALU.mult)
                        done(ins, out_taken, "o")

                def take(k):
                    s = steps[k]
                    if not has(s, "take") or s["kind"] == "sm":
                        return
                    kind = s["kind"]

                    def f(ins):
                        done(ins, taken_dve, "t")

                    if has(s, "turn"):
                        dve.wait_ge(turned, count["turn"][k])
                    q = slice(P * s.get("j", 0), P * s.get("j", 0) + P)
                    p4 = pt[:].rearrange("p (b n) -> p b n", b=4)
                    if kind == "gp":
                        f(V.tensor_copy(gp[:, 512 * s["c"]:512 * s["c"] + 512], pt[:]))
                    elif kind == "tr":
                        to = s["to"]
                        if to == "n1":
                            V.tensor_copy(kvT[:, :, q], p4[:, 0:2])
                            f(V.tensor_copy(ncT[:, 0:2, q], p4[:, 2:4]))
                        elif to == "n2":
                            f(V.tensor_copy(ncT[:, 2:4, q], p4[:, 0:2]))
                        elif to == "rk":
                            f(V.tensor_copy(rkT[:, :, q], p4))
                        elif to in ("nq", "rq"):
                            f(V.tensor_scalar({"nq": nqT, "rq": rqT}[to][:, :, q], p4, DH ** -0.5, None, ALU.mult))
                        elif to == "mk":
                            f(V.tensor_scalar(kmT[:, :, q], p4, CI["gmk"], None, ALU.mult))
                        elif to == "Q":
                            f(V.tensor_scalar(qT[:, :, q], p4, CI["gq"], DH ** -0.5, ALU.mult, ALU.mult))
                        elif to == "K":
                            f(V.tensor_scalar(kT[:, :, q], p4, CI["gk"], None, ALU.mult))
                        else:
                            f(V.tensor_scalar(qmT[:, :, q], p4, CI["gmq"], MDH ** -0.5, ALU.mult, ALU.mult))
                    elif kind == "trh":
                        kt = slice(s["kt"], s["kt"] + 4)
                        dve.wait_ge(high_taken, count["high"][k])
                        f(V.tensor_tensor(a_lo[:, kt, q], turn_bank(s)[:].rearrange("p (b n) -> p b n", b=4),
                                          a_hi[:, kt, q].bitcast(F32), ALU.subtract))
                    elif kind == "hid":
                        k3 = kcr[0:64, 0:DH].unsqueeze(1)
                        link(V.tensor_copy(kcr[0:64, 0:DH], pt[0:64, 0:DH]))
                        link(rotate(k3, pt[0:64, 0:DH].unsqueeze(1), 1, 8, rope_c[0:64, 4, NF_RET:NF],
                                    rope_s[0:64, 4, NF_RET:NF]))
                        link(V.tensor_copy(kcr[0:64, DH:2 * DH], kcr[0:64, 0:DH]))
                        for r in range(4):
                            z = slice(32 * r, 32 * r + 32)
                            ins = V.tensor_copy(vbd[z, :, r], pt[z, 64:192].rearrange("p (g n) -> p g n", g=2))
                        f(ins)
                    elif kind == "kct":
                        for e in range(2):
                            z = slice(DH * e, DH * e + DH)
                            ins = V.tensor_copy(kcT[z, :, e], pt[z, 0:64].rearrange("p (g n) -> p g n", g=2))
                        f(ins)
                    elif kind == "cmp":
                        f(V.tensor_copy(probT[:, k % 2, 0:256], pt[:, 0:256]))
                    elif kind == "ret":
                        e = slice(DH * s["half"], DH * s["half"] + DH)
                        d, new = Rst[e, (s["j"] + 1) % 2], h3(pt[e, 0:256], DH)
                        decay = cst[e, C_DEC:C_DEC + 4].unsqueeze(2).broadcast_to([DH, 4, DH])
                        if s["j"] == 0:
                            f(V.tensor_tensor(d, new, decay, ALU.mult))
                        else:
                            link(V.tensor_tensor(d, Rst[e, s["j"] % 2], new, ALU.add))
                            f(V.tensor_tensor(d, d, decay, ALU.mult))

                def normalise(k):
                    s = steps[k]
                    if not has(s, "norm"):
                        return
                    kind = s["kind"]
                    dve.wait_ge(probs_ready, count["probs"][k])
                    if kind == "gn":
                        done(V.reduce_sum(gvar[:, s["j"]], h3(tmp[:, s["j"] % 2], DH), axis=AX_X), normed, "n")
                    elif kind == "mnorm":
                        rms = norm[:, s["norm"]:s["norm"] + 1]
                        link(V.reciprocal(rms, rms))
                        dve.wait_ge(gmem_in, 16)
                        m = memr[:, s["j"]]
                        done(V.scalar_tensor_tensor(m, m, rms, g_mem_row, ALU.mult, ALU.mult), normed, "n")
                    elif kind == "j1":
                        rms = norm[:, s["norm"]:s["norm"] + 1]
                        if s["j"] == 0:
                            dve.wait_ge(xres_in, 16)
                        link(V.reciprocal(rms, rms))
                        y = yo[:, s["j"]]
                        link(V.scalar_tensor_tensor(y, y, rms, gp[:], ALU.mult, ALU.mult))
                        done(V.tensor_tensor(x1[:, s["j"]], x1[:, s["j"]], y, ALU.add), normed, "n")
                    elif kind == "j2":
                        rms = norm[:, s["norm"]:s["norm"] + 1]
                        link(V.reciprocal(rms, rms))
                        if s["j"] == 0:
                            dve.wait_ge(grow_in, 16 * (s["which"] + 1))
                        if s["j"] >= 2 and not s["which"]:
                            p = max(p for p in range(k) if steps[p]["kind"] == "trh" and steps[p]["j"] == s["j"] - 2)
                            dve.wait_ge(turned, count["turn"][p])
                        place = xn[s["j"] if s["which"] else s["j"] % 2]
                        done(V.scalar_tensor_tensor(place, (x1, x2)[s["which"]][:, s["j"]], rms,
                                                 g_row, ALU.mult, ALU.mult), normed, "n")
                    elif kind == "qn":
                        n = s["nh"]
                        t = h3(src[:, s["slot"]], S // n)
                        link(V.reciprocal(qri[:, 0:n], qsd[:, s["slot"], 0:n]))
                        done(V.tensor_tensor(t, t, qri[:, 0:n].unsqueeze(2).broadcast_to([P, n, S // n]), ALU.mult),
                             normed, "n")

                def step(k):
                    if k >= 1:
                        normalise(k - 1)
                    if k >= 2 and steps[k - 2]["kind"] == "cmp":
                        dve.wait_ge(probs_ready, count["probs"][k - 2])
                        link(V.reduce_sum((rs8, rs8_odd)[k % 2],
                                          prob[:, k % 2, 0:256].rearrange("p (h n) -> p h n", h=H), axis=AX_X))
                    rows(k)
                    if k >= 3:
                        outputs(k - 3)
                    if k >= 2:
                        take(k - 2)

                for b in beats:
                    for k in b["mid"]:
                        step(k)
                    evacuate(b)
                    for k in b["steps"]:
                        step(k)
                    if b["name"] == "N2" and b["first"] and b["j"] < 3:
                        gate_chunk(8 + b["j"])
                    if b["name"] == "NQ" and b["first"] and b["j"] == 0:
                        gate_chunk(11)


def pack(unit, w):
    name, r, c, n = unit
    u = np.zeros((P, 4, 512), np.float32)
    if name == "w_up2":
        for i, c0 in enumerate((c, DFF + c)):
            u[:, :, n * i:n * i + n] = w["w_up"][r:r + 512, c0:c0 + n].reshape(4, P, n).transpose(1, 0, 2)
    elif name == "w_down2":
        u[:] = w["w_down"][r:r + 2 * P].reshape(2, P, 2, 512).transpose(1, 0, 2, 3).reshape(P, 4, 512)
    else:
        u[:, :, 0:n] = w[name][r:r + 512, c:c + n].reshape(4, P, n).transpose(1, 0, 2)
    return u.reshape(P, 2048)


_INS = ["x", "c", "positions", "cmp_w1_k", "cmp_w2_k", "cmp_w1_v", "cmp_w2_v", "mem_2", "g_mem_2",
        "g_mix_2", "g_ffn_2"]


def kernel(**inputs):
    import concourse.bacc as _bacc
    from concourse.bass_utils import run_bass_kernel_spmd as _run

    a = {k: np.asarray(v) for k, v in inputs.items()}
    w = {"w_in": a["w_in"][0], "w_out": a["w_out"][0], "w_mem": a["w_mem_kv_2"], "w_in_2": a["w_in_2"],
         "w_br_conv": a["w_br_conv_2"], "w_br_mem": a["w_br_mem_2"], "w_br_moba": a["w_br_moba_2"],
         "w_o": a["w_o_2"], "w_up": a["w_up_2"], "w_down": a["w_down_2"]}
    arrays = {k: np.ascontiguousarray(a[k]) for k in _INS}
    arrays["weights"] = np.stack([pack(u, w) for u in make_plan().units])
    arrays["ada_t"] = np.ascontiguousarray(a["w_ada"][0].T)
    arrays["cols"] = columns(a)
    arrays["cst"] = constants()

    nc = _bacc.Bacc("TRN2", target_bir_lowering=False, num_devices=1)
    t_in = {}
    named = {}
    for name, v in arrays.items():
        named[f"in_{name}"] = v
        t_in[name] = nc.dram_tensor(f"in_{name}", v.shape, mybir.dt.from_np(v.dtype), kind="ExternalInput").ap()
    out = nc.dram_tensor("out", (1, S, D), F32, kind="ExternalOutput").ap()
    with nc.allow_non_contiguous_dma(reason="small per-channel columns"):
        build(nc, t_in, out)
    r = _run(nc, [named], core_ids=[0])
    return r.results[0]["out"]
```
